# Optimizing a Trainium2 kernel written in Bass

```python
import jax
import jax.numpy as jnp
from jax import lax
import numpy as np

D_MODEL = 1024
BATCH = 1
SEQ = 256
DEPTH = 2

CHUNK = 64
NORM_EPS = 1e-6
ROPE_BASE = 10000.0

RET_HEADS = 4
RET_DK = 128
RET_DV = 128
RET_QK_W = RET_HEADS * RET_DK
RET_W = RET_HEADS * RET_DV
RET_GN_EPS = 1e-5

RWKV_HEAD = 64
RWKV_HEADS = 8
RWKV_W = RWKV_HEADS * RWKV_HEAD
RWKV_DECAY_LORA = 64
RWKV_AAA_LORA = 64
RWKV_GATE_LORA = 160
RWKV_GN_EPS = 64e-5
RWKV_SPLITS = (RWKV_W, 2 * RWKV_W, 3 * RWKV_W, 3 * RWKV_W + RWKV_DECAY_LORA, 3 * RWKV_W + RWKV_DECAY_LORA + RWKV_AAA_LORA)
RWKV_COLS = 3 * RWKV_W + RWKV_DECAY_LORA + RWKV_AAA_LORA + RWKV_GATE_LORA

MLA_HEADS = 8
MLA_Q_LORA = 256
MLA_KV_LORA = 128
MLA_NOPE = 64
MLA_ROPE = 32
MLA_V = 64
MLA_W = MLA_HEADS * MLA_V
Q_BLOCK = 128

N_BRANCH = 3
BRANCH_W = 512

IN_SIZES = (RET_QK_W, RET_QK_W, RET_W, RET_W, RWKV_COLS, MLA_Q_LORA, MLA_KV_LORA + MLA_ROPE, N_BRANCH * D_MODEL)
IN_SPLITS = tuple(np.cumsum(IN_SIZES)[:-1].tolist())
IN_COLS = sum(IN_SIZES)

D_FF = 2816
N_EXPERTS = 8
TOP_K = 2
D_FF_EXPERT = 3584
N_DENSE = (DEPTH + 1) // 2
N_MOE = DEPTH // 2

kernel_name = "hybrid_retention_rwkv7_mla_moe_encoder"

def rms_norm(x, g):
    xf = x.astype(jnp.float32)
    y = xf * lax.rsqrt(jnp.mean(xf * xf, axis=-1, keepdims=True) + NORM_EPS)
    return (y * g.astype(jnp.float32)).astype(x.dtype)

def group_norm(x, eps):
    xc = x - jnp.mean(x, axis=-1, keepdims=True)
    return xc * lax.rsqrt(jnp.mean(xc * xc, axis=-1, keepdims=True) + eps)

def rope_tables(positions, dim):
    inv_freq = 1.0 / (ROPE_BASE ** (jnp.arange(0, dim, 2, dtype=jnp.float32) / dim))
    ang = positions.astype(jnp.float32)[..., None] * inv_freq
    return jnp.cos(ang), jnp.sin(ang)

def apply_rope(x, cos, sin):
    x1, x2 = jnp.split(x, 2, axis=-1)
    c = cos[:, :, None, :]
    s = sin[:, :, None, :]
    return jnp.concatenate([x1 * c - x2 * s, x1 * s + x2 * c], axis=-1).astype(x.dtype)

def token_shift(p):
    return jnp.pad(p, ((0, 0), (1, 0), (0, 0)))[:, :-1]

def retention_mix(q, k, v, g, cos, sin):
    f32 = jnp.float32
    B, S, _ = q.shape
    N, H = S // CHUNK, RET_HEADS
    q = apply_rope(q.reshape(B, S, H, RET_DK), cos, sin).astype(f32)
    k = apply_rope(k.reshape(B, S, H, RET_DK), cos, sin).astype(f32) * (RET_DK ** -0.5)
    v = v.reshape(B, S, H, RET_DV).astype(f32)
    log_gamma = jnp.log(1.0 - 2.0 ** (-5.0 - jnp.arange(H, dtype=f32)))
    idx = jnp.arange(CHUNK, dtype=f32)
    intra = jnp.exp(log_gamma[:, None, None] * jnp.abs(idx[:, None] - idx[None, :]))
    q_decay = jnp.exp(log_gamma[None, :] * (idx[:, None] + 1.0))
    k_decay = jnp.exp(log_gamma[None, :] * (CHUNK - 1.0 - idx[:, None]))
    chunk_decay = jnp.exp(log_gamma * CHUNK)
    qc = q.reshape(B, N, CHUNK, H, RET_DK)
    kc = k.reshape(B, N, CHUNK, H, RET_DK)
    vc = v.reshape(B, N, CHUNK, H, RET_DV)
    scores = jnp.einsum('bnihd,bnjhd->bnhij', qc, kc) * intra
    o = jnp.einsum('bnhij,bnjhe->bnihe', scores, vc)
    kv = jnp.einsum('bnjhd,bnjhe->bnhde', kc * k_decay[:, :, None], vc)

    def step(state, kv_n):
        return state * chunk_decay[None, :, None, None] + kv_n, state

    _, prev = lax.scan(step, jnp.zeros((B, H, RET_DK, RET_DV), f32), jnp.moveaxis(kv, 1, 0))
    prev = jnp.moveaxis(prev, 0, 1)
    o = o + jnp.einsum('bnihd,bnhde->bnihe', qc, prev) * q_decay[:, :, None]
    o = group_norm(o.reshape(B, S, H, RET_DV), RET_GN_EPS).reshape(B, S, RET_W)
    return o * jax.nn.silu(g.astype(f32))

def rwkv7_mix(p, mu, w0, w2, a0, a2, g2, k_k, k_a, r_k, lnx_w):
    f32 = jnp.float32
    B, S, _ = p.shape
    p = p.astype(f32)
    xs = p + (token_shift(p) - p) * mu.astype(f32)
    r, k, v, xw, xa, xg = jnp.split(xs, RWKV_SPLITS, axis=-1)
    w_log = -jax.nn.softplus(-(w0.astype(f32) + jnp.tanh(xw) @ w2.astype(f32))) - 0.5
    decay = jnp.exp(-jnp.exp(w_log))
    a = jax.nn.sigmoid(a0.astype(f32) + xa @ a2.astype(f32))
    g = jax.nn.sigmoid(xg) @ g2.astype(f32)
    shp = (B, S, RWKV_HEADS, RWKV_HEAD)
    kk = (k * k_k.astype(f32)).reshape(shp)
    kk = kk * lax.rsqrt(jnp.sum(kk * kk, axis=-1, keepdims=True) + 1e-12)
    k = k * (1.0 + (a - 1.0) * k_a.astype(f32))
    r, k, v, decay, a = (t.reshape(shp) for t in (r, k, v, decay, a))
    b = kk * a

    def step(state, inp):
        r_t, w_t, k_t, v_t, kk_t, b_t = inp
        sa = -jnp.einsum('bhvk,bhk->bhv', state, kk_t)
        state = state * w_t[:, :, None, :] + sa[..., None] * b_t[:, :, None, :] + v_t[..., None] * k_t[:, :, None, :]
        return state, jnp.einsum('bhvk,bhk->bhv', state, r_t)

    seq = tuple(jnp.moveaxis(t, 1, 0) for t in (r, decay, k, v, kk, b))
    _, y = lax.scan(step, jnp.zeros((B, RWKV_HEADS, RWKV_HEAD, RWKV_HEAD), f32), seq)
    y = jnp.moveaxis(y, 0, 1)
    y = group_norm(y, RWKV_GN_EPS) * lnx_w.astype(f32).reshape(RWKV_HEADS, RWKV_HEAD)
    y = y + jnp.sum(r * k * r_k.astype(f32), axis=-1, keepdims=True) * v
    return y.reshape(B, S, RWKV_W) * g

def mla_mix(qa, kva, q_norm, w_qb, kv_norm, w_kvb, cos, sin):
    B, S, _ = qa.shape
    q = (rms_norm(qa, q_norm) @ w_qb).reshape(B, S, MLA_HEADS, MLA_NOPE + MLA_ROPE)
    q_nope = q[..., :MLA_NOPE]
    q_pe = apply_rope(q[..., MLA_NOPE:], cos, sin)
    c_kv, k_pe = kva[..., :MLA_KV_LORA], kva[..., MLA_KV_LORA:]
    kv = (rms_norm(c_kv, kv_norm) @ w_kvb).reshape(B, S, MLA_HEADS, MLA_NOPE + MLA_V)
    k_nope, v = kv[..., :MLA_NOPE], kv[..., MLA_NOPE:]
    k_pe = apply_rope(k_pe[:, :, None, :], cos, sin)[:, :, 0, :]
    scale = (MLA_NOPE + MLA_ROPE) ** -0.5
    outs = []
    for i in range(S // Q_BLOCK):
        q0, k_end = i * Q_BLOCK, (i + 1) * Q_BLOCK
        s = (jnp.einsum('bqhd,bkhd->bhqk', q_nope[:, q0:k_end], k_nope[:, :k_end])
             + jnp.einsum('bqhr,bkr->bhqk', q_pe[:, q0:k_end], k_pe[:, :k_end])).astype(jnp.float32) * scale
        q_chunk = (q0 + np.arange(Q_BLOCK)) // CHUNK
        k_chunk = np.arange(k_end) // CHUNK
        s = jnp.where(k_chunk[None, :] <= q_chunk[:, None], s, -1e30)
        pr = jax.nn.softmax(s, axis=-1).astype(v.dtype)
        outs.append(jnp.einsum('bhqk,bkhe->bqhe', pr, v[:, :k_end]))
    return jnp.concatenate(outs, axis=1).reshape(B, S, MLA_W)

def swiglu(h, wg, wu, wd):
    return (jax.nn.silu(h @ wg) * (h @ wu)) @ wd

def moe_swiglu(h, router, wg, wu, wd):
    logits = (h @ router).astype(jnp.float32)
    top_v, top_i = lax.top_k(logits, TOP_K)
    top_w = jax.nn.softmax(top_v, axis=-1)
    comb = jnp.sum(jax.nn.one_hot(top_i, N_EXPERTS, dtype=jnp.float32) * top_w[..., None], axis=-2)
    out = jnp.zeros(h.shape, jnp.float32)
    for e in range(N_EXPERTS):
        out = out + comb[..., e:e + 1] * swiglu(h, wg[e], wu[e], wd[e]).astype(jnp.float32)
    return out.astype(h.dtype)

def setup_inputs(seed: int = 0) -> dict:
    key = jax.random.key(seed)
    ks = iter(jax.random.split(key, 40))
    f32 = jnp.float32

    def nrm(shape, scale):
        return jax.random.normal(next(ks), shape, f32) * scale

    def gain(shape):
        return 1.0 + nrm(shape, 0.05)

    L = DEPTH
    x = nrm((BATCH, SEQ, D_MODEL), 1.0)
    start = jax.random.randint(next(ks), (BATCH, 1), 0, 4096, dtype=jnp.int32)
    positions = start + jnp.arange(SEQ, dtype=jnp.int32)[None, :]
    rwkv_w0 = jnp.linspace(-6.5, -1.5, RWKV_W, dtype=f32)[None, :] + nrm((L, RWKV_W), 0.1)
    return {
        'x': x,
        'positions': positions,
        'attn_norm': gain((L, D_MODEL)),
        'w_in': nrm((L, D_MODEL, IN_COLS), D_MODEL ** -0.5),
        'rwkv_mu': jax.random.uniform(next(ks), (L, RWKV_COLS), f32),
        'rwkv_w0': rwkv_w0,
        'rwkv_w2': nrm((L, RWKV_DECAY_LORA, RWKV_W), 0.1),
        'rwkv_a0': nrm((L, RWKV_W), 0.1),
        'rwkv_a2': nrm((L, RWKV_AAA_LORA, RWKV_W), RWKV_AAA_LORA ** -0.5),
        'rwkv_g2': nrm((L, RWKV_GATE_LORA, RWKV_W), RWKV_GATE_LORA ** -0.5),
        'rwkv_k_k': 0.85 + nrm((L, RWKV_W), 0.05),
        'rwkv_k_a': gain((L, RWKV_W)),
        'rwkv_r_k': nrm((L, RWKV_HEADS, RWKV_HEAD), 0.1),
        'rwkv_lnx_w': gain((L, RWKV_W)),
        'mla_q_norm': gain((L, MLA_Q_LORA)),
        'mla_w_qb': nrm((L, MLA_Q_LORA, MLA_HEADS * (MLA_NOPE + MLA_ROPE)), MLA_Q_LORA ** -0.5),
        'mla_kv_norm': gain((L, MLA_KV_LORA)),
        'mla_w_kvb': nrm((L, MLA_KV_LORA, MLA_HEADS * (MLA_NOPE + MLA_V)), MLA_KV_LORA ** -0.5),
        'w_branch': nrm((L, N_BRANCH, BRANCH_W, D_MODEL), BRANCH_W ** -0.5),
        'w_o': nrm((L, D_MODEL, D_MODEL), D_MODEL ** -0.5),
        'ffn_norm': gain((L, D_MODEL)),
        'ffn_w_gate': nrm((N_DENSE, D_MODEL, D_FF), D_MODEL ** -0.5),
        'ffn_w_up': nrm((N_DENSE, D_MODEL, D_FF), D_MODEL ** -0.5),
        'ffn_w_down': nrm((N_DENSE, D_FF, D_MODEL), D_FF ** -0.5),
        'moe_router': nrm((N_MOE, D_MODEL, N_EXPERTS), D_MODEL ** -0.5),
        'moe_w_gate': nrm((N_MOE, N_EXPERTS, D_MODEL, D_FF_EXPERT), D_MODEL ** -0.5),
        'moe_w_up': nrm((N_MOE, N_EXPERTS, D_MODEL, D_FF_EXPERT), D_MODEL ** -0.5),
        'moe_w_down': nrm((N_MOE, N_EXPERTS, D_FF_EXPERT, D_MODEL), D_FF_EXPERT ** -0.5),
        'final_norm': gain((D_MODEL,)),
    }

def reference(x, positions, attn_norm, w_in, rwkv_mu, rwkv_w0, rwkv_w2, rwkv_a0, rwkv_a2, rwkv_g2,
              rwkv_k_k, rwkv_k_a, rwkv_r_k, rwkv_lnx_w, mla_q_norm, mla_w_qb, mla_kv_norm, mla_w_kvb,
              w_branch, w_o, ffn_norm, ffn_w_gate, ffn_w_up, ffn_w_down, moe_router, moe_w_gate,
              moe_w_up, moe_w_down, final_norm):
    B, S, _ = x.shape
    dt = x.dtype
    cos_ret, sin_ret = rope_tables(positions, RET_DK)
    cos_mla, sin_mla = rope_tables(positions, MLA_ROPE)
    h = x
    for l in range(DEPTH):
        hn = rms_norm(h, attn_norm[l])
        p = hn @ w_in[l]
        rq, rk, rv, rg, pw, qa, kva, gl = jnp.split(p, IN_SPLITS, axis=-1)
        y_ret = retention_mix(rq, rk, rv, rg, cos_ret, sin_ret)
        y_rwkv = rwkv7_mix(pw, rwkv_mu[l], rwkv_w0[l], rwkv_w2[l], rwkv_a0[l], rwkv_a2[l], rwkv_g2[l],
                           rwkv_k_k[l], rwkv_k_a[l], rwkv_r_k[l], rwkv_lnx_w[l])
        y_mla = mla_mix(qa, kva, mla_q_norm[l], mla_w_qb[l], mla_kv_norm[l], mla_w_kvb[l], cos_mla, sin_mla)
        ys = jnp.stack([y_ret.astype(dt), y_rwkv.astype(dt), y_mla.astype(dt)], axis=2)
        branch = jnp.einsum('bsnc,ncd->bsnd', ys, w_branch[l])
        gates = jax.nn.sigmoid(gl.reshape(B, S, N_BRANCH, D_MODEL))
        merged = jnp.sum(gates * branch, axis=2)
        h = h + (merged @ w_o[l]).astype(dt)
        hn = rms_norm(h, ffn_norm[l])
        if l % 2 == 0:
            f = swiglu(hn, ffn_w_gate[l // 2], ffn_w_up[l // 2], ffn_w_down[l // 2])
        else:
            f = moe_swiglu(hn, moe_router[l // 2], moe_w_gate[l // 2], moe_w_up[l // 2], moe_w_down[l // 2])
        h = h + f.astype(dt)
    return rms_norm(h, final_norm)


_drawn_inputs = setup_inputs


def setup_inputs(seed=0):
    import zlib

    import numpy as np

    out = dict(_drawn_inputs(seed))
    spreads = {}
    factors = {}
    for name, (base, spread) in spreads.items():
        noise = np.random.default_rng([zlib.crc32(name.encode()), seed]).standard_normal(out[name].shape)
        drawn = base * np.exp(spread * noise) if base else spread * noise
        out[name] = jnp.asarray(drawn.astype(out[name].dtype))
    for name, factor in factors.items():
        out[name] = (out[name] * factor).astype(out[name].dtype)
    return out
```

```python
import numpy as np
import concourse.bass as bass
from concourse import mybir

F32 = mybir.dt.float32
I32 = mybir.dt.int32
ALU = mybir.AluOpType
ACT = mybir.ActivationFunctionType
AX = mybir.AxisListType

P = 128
SEQ, D, DEPTH, CHUNK = 256, 1024, 2, 64
T = SEQ // P
KD = D // P
RH, RW = 4, 512
NH, HD, W = 8, 64, 512
LORA = 288
RWCOLS = 3 * W + LORA
NOPE, ROPE, QK = 64, 32, 96
MLAC = 256 + 160
DFF, NE, FE = 2816, 8, 3584
DECAY = float(np.exp(-0.5))
EPS = 1e-6
RING = 3
BANKS = 8
SLOT = 4096

C_RET, C_RWKV, C_MLA, C_GATE = 0, 2048, 2048 + RWCOLS, 2048 + RWCOLS + MLAC


def constants():
    i = np.arange(P)
    same = (i[:, None] // CHUNK) == (i[None, :] // CHUNK)
    s, t = i[:, None], i[None, :]
    c = {"ident": np.eye(P)}
    c["ones"] = np.ones((P, P))
    c["upto"] = (s <= t)
    c["chunk_upto"] = (s <= t) & same
    c["chunk_sel"] = np.stack([i < CHUNK, i >= CHUNK], 1)
    strict = (s < t) & same
    incl = (s <= t) & same
    c["pair_mask"] = np.concatenate([-1.0 * strict, incl, -1.0 * strict, incl], 1)
    c["a_mask"] = -1.0 * ((s > t) & same)
    b = 1
    lv = []
    while b < CHUNK:
        lv.append((s // (2 * b) == t // (2 * b)) & ((s // b) % 2 == 1) & ((t // b) % 2 == 0))
        b *= 2
    c["levels"] = np.concatenate([x.astype(np.float64) for x in lv], 1)
    c["level0_t"] = lv[0].T
    g = np.arange(SEQ)
    lg = np.log(1.0 - 2.0 ** (-5.0 - np.arange(RH)))
    ret = []
    for h in range(RH):
        m = np.exp(lg[h] * np.abs(g[None, :] - i[:, None])) * 128 ** -0.5
        ret.append(m * (i[:, None] // CHUNK <= g[None, :] // CHUNK))
    c["ret_mask"] = np.concatenate(ret, 1)
    c["mla_mask"] = np.where(i[None, :] // CHUNK <= i[:, None] // CHUNK, 0.0, -1e30)
    c["slots"] = np.tile(np.arange(P, dtype=np.float64), (P, 1))
    f32 = np.float32
    inv = [f32(1.0) / (f32(10000.0) ** (np.arange(0, d, 2, dtype=f32) / f32(d))) for d in (128, ROPE)]
    c["inv_freq"] = np.tile(np.concatenate(inv), (P, 1))
    c["experts"] = np.tile(np.arange(NE, dtype=np.float64), (P, 1))
    out, at = {}, 0
    for k, v in c.items():
        v = v.astype(np.float32)
        out[k] = (at, v.shape[1])
        at += v.shape[1]
    return out, np.ascontiguousarray(np.concatenate([v.astype(np.float32) for v in c.values()], 1))


CONST_AT, CONST = constants()
LEVELS = 6
VECTORS = ["mu", "w0", "a0", "k_k", "k_a", "r_k", "lnx"]
VEC_AT = {"mu": (0, RWCOLS)}
for _n, _v in enumerate(VECTORS[1:]):
    VEC_AT[_v] = (RWCOLS + _n * W, W)
VEC_COLS = RWCOLS + 6 * W

TWO_PI = [6.28125]
_left = 2 * np.pi - TWO_PI[0]
_c2 = float(np.round(_left * 2 ** 20) / 2 ** 20)
TWO_PI += [_c2, float(np.float32(_left - _c2))]
ROUND = 1.5 * 2 ** 23


def panels():
    out = []
    for l in range(DEPTH):
        out += [("in", l, j, 1) for j in range(9)]
        out += [("lora", l, 0, 4), ("mla", l, 0, 2)]
        for n in range(3):
            out += [("gate", l, 2 * n, 1), ("gate", l, 2 * n + 1, 1), ("branch", l, n, 1)]
        out += [("o", l, 0, 1), ("o", l, 1, 1)]
        if l == 0:
            for j in range(6):
                out += [("ffn_gate", 0, j, 1), ("ffn_up", 0, j, 1)]
            out += [("ffn_down", 0, j, 1) for j in range(6)]
    return out


IN_PANELS = [(C_RWKV + 1536, LORA), (C_RWKV, 512), (C_RWKV + 512, 512), (C_RWKV + 1024, 512),
             (0, 512), (512, 512), (1024, 512), (1536, 512), (C_MLA, MLAC)]
FFN_COLS = [512] * 5 + [256]


def layer_jobs(l):
    A, V = "act", "vec"
    out = [(f"nT{q}", A) for q in range(4)]
    out += [(f"in{j}_{t}", A) for j in range(9) for t in range(T)]
    out += [(f"loT{t}", A) for t in range(T)]
    out += [(f"{n}{t}", e) for t in range(T) for n, e in (("z", V), ("a", V), ("g", A))]
    out += [(f"rT{s}{t}", A) for t in range(T) for s in range(2)]
    out += [(f"sR{h}", V) for h in range(RH)]
    out += [(f"cum{t}", A) for t in range(T)] + [("pc", A)]
    out += [(f"oR{t}", A) for t in range(T)]
    out += [(f"cT{t}", A) for t in range(T)]
    out += [(f"mq{t}{u}", A) for t in range(T) for u in range(2)]
    out += [(f"mk{t}{u}", A) for t in range(T) for u in range(2)]
    out += [(f"mT{s}{u}", A) for s in range(2) for u in range(4)]
    for i in range(NH + 2):
        out += [(f"sM{i}", V)] * (i < NH) + [(f"pT{i - 1}", A)] * (0 < i <= NH) + [(f"oM{i - 2}", V)] * (i > 1)
    for t in range(T):
        out += [(f"kT{t}{hp}", A) for hp in range(4)]
        out += [(f"M{t}{i}", V) for i in range(NH)] + [(f"A{t}{g}", V) for g in range(2)]
        for lv in range(1, LEVELS):
            out += [(f"T{t}{lv}{g}", V) for g in range(2)]
            for g in range(2):
                out += [(f"X{t}{lv}{g}", V)] * (lv < LEVELS - 1) + [(f"XT{t}{lv}{g}", V)]
        out += [(f"W{t}", A), (f"Z{t}", A), (f"U{t}", A)]
        for n in (2 * t, 2 * t + 1):
            out += [(f"dU{n}{e}", V) for e in range(2)] * (n > 0) + [(f"S{n + 1}", V)] * (n < 3)
        out += [(f"Y{t}{e}", A) for e in range(2)]
    for n in range(3):
        out += [(f"yT{n}{u}", A) for u in range(2)]
        out += [(f"gt{n}{u}{t}", A) for u in range(2) for t in range(T)]
        out += [(f"br{n}{u}{t}", V) for u in range(2) for t in range(T)]
    out += [(f"gT{q}", A) for q in range(4)]
    out += [(f"o{u}{t}", V) for u in range(2) for t in range(T)]
    out += [(f"fT{q}", A) for q in range(4)]
    if l == 0:
        for j in range(7):
            if j < 6:
                out += [(f"fg{j}{t}", A) for t in range(T)] + [(f"fu{j}{t}", V) for t in range(T)]
            if j > 0:
                out += [(f"hT{j - 1}{t}", A) for t in range(T)]
        out += [(f"fd{u}{t}", V) for u in range(2) for t in range(T)]
    else:
        out += [("router", V), ("rank", V)]
    return [(f"{n}.{l}", e) for n, e in out]


def moe_jobs():
    A, V = "act", "vec"
    out = [("csT", A), ("gx0", A), ("gx1", A)]
    for j in range(8):
        out += ([(f"eg{j}", A), (f"eu{j}", V)] if j < 7 else []) + ([(f"eT{j - 1}", A)] if j else [])
    out += [("ed0", V), ("ed1", V)]
    out += [(f"sc{u}{t}", V) for u in range(2) for t in range(T)]
    return out


JOBS = layer_jobs(0) + layer_jobs(1)
JOB_AT = {n: i for i, (n, _) in enumerate(JOBS)}
ITEM = moe_jobs()
ITEM_AT = {n: i for i, (n, _) in enumerate(ITEM)}
PANELS = panels()
EP = 21
SURE = NE


def freed_count(k, eng):
    return sum(e == eng for _, e in JOBS[:k + 1])


def item_freed(k, eng):
    return sum(e == eng for _, e in ITEM[:k + 1])


class Own:

    def __init__(self, eng, name, step_sem, freed_sem):
        self.eng, self.name, self.step_sem, self.freed_sem = eng, name, step_sem, freed_sem
        self.count, self.last = {}, None

    def step(self, ins, sem=None):
        sem = sem or self.step_sem
        self.count[id(sem)] = self.count.get(id(sem), 0) + 1
        ins.then_inc(sem, 1)
        self.last = (sem, self.count[id(sem)])

    def free(self, ins, job):
        self.step(ins, self.freed_sem)
        assert JOBS[JOB_AT[job]][1] == self.name
        assert self.count[id(self.freed_sem)] == freed_count(JOB_AT[job], self.name), job

    def settle(self):
        self.eng.wait_ge(*self.last)


class Signals:

    def __init__(self, nc):
        new = nc.alloc_semaphore
        self.const_loaded = new("const_loaded")
        self.pos_loaded = new("pos_loaded")
        self.x_loaded = new("x_loaded")
        self.vec_loaded = new("vec_loaded")
        self.gain_loaded = new("gain_loaded")
        self.router_loaded = new("router_loaded")
        self.fgain_loaded = new("fgain_loaded")
        self.down_used = new("down_used")
        self.product_ready = new("product_ready")
        self.freed_act = new("freed_act")
        self.freed_vec = new("freed_vec")
        self.act_step = new("act_step")
        self.vec_step = new("vec_step")
        self.pool_step = new("pool_step")
        self.out_stored = new("out_stored")
        self.angles_ready = new("angles_ready")
        self.trig_ready = new("trig_ready")
        self.sumsq_ready = new("sumsq_ready")
        self.var_ready = new("var_ready")
        self.root_ready = new("root_ready")
        self.hn_ready = new("hn_ready")
        self.shift_zero = new("shift_zero")
        self.shift_loaded = new("shift_loaded")
        self.xs_ready = new("xs_ready")
        self.lora_act_ready = new("lora_act_ready")
        self.knsq_ready = new("knsq_ready")
        self.knroot_ready = new("knroot_ready")
        self.decay_sig_ready = new("decay_sig_ready")
        self.rate_sig_ready = new("rate_sig_ready")
        self.logd_ready = new("logd_ready")
        self.exps_ready = new("exps_ready")
        self.cex_ready = new("cex_ready")
        self.scan_in_ready = new("scan_in_ready")
        self.rope_ready = new("rope_ready")
        self.silu_g_ready = new("silu_g_ready")
        self.gn_var_ready = new("gn_var_ready")
        self.gn_root_ready = new("gn_root_ready")
        self.ret_done = new("ret_done")
        self.qa_sumsq = new("qa_sumsq")
        self.qa_ready = new("qa_ready")
        self.mla_key_ready = new("mla_key_ready")
        self.masked_ready = new("masked_ready")
        self.prob_ready = new("prob_ready")
        self.merged_done = new("merged_done")
        self.x_ready = new("x_ready")
        self.state_ready = new("state_ready")
        self.rwkv_done = new("rwkv_done")
        self.route_exp = new("route_exp")
        self.route_diff = new("route_diff")
        self.mask_ready = new("mask_ready")
        self.items_ready = new("items_ready")
        self.sel_ready = new("sel_ready")
        self.item_step = new("item_step")
        self.fin_ready = new("fin_ready")
        self.items_done = new("items_done")


def build(nc, x, positions, attn_norm, w_in, rwkv_mu, rwkv_w0, rwkv_w2, rwkv_a0, rwkv_a2, rwkv_g2, rwkv_k_k,
          rwkv_k_a, rwkv_r_k, rwkv_lnx_w, mla_q_norm, mla_w_qb, mla_kv_norm, mla_w_kvb, w_branch, w_o, ffn_norm,
          ffn_w_gate, ffn_w_up, ffn_w_down, moe_router, moe_w_gate, moe_w_up, moe_w_down, final_norm, const, out):
    at = [-(-int(nc.sbuf_base) // 64) * 64]

    def sb(name, shape, dt=F32, where=None):
        size = -(-int(np.prod(shape[1:])) * 4 // 32) * 32
        if where is None:
            where = at[0]
            at[0] += size
        return nc.alloc_sbuf_tensor_at(name, shape, dt, offset=where)

    h = sb("h", [P, T, D])
    hnT = sb("hnT", [P, KD, SEQ])
    hn_at = at[0]
    hn = sb("hn", [P, T, D])
    y_ret = sb("y_ret", [P, T, W], where=hn_at)
    y_mla = sb("y_mla", [P, T, W], where=hn_at + 4096)
    ring = sb("ring", [P, RING, SLOT])
    cst = sb("cst", [P, CONST.shape[1]])
    vec = sb("vec", [P, VEC_COLS])
    gains = sb("gains", [P, DEPTH, 2, KD])
    mgain = sb("mgain", [P, DEPTH, 3])
    cosT = sb("cosT", [P, T, 80])
    sinT = sb("sinT", [P, T, 80])
    pos_i = sb("pos_i", [P, T], I32)
    pos_f = sb("pos_f", [P, T])
    stat = sb("stat", [P, 8, 16])
    den = sb("den", [P, NH, T])
    smax = sb("smax", [P, NH, T])
    decay_end = sb("decay_end", [P, T, 4, 2])
    pr = sb("pr", [P, T, RWCOLS])
    E = at[0]
    prev = sb("prev", [P, T, RWCOLS])
    kk = sb("kk", [P, T, W], where=E)
    tmp = sb("tmp", [P, T, W], where=E + 4096)
    ab = sb("ab", [P, T, W], where=E + 8192)
    ld = sb("ld", [P, T, W])
    ec_at = at[0]
    ec = sb("ec", [P, T, W])
    enc = sb("enc", [P, T, W])
    gg = sb("gg", [P, T, W])
    y_rwkv = sb("y_rwkv", [P, T, W], where=ec_at)
    qa = sb("qa", [P, T, MLAC])
    B = at[0]
    raw = sb("raw", [P, T, 4, W], where=B)
    qkT = sb("qkT", [P, 2, RH, T, P], where=B + 16384)
    rope_tmp = sb("rope_tmp", [P, 2048], where=B + 16384)
    sR = sb("sR", [P, RH, 384], where=B + 24576)
    mqT = sb("mqT", [P, NH, SEQ], where=B)
    mkT = sb("mkT", [P, NH, SEQ], where=B + 8192)
    mq = sb("mq", [P, T, NH, QK], where=B + 30720)
    mk = sb("mk", [P, T, NH, QK], where=B + 36864)
    mv = sb("mv", [P, T, NH, NOPE], where=B + 43008)
    sm = sb("sm", [P, 2, 384], where=B + 47104)
    pT = sb("pT", [P, 2, 384], where=B + 50176)
    loT = sb("loT", [P, T, 384], where=B + 47104)
    cT = sb("cT", [P, 3, SEQ], where=B + 50176)
    mrope_tmp = sb("mrope_tmp", [P, 4, P], where=B + 47104)
    tT = sb("tT", [P, 4, 512], where=B)
    m1 = sb("m1", [P, NH, 512], where=B + 8192)
    am = sb("am", [P, NH, P], where=B + 24576)
    xi = sb("xi", [P, NH, P], where=B + 28672)
    xt = sb("xt", [P, NH, P], where=B + 32768)
    t1 = sb("t1", [P, NH, P], where=B + 36864)
    zz = sb("zz", [P, W], where=B + 40960)
    uu = sb("uu", [P, T, W], where=B + 43008)
    nw = sb("nw", [P, 4, P], where=B + 47104)
    st = sb("st", [P, 3, 4, HD], where=B + 49152)
    merged = sb("merged", [P, T, D], where=B)
    sig = sb("sig", [P, 2, 2, T, 512], where=B + 8192)
    yT = sb("yT", [P, 2, 4, SEQ], where=B + 24576)
    gT = sb("gT", [P, KD, SEQ], where=B + 32768)
    hmT = sb("hmT", [P, 22, SEQ], where=B)
    hm = sb("hm", [P, 2, T, 512], where=B + 24576)
    sg = sb("sg", [P, 2, T, 512], where=B + 32768)
    sel = sb("sel", [P, T, P], where=E)
    csel = sb("csel", [P, T, P], where=E + 1024)
    cselT = sb("cselT", [P, SEQ], where=E + 2048)
    xg = sb("xg", [P, KD, P], where=E + 3072)
    ehT = sb("ehT", [P, 28, P], where=E + 7168)
    ehm = sb("ehm", [P, 2, 512], where=E + 21504)
    esg = sb("esg", [P, 2, 512], where=E + 25600)
    ey = sb("ey", [P, D], where=E + 29696)
    rt = sb("rt", [P, 16, T, NE], where=B + 32768)
    router = sb("router", [P, KD, NE], where=B + 33792)
    it_f = sb("it_f", [1, 64], where=B + 34048)
    items = sb("items", [1, 32], I32, where=B + 34304)
    spos = sb("spos", [P, 2, T, NE], where=B + 34432)
    comb = sb("comb", [P, 2, T, NE], where=B + 34560)
    fin = sb("fin", [P, T, D], where=B)
    fgain = sb("fgain", [P, D], where=B + 8192)
    assert B + 53248 <= int(nc.sbuf_usable_end), (B, int(nc.sbuf_usable_end))

    def C(name, a=0, b=None):
        o, n = CONST_AT[name]
        return cst[:, o + a:o + (n if b is None else b)]

    def VEC(name, a=0, b=None):
        o, n = VEC_AT[name]
        return vec[:, o + a:o + (n if b is None else b)]

    def each(ap, n=T):
        return ap.unsqueeze(1).to_broadcast([ap.shape[0], n, ap.shape[1]])

    def wide(ap, n):
        return ap.unsqueeze(len(ap.shape)).to_broadcast(list(ap.shape) + [n])

    banks = [nc.alloc_psum_tensor(f"bank{i}", [P, 512], F32) for i in range(BANKS)]

    s = Signals(nc)
    slot_loaded = [nc.alloc_semaphore(f"slot{i}_loaded") for i in range(RING)]
    freed = {"act": s.freed_act, "vec": s.freed_vec}
    FR = {e: freed_count(len(JOBS) - 1, e) for e in freed}
    IF = {e: item_freed(len(ITEM) - 1, e) for e in freed}
    NPAN = len(PANELS)

    def product(eng, job):
        eng.wait_ge(s.product_ready, JOB_AT[job] + 1)
        return banks[JOB_AT[job] % BANKS]

    def read_out(eng, job):
        k = JOB_AT[job]
        eng.wait_ge(freed[JOBS[k][1]], freed_count(k, JOBS[k][1]))

    def used_up(n):
        kind, l, j, _ = PANELS[n]
        if kind == "ffn_down" and j < 5:
            return s.down_used, j + 1
        job = {"in": f"in{j}_1.{l}", "lora": f"g1.{l}", "mla": f"mk11.{l}", "gate": f"gt{j // 2}{j % 2}1.{l}",
               "branch": f"br{j}11.{l}", "o": f"o{j}1.{l}", "ffn_gate": f"fg{j}1.{l}", "ffn_up": f"fu{j}1.{l}",
               "ffn_down": "fd11.0"}[kind]
        return s.product_ready, JOB_AT[job] + 1

    def item_used_up(m, item):
        before, m = (1, m + EP) if m < 0 else (0, m)
        if 14 <= m < EP - 1:
            return s.down_used, item * 6 + (5 + m - 13 - 6 * before)
        job = f"e{'gu'[m % 2]}{m // 2}" if m < 14 else "ed1"
        return s.product_ready, item * len(ITEM) + (len(JOBS) + ITEM_AT[job] + 1 - len(ITEM) * before)

    def rows(w):
        return w.rearrange("(p c) n -> p c n", p=P)

    blk = nc.Block()
    block = blk.__enter__()

    @block.sync
    def _(sp):
        sp.dma_start(cst[:], const).then_inc(s.const_loaded, 16)
        for t in range(T):
            sp.dma_start(h[:, t, :], x[0, t * P:(t + 1) * P, :]).then_inc(s.x_loaded, 16)
        for n, (kind, l, j, _) in enumerate(PANELS):
            if n >= RING:
                sp.wait_ge(*used_up(n - RING))
            slot = ring[:, n % RING, :]
            sem = slot_loaded[n % RING]

            def cols(w, c0, width):
                k = w.shape[0] // P
                dst = slot[:, 0:k * width].rearrange("p (c n) -> p c n", c=k)
                sp.dma_start(dst, rows(w)[:, :, c0:c0 + width]).then_inc(sem, 16)

            if kind == "in":
                cols(w_in[l], *IN_PANELS[j])
            elif kind == "gate":
                cols(w_in[l], C_GATE + 512 * j, 512)
            elif kind == "lora":
                sp.dma_start(slot[0:64, 0:512], rwkv_w2[l]).then_inc(sem, 16)
                sp.dma_start(slot[64:128, 0:512], rwkv_a2[l]).then_inc(sem, 16)
                sp.dma_start(slot[:, 512:1024], rwkv_g2[l, 0:128, :]).then_inc(sem, 16)
                sp.dma_start(slot[0:32, 1024:1536], rwkv_g2[l, 128:160, :]).then_inc(sem, 16)
            elif kind == "mla":
                sp.dma_start(slot[:, 0:1536].rearrange("p (c n) -> p c n", c=2), rows(mla_w_qb[l])).then_inc(sem, 16)
                sp.dma_start(slot[:, 1536:2560], mla_w_kvb[l]).then_inc(sem, 16)
            elif kind == "branch":
                cols(w_branch[l, j], 0, D)
            elif kind == "o":
                cols(w_o[l], 512 * j, 512)
            elif kind == "ffn_gate":
                cols(ffn_w_gate[0], 512 * j, FFN_COLS[j])
            elif kind == "ffn_up":
                cols(ffn_w_up[0], 512 * j, FFN_COLS[j])
            else:
                cols(ffn_w_down[0, 512 * j:512 * j + FFN_COLS[j], :], 0, D)

        def expert_panels(e, item):
            for m in range(EP):
                i = (NPAN + m) % RING
                sp.wait_ge(*item_used_up(m - RING, item))
                if m < 14:
                    w = (moe_w_gate, moe_w_up)[m % 2][0, bass.ds(e, 1), :, 512 * (m // 2):512 * (m // 2) + 512]
                    k = KD
                else:
                    w = moe_w_down[0, bass.ds(e, 1), 512 * (m - 14):512 * (m - 14) + 512, :]
                    k = 4
                sp.dma_start(ring[:, i, :].rearrange("p (c n) -> p c n", c=k),
                             w.rearrange("o (p c) n -> p (o c) n", p=P)).then_inc(slot_loaded[i], 16)

        sp.wait_ge(*used_up(NPAN - 1))
        with sp.Fori(0, SURE) as item:
            expert_panels(item, item)
        sp.wait_ge(s.items_ready, 1)
        n_items = sp.value_load(items[0:1, 24:25], min_val=SURE, max_val=SURE + 3)
        with sp.If(n_items > SURE):
            with sp.Fori(SURE, n_items) as item:
                e = sp.value_load(items[0:1, bass.ds(item + 12, 1)], min_val=0, max_val=NE - 1)
                expert_panels(e, item)
            sp.nop()
        with sp.Else():
            sp.nop()
        for t in range(T):
            sp.wait_ge(s.fin_ready, t + 1)
            sp.dma_start(out[0, t * P:(t + 1) * P, :], fin[:, t, :]).then_inc(s.out_stored, 16)
        sp.wait_ge(s.out_stored, 16 * T)

    @block.gpsimd
    def _(pool):
        for t in range(T):
            pool.dma_start(pos_i[:, t:t + 1], positions[:, t * P:(t + 1) * P].rearrange("a p -> p a"))\
                .then_inc(s.pos_loaded, 16)
        for l in range(DEPTH):
            for g, w in enumerate((attn_norm, ffn_norm)):
                pool.dma_start(gains[:, l, g, :], w[l].rearrange("(p c) -> p c", p=P)).then_inc(s.gain_loaded, 16)
            pool.dma_start(mgain[:, l, 0:2], mla_q_norm[l].rearrange("(p c) -> p c", p=P)).then_inc(s.gain_loaded, 16)
            pool.dma_start(mgain[:, l, 2:3], mla_kv_norm[l].rearrange("(p c) -> p c", p=P)).then_inc(s.gain_loaded, 16)
        own = Own(pool, "pool", s.pool_step, None)
        G = nc.gpsimd

        def rotate(x1, x2, c, sn, f, ready):
            own.step(G.tensor_tensor(f[0], x1, sn, ALU.mult))
            own.step(G.tensor_tensor(f[1], x2, sn, ALU.mult))
            own.step(G.tensor_tensor(f[2], x1, c, ALU.mult))
            own.step(G.tensor_tensor(f[3], x2, c, ALU.mult))
            own.settle()
            own.step(G.tensor_tensor(x1, f[2], f[1], ALU.subtract))
            own.step(G.tensor_tensor(x2, f[0], f[3], ALU.add), ready)

        for l in range(DEPTH):
            if l:
                pool.wait_ge(s.rwkv_done, l)
            for name, w in (("mu", rwkv_mu[l]), ("w0", rwkv_w0[l]), ("a0", rwkv_a0[l]), ("k_k", rwkv_k_k[l]),
                            ("k_a", rwkv_k_a[l]), ("r_k", rwkv_r_k[l].rearrange("h d -> (h d)")),
                            ("lnx", rwkv_lnx_w[l])):
                pool.dma_start(VEC(name), w.partition_broadcast(P)).then_inc(s.vec_loaded, 16)
            own.step(G.memset(prev[0:1, 0, :], 0.0), s.shift_zero)
            pool.wait_ge(s.trig_ready, 2)
            read_out(pool, f"in5_1.{l}")
            for t in range(T):
                qk = raw[:, t, 0:2, :].rearrange("p a (h e) -> p (a h) e", h=RH)
                c = each(cosT[:, t, 0:64], 8)
                sn = each(sinT[:, t, 0:64], 8)
                f = [rope_tmp[:, 512 * i:512 * i + 512].rearrange("p (h e) -> p h e", h=8) for i in range(4)]
                if t:
                    own.settle()
                rotate(qk[:, :, 0:64], qk[:, :, 64:128], c, sn, f, s.rope_ready)
            read_out(pool, f"mk11.{l}")
            for t in range(T):
                own.settle()
                f = [mrope_tmp[:, i, :].rearrange("p (h e) -> p h e", h=8) for i in range(4)]
                rotate(mq[:, t, :, 64:80], mq[:, t, :, 80:96], each(cosT[:, t, 64:80], 8),
                       each(sinT[:, t, 64:80], 8), f, s.pool_step)
                own.settle()
                rotate(qa[:, t, 384:400], qa[:, t, 400:416], cosT[:, t, 64:80], sinT[:, t, 64:80],
                       [mrope_tmp[:, i, 0:16] for i in range(4)], s.pool_step)
                own.settle()
                own.step(G.tensor_copy(mk[:, t, :, 64:96], each(qa[:, t, 384:416], NH)), s.mla_key_ready)
        read_out(pool, "o11.1")
        pool.dma_start(router[:], moe_router[0].rearrange("(p c) n -> p c n", p=P)).then_inc(s.router_loaded, 16)
        pool.dma_start(fgain[:], final_norm.partition_broadcast(P)).then_inc(s.fgain_loaded, 16)

    @block.scalar
    def _(act):
        own = Own(act, "act", s.act_step, s.freed_act)
        A = nc.scalar

        def norm_sums(m):
            for t in range(T):
                own.step(A.activation(hn[:, t, :], h[:, t, :], ACT.Square, accum_out=stat[:, 0, t:t + 1]),
                         s.sumsq_ready)
            act.wait_ge(s.var_ready, m + 1)
            own.step(A.activation(stat[:, 0, 0:T], stat[:, 0, 0:T], ACT.Sqrt), s.root_ready)

        def norm_transposed(name, l, g):
            for q in range(4):
                b = product(act, f"{name}{q}.{l}")
                for i in range(2):
                    c = 2 * q + i
                    ins = A.activation(hnT[:, c, :], b[:, 256 * i:256 * i + 256], ACT.Copy,
                                       scale=gains[:, l, g, c:c + 1])
                    own.step(ins) if i == 0 else own.free(ins, f"{name}{q}.{l}")

        def copy_out(job, dst, cols=None, rows_=P, scale=1.0):
            b = product(act, job)
            src = b[0:rows_, 0:cols or 512]
            if len(dst.shape) == 3:
                src = src.rearrange("p (a b) -> p a b", a=dst.shape[1])
            own.free(A.activation(dst, src, ACT.Copy, scale=scale), job)

        act.wait_ge(s.angles_ready, 1)
        own.step(A.activation(sinT[:], sinT[:], ACT.Sin), s.trig_ready)
        own.step(A.activation(cosT[:], cosT[:], ACT.Sin), s.trig_ready)
        act.wait_ge(s.gain_loaded, 16 * 4 * DEPTH)
        for l in range(DEPTH):
            if l:
                read_out(act, f"fd11.{l - 1}")
            else:
                act.wait_ge(s.x_loaded, 16 * T)
            norm_sums(2 * l)
            norm_transposed("nT", l, 0)
            for j, (c0, width) in enumerate(IN_PANELS):
                for t in range(T):
                    if j < 4:
                        o = 1536 if j == 0 else 512 * (j - 1)
                        dst = pr[:, t, o:o + width]
                    elif j < 8:
                        dst = raw[:, t, j - 4, :]
                    else:
                        dst = qa[:, t, :]
                    copy_out(f"in{j}_{t}.{l}", dst, width)
                if j == 3:
                    own.settle()
                    act.wait_ge(s.shift_zero, l + 1)
                    act.dma_start(prev[1:P, :, :], pr[0:P - 1, :, :]).then_inc(s.shift_loaded, 16)
                    act.dma_start(prev[0:1, 1, :], pr[P - 1:P, 0, :]).then_inc(s.shift_loaded, 16)
            own.settle()
            for t in range(T):
                own.step(A.activation(hn[:, t, 0:256], qa[:, t, 0:256], ACT.Square,
                                      accum_out=stat[:, 2, 2 * t:2 * t + 1]), s.qa_sumsq)
                own.step(A.activation(hn[:, t, 256:384], qa[:, t, 256:384], ACT.Square,
                                      accum_out=stat[:, 2, 2 * t + 1:2 * t + 2]), s.qa_sumsq)
            own.step(A.activation(raw[:, :, 3, :], raw[:, :, 3, :], ACT.Silu), s.silu_g_ready)
            act.wait_ge(s.xs_ready, l + 1)
            own.step(A.activation(pr[:, :, 1536:1600], pr[:, :, 1536:1600], ACT.Tanh))
            own.step(A.activation(pr[:, :, 1664:1824], pr[:, :, 1664:1824], ACT.Sigmoid), s.lora_act_ready)
            for t in range(T):
                b = product(act, f"loT{t}.{l}")
                own.step(A.activation(loT[:, t, 0:256], b[:, 0:256], ACT.Copy))
                own.free(A.activation(loT[0:32, t, 256:384], b[0:32, 256:384], ACT.Copy), f"loT{t}.{l}")
            for t in range(T):
                copy_out(f"g{t}.{l}", gg[:, t, :])
            read_out(act, f"z1.{l}")
            own.step(A.activation(ld[:], ld[:], ACT.Sigmoid), s.decay_sig_ready)
            read_out(act, f"a1.{l}")
            own.step(A.activation(ab[:], ab[:], ACT.Sigmoid), s.rate_sig_ready)
            act.wait_ge(s.knsq_ready, l + 1)
            own.step(A.activation(stat[:, 1, :], stat[:, 1, :], ACT.Sqrt))
            own.step(A.activation(stat[:, 2, 0:4], stat[:, 2, 0:4], ACT.Sqrt), s.knroot_ready)
            act.wait_ge(s.rope_ready, T * (l + 1))
            for t in range(T):
                for q in range(2):
                    copy_out(f"rT{q}{t}.{l}", qkT[:, q, :, t, :])
            for t in range(T):
                b = product(act, f"cum{t}.{l}")
                own.step(A.activation(ec[:, t, :], b[:], ACT.Exp))
                own.step(A.activation(enc[:, t, :], b[:], ACT.Exp, scale=-1.0), s.exps_ready)
            for t in range(T):
                act.wait_ge(s.cex_ready, T * l + t + 1)
                own.free(A.activation(ld[:, t, :], ld[:, t, :], ACT.Exp), f"cum{t}.{l}")
            b = product(act, f"pc.{l}")
            own.free(A.activation(decay_end[:], b[:, 0:16].rearrange("p (t a c) -> p t a c", t=T, a=4), ACT.Exp),
                     f"pc.{l}")
            for t in range(T):
                copy_out(f"oR{t}.{l}", y_ret[:, t, :])
            act.wait_ge(s.gn_var_ready, 2 * l + 1)
            own.step(A.activation(stat[:, 4, 0:8], stat[:, 4, 0:8], ACT.Sqrt), s.gn_root_ready)
            for t in range(T):
                b = product(act, f"cT{t}.{l}")
                for i in range(3):
                    ins = A.activation(cT[:, i, t * P:(t + 1) * P], b[:, i * P:(i + 1) * P], ACT.Copy,
                                       scale=mgain[:, l, i:i + 1])
                    own.step(ins) if i < 2 else own.free(ins, f"cT{t}.{l}")
            for t in range(T):
                for u in range(2):
                    copy_out(f"mq{t}{u}.{l}", mq[:, t, 4 * u:4 * u + 4, :], 384)
            for t in range(T):
                for u in range(2):
                    b = product(act, f"mk{t}{u}.{l}")
                    kv = b[:].rearrange("p (h e) -> p h e", h=4)
                    own.step(A.activation(mk[:, t, 4 * u:4 * u + 4, 0:64], kv[:, :, 0:64], ACT.Copy))
                    own.free(A.activation(mv[:, t, 4 * u:4 * u + 4, :], kv[:, :, 64:128], ACT.Copy),
                             f"mk{t}{u}.{l}")
            act.wait_ge(s.ret_done, l + 1)
            for q, dst in enumerate((mqT, mkT)):
                for u in range(4):
                    copy_out(f"mT{q}{u}.{l}", dst[0:QK, 2 * u:2 * u + 2, :], rows_=QK)
            for i in range(NH + 1):
                if i < NH:
                    act.wait_ge(s.masked_ready, NH * l + i + 1)
                    own.step(A.activation(sm[:, i % 2, 0:128], sm[:, i % 2, 0:128], ACT.Exp,
                                          bias=smax[:, i, 0:1], accum_out=den[:, i, 0:1]))
                    own.step(A.activation(sm[:, i % 2, 128:384], sm[:, i % 2, 128:384], ACT.Exp,
                                          bias=smax[:, i, 1:2], accum_out=den[:, i, 1:2]), s.prob_ready)
                if i:
                    copy_out(f"pT{i - 1}.{l}", pT[:, (i - 1) % 2, :], 384)
            for t in range(T):
                for hp in range(4):
                    copy_out(f"kT{t}{hp}.{l}", tT[:, hp, :])
                copy_out(f"W{t}.{l}", nw[:], scale=-1.0)
                copy_out(f"Z{t}.{l}", zz[:])
                copy_out(f"U{t}.{l}", uu[:, t, :])
                for e in range(2):
                    copy_out(f"Y{t}{e}.{l}", y_rwkv[:, t, :].rearrange("p (a b d) -> p a b d", a=4, b=2)[:, :, e, :],
                             256)
            act.wait_ge(s.gn_var_ready, 2 * l + 2)
            own.step(A.activation(stat[:, 4, :], stat[:, 4, :], ACT.Sqrt), s.gn_root_ready)
            for n in range(3):
                for u in range(2):
                    copy_out(f"yT{n}{u}.{l}", yT[:, n % 2, 2 * u:2 * u + 2, :])
                if n == 2:
                    read_out(act, f"br011.{l}")
                for u in range(2):
                    for t in range(T):
                        b = product(act, f"gt{n}{u}{t}.{l}")
                        own.free(A.activation(sig[:, n % 2, u, t, :], b[:], ACT.Sigmoid), f"gt{n}{u}{t}.{l}")
            for q in range(4):
                copy_out(f"gT{q}.{l}", gT[:, 2 * q:2 * q + 2, :])
            read_out(act, f"o11.{l}")
            norm_sums(2 * l + 1)
            norm_transposed("fT", l, 1)
            if l == 0:
                for j in range(7):
                    if j < 6:
                        w_ = FFN_COLS[j]
                        for t in range(T):
                            if j > 1:
                                read_out(act, f"fu{j - 2}{t}.0")
                            b = product(act, f"fg{j}{t}.0")
                            own.free(A.activation(sg[:, j % 2, t, 0:w_], b[:, 0:w_], ACT.Silu), f"fg{j}{t}.0")
                    if j:
                        k = FFN_COLS[j - 1] // P
                        for t in range(T):
                            copy_out(f"hT{j - 1}{t}.0", hmT[:, 4 * (j - 1):4 * (j - 1) + k, t * P:(t + 1) * P],
                                     k * P)
        act.wait_ge(s.route_diff, 1)
        own.step(A.activation(stat[:, 6, 0:2], stat[:, 6, 0:2], ACT.Exp), s.route_exp)
        act.wait_ge(s.items_ready, 1)
        n_items = act.value_load(items[0:1, 24:25], min_val=SURE, max_val=SURE + 3)
        with act.Fori(0, n_items) as item:
            def item_product(job):
                act.wait_ge(s.product_ready, item * len(ITEM) + (len(JOBS) + ITEM_AT[job] + 1))
                return banks[ITEM_AT[job] % BANKS]

            A.activation(cselT[:], item_product("csT")[:, 0:SEQ], ACT.Copy).then_inc(s.freed_act, 1)
            for u in range(2):
                b = item_product(f"gx{u}")
                for i in range(4):
                    ins = A.activation(xg[:, 4 * u + i, :], b[:, i * P:(i + 1) * P], ACT.Copy,
                                       scale=gains[:, 1, 1, 4 * u + i:4 * u + i + 1])
                ins.then_inc(s.freed_act, 1)
            for j in range(8):
                if j < 7:
                    if j > 1:
                        act.wait_ge(s.freed_vec, item * IF["vec"] + (FR["vec"] + item_freed(ITEM_AT[f"eu{j - 2}"], "vec")))
                    A.activation(esg[:, j % 2, :], item_product(f"eg{j}")[:], ACT.Silu).then_inc(s.freed_act, 1)
                if j:
                    A.activation(ehT[:, 4 * (j - 1):4 * j, :],
                                 item_product(f"eT{j - 1}")[:].rearrange("p (c n) -> p c n", c=4),
                                 ACT.Copy).then_inc(s.freed_act, 1)
        act.wait_ge(s.items_done, 1)
        norm_sums(4)

    @block.tensor
    def _(pe):
        M, TR = nc.tensor.matmul, nc.tensor.transpose
        ident = C("ident")
        used = [0]

        def bank(job):
            k = JOB_AT[job]
            if k >= BANKS:
                e = JOBS[k - BANKS][1]
                pe.wait_ge(freed[e], freed_count(k - BANKS, e))
            return banks[k % BANKS]

        def panel(kind):
            n = used[0]
            assert PANELS[n][0] == kind, (n, PANELS[n], kind)
            pe.wait_ge(slot_loaded[n % RING], 16 * sum(PANELS[m][3] for m in range(n + 1) if m % RING == n % RING))
            used[0] += 1
            return ring[:, n % RING, :]

        def done(ins):
            ins.then_inc(s.product_ready, 1)

        def transpose_in(jobs, src):
            for q in range(4):
                b = bank(jobs.format(q))
                for i in range(2):
                    for t in range(T):
                        ins = TR(b[:, 256 * i + 128 * t:256 * i + 128 * t + 128], src[:, t, 2 * q + i:D:KD], ident)
                done(ins)

        def project(job, lhs, slot, k, width, t, c0=0, row=None):
            b = bank(job)
            w = slot[:, 0:k * (row or width)].rearrange("p (c n) -> p c n", c=k)
            for c in range(k):
                ins = M(b[:, 0:width], lhs[:, c, t * P:(t + 1) * P], w[:, c, c0:c0 + width], start=c == 0,
                        stop=c == k - 1)
            done(ins)

        pe.wait_ge(s.const_loaded, 16)
        for l in range(DEPTH):
            pe.wait_ge(s.hn_ready, 2 * T * l + T)
            transpose_in("nT{}." + str(l), hn)
            read_out(pe, f"nT3.{l}")
            for j, (_, width) in enumerate(IN_PANELS):
                slot = panel("in")
                for t in range(T):
                    project(f"in{j}_{t}.{l}", hnT, slot, KD, width, t)
            slot = panel("lora")
            pe.wait_ge(s.lora_act_ready, l + 1)
            for t in range(T):
                b = bank(f"loT{t}.{l}")
                TR(b[:, 0:128], pr[:, t, 1536:1664], ident)
                TR(b[:, 128:256], pr[:, t, 1664:1792], ident)
                done(TR(b[0:32, 256:384], pr[:, t, 1792:1824], ident))
            for t in range(T):
                read_out(pe, f"loT{t}.{l}")
                done(M(bank(f"z{t}.{l}")[:], loT[0:64, t, 0:128], slot[0:64, 0:512], start=True, stop=True))
                done(M(bank(f"a{t}.{l}")[:], loT[64:128, t, 0:128], slot[64:128, 0:512], start=True, stop=True))
                b = bank(f"g{t}.{l}")
                M(b[:], loT[:, t, 128:256], slot[:, 512:1024], start=True, stop=False)
                done(M(b[:], loT[0:32, t, 256:384], slot[0:32, 1024:1536], start=False, stop=True))
            for t in range(T):
                pe.wait_ge(s.rope_ready, T * l + t + 1)
                for q in range(2):
                    b = bank(f"rT{q}{t}.{l}")
                    for i in range(RH):
                        ins = TR(b[:, i * P:(i + 1) * P], raw[:, t, q, i * P:(i + 1) * P], ident)
                    done(ins)
            read_out(pe, f"rT11.{l}")
            for i in range(RH):
                b = bank(f"sR{i}.{l}")
                M(b[:, 0:256], qkT[:, 1, i, 0, :], qkT[:, 0, i, :, :], start=True, stop=True)
                done(M(b[:, 256:384], qkT[:, 1, i, 1, :], qkT[:, 0, i, 1, :], start=True, stop=True))
            pe.wait_ge(s.logd_ready, l + 1)
            for t in range(T):
                done(M(bank(f"cum{t}.{l}")[:], C("chunk_upto"), ld[:, t, :], start=True, stop=True))
            b = bank(f"pc.{l}")
            for t in range(T):
                for hp in range(4):
                    o = 2 * (4 * t + hp)
                    ins = M(b[:, o:o + 2], ld[:, t, hp * P:(hp + 1) * P], C("chunk_sel"), start=True, stop=True)
            done(ins)
            read_out(pe, f"sR3.{l}")
            for t in range(T):
                b = bank(f"oR{t}.{l}")
                for i in range(RH):
                    o = b[:, i * P:(i + 1) * P]
                    cols = slice(i * P, (i + 1) * P)
                    if t == 0:
                        ins = M(o, sR[:, i, 0:128], raw[:, 0, 2, cols], start=True, stop=True)
                    else:
                        M(o, sR[:, i, 128:256], raw[:, 0, 2, cols], start=True, stop=False)
                        ins = M(o, sR[:, i, 256:384], raw[:, 1, 2, cols], start=False, stop=True)
                done(ins)
            slot = panel("mla")
            pe.wait_ge(s.qa_ready, l + 1)
            for t in range(T):
                b = bank(f"cT{t}.{l}")
                for i in range(2):
                    TR(b[:, i * P:(i + 1) * P], qa[:, t, i:256:2], ident)
                done(TR(b[:, 256:384], qa[:, t, 256:384], ident))
            read_out(pe, f"cT1.{l}")
            for t in range(T):
                for u in range(2):
                    project(f"mq{t}{u}.{l}", cT, slot, 2, 384, t, 384 * u, 768)
            for t in range(T):
                for u in range(2):
                    done(M(bank(f"mk{t}{u}.{l}")[:], cT[:, 2, t * P:(t + 1) * P],
                           slot[:, 1536 + 512 * u:2048 + 512 * u], start=True, stop=True))
            pe.wait_ge(s.mla_key_ready, T * (l + 1))
            for q, src in enumerate((mq, mk)):
                for u in range(4):
                    b = bank(f"mT{q}{u}.{l}")
                    for i in range(2):
                        for t in range(T):
                            ins = TR(b[0:QK, 256 * i + 128 * t:256 * i + 128 * t + 128], src[:, t, 2 * u + i, :],
                                     ident)
                    done(ins)
            read_out(pe, f"mT13.{l}")
            for i in range(NH + 2):
                if i < NH:
                    b = bank(f"sM{i}.{l}")
                    M(b[:, 0:128], mqT[0:QK, i, 0:128], mkT[0:QK, i, 0:128], start=True, stop=True)
                    done(M(b[:, 128:384], mqT[0:QK, i, 128:256], mkT[0:QK, i, :], start=True, stop=True))
                if 0 < i <= NH:
                    pe.wait_ge(s.prob_ready, NH * l + i)
                    b = bank(f"pT{i - 1}.{l}")
                    for c in range(3):
                        ins = TR(b[:, c * P:(c + 1) * P], sm[:, (i - 1) % 2, c * P:(c + 1) * P], ident)
                    done(ins)
                if i > 1:
                    k = i - 2
                    read_out(pe, f"pT{k}.{l}")
                    b = bank(f"oM{k}.{l}")
                    M(b[:, 0:64], pT[:, k % 2, 0:128], mv[:, 0, k, :], start=True, stop=True)
                    M(b[:, 64:128], pT[:, k % 2, 128:256], mv[:, 0, k, :], start=True, stop=False)
                    done(M(b[:, 64:128], pT[:, k % 2, 256:384], mv[:, 1, k, :], start=False, stop=True))
            pe.wait_ge(s.scan_in_ready, l + 1)
            scan_in = ((kk, 0), (pr, 0), (ab, 0), (pr, 512))
            for t in range(T):
                for hp in range(4):
                    b = bank(f"kT{t}{hp}.{l}")
                    for i, (src, c0) in enumerate(scan_in):
                        ins = TR(b[:, i * P:(i + 1) * P], src[:, t, c0 + hp * P:c0 + (hp + 1) * P], ident)
                    done(ins)
                for i in range(NH):
                    e, hp = i // 4, i % 4
                    half = slice(64 * e, 64 * e + 64)
                    if e == 0:
                        read_out(pe, f"kT{t}{hp}.{l}")
                    b = bank(f"M{t}{i}.{l}")
                    M(b[:, 0:256], tT[half, hp, 256:384], tT[half, hp, 0:256], start=True, stop=True)
                    done(M(b[:, 256:512], tT[half, hp, 384:512], tT[half, hp, 0:256], start=True, stop=True))
                for g in range(2):
                    b = bank(f"A{t}{g}.{l}")
                    half = slice(64 * g, 64 * g + 64)
                    for hp in range(4):
                        ins = M(b[:, hp * P:(hp + 1) * P], tT[half, hp, 0:128], tT[half, hp, 256:384], start=True,
                                stop=True)
                    done(ins)
                for lv in range(1, LEVELS):
                    for g in range(2):
                        pe.wait_ge(s.x_ready, 2 * (T * l + t) + g + 1) if lv == 1 else \
                            read_out(pe, f"XT{t}{lv - 1}{g}.{l}")
                        b = bank(f"T{t}{lv}{g}.{l}")
                        for i in range(4):
                            ins = M(b[:, i * P:(i + 1) * P], m1[:, 4 * g + i, 0:128], xi[:, 4 * g + i, :],
                                    start=True, stop=True)
                        done(ins)
                    for g in range(2):
                        read_out(pe, f"T{t}{lv}{g}.{l}")
                        if lv < LEVELS - 1:
                            b = bank(f"X{t}{lv}{g}.{l}")
                            for i in range(4):
                                ins = M(b[:, i * P:(i + 1) * P], xt[:, 4 * g + i, :], t1[:, 4 * g + i, :],
                                        start=True, stop=True)
                            done(ins)
                        b = bank(f"XT{t}{lv}{g}.{l}")
                        for i in range(4):
                            ins = M(b[:, i * P:(i + 1) * P], t1[:, 4 * g + i, :], xt[:, 4 * g + i, :],
                                    start=True, stop=True)
                        done(ins)
                read_out(pe, f"XT{t}{LEVELS - 1}1.{l}")
                vcol = pr[:, t, 1024:1536]
                b = bank(f"W{t}.{l}")
                for hp in range(4):
                    for e in range(2):
                        ins = M(b[64 * e:64 * e + 64, hp * P:(hp + 1) * P],
                                kk[:, t, (2 * hp + e) * 64:(2 * hp + e) * 64 + 64], xt[:, 4 * e + hp, :],
                                start=True, stop=True)
                done(ins)
                b = bank(f"Z{t}.{l}")
                for i in range(NH):
                    hh = slice(64 * i, 64 * i + 64)
                    ins = M(b[:, hh], m1[:, 4 * (i % 2) + i // 2, 256:384], vcol[:, hh], start=True, stop=True)
                done(ins)
                read_out(pe, f"Z{t}.{l}")
                b = bank(f"U{t}.{l}")
                for i in range(NH):
                    hh = slice(64 * i, 64 * i + 64)
                    ins = M(b[:, hh], xt[:, 4 * (i % 2) + i // 2, :], zz[:, hh], start=True, stop=True)
                done(ins)
                read_out(pe, f"U{t}.{l}")
                for n in (2 * t, 2 * t + 1):
                    o = slice(64 * (n % 2), 64 * (n % 2) + 64)
                    if n:
                        pe.wait_ge(s.state_ready, 3 * l + n)
                        for e in range(2):
                            b = bank(f"dU{n}{e}.{l}")
                            half = slice(64 * e, 64 * e + 64)
                            for hp in range(4):
                                ins = M(b[o, 64 * hp:64 * hp + 64], nw[half, hp, o], st[half, n - 1, hp, :],
                                        start=True, stop=True)
                            done(ins)
                        read_out(pe, f"dU{n}1.{l}")
                    if n < 3:
                        b = bank(f"S{n + 1}.{l}")
                        for hp in range(4):
                            for e in range(2):
                                hh = slice((2 * hp + e) * 64, (2 * hp + e) * 64 + 64)
                                dst = b[64 * e:64 * e + 64, 64 * hp:64 * hp + 64]
                                M(dst, ab[o, t, hh], uu[o, t, hh], start=True, stop=False)
                                ins = M(dst, pr[o, t, 512 + hh.start:512 + hh.stop],
                                        pr[o, t, 1024 + hh.start:1024 + hh.stop], start=False, stop=True)
                        done(ins)
                for e in range(2):
                    b = bank(f"Y{t}{e}.{l}")
                    half = slice(64 * e, 64 * e + 64)
                    for hp in range(4):
                        hh = slice((2 * hp + e) * 64, (2 * hp + e) * 64 + 64)
                        dst = slice(64 * hp, 64 * hp + 64)
                        M(b[:, dst], m1[:, 4 * e + hp, 384:512], vcol[:, hh], start=True, stop=False)
                        for n in (2 * t, 2 * t + 1):
                            if n:
                                o = 64 * (n % 2)
                                M(b[o:o + 64, dst], tT[half, hp, 128 + o:192 + o], st[half, n - 1, hp, :],
                                  start=False, stop=False)
                        ins = M(b[:, dst], m1[:, 4 * e + hp, 128:256], uu[:, t, hh], start=False, stop=True)
                    done(ins)
            for n in range(3):
                y = (y_ret, y_rwkv, y_mla)[n]
                if n == 2:
                    read_out(pe, f"oM{NH - 1}.{l}")
                else:
                    pe.wait_ge((s.ret_done, s.rwkv_done)[n], l + 1)
                for u in range(2):
                    b = bank(f"yT{n}{u}.{l}")
                    for i in range(2):
                        for t in range(T):
                            ins = TR(b[:, 256 * i + 128 * t:256 * i + 128 * t + 128], y[:, t, 2 * u + i:W:4], ident)
                    done(ins)
                for u in range(2):
                    slot = panel("gate")
                    for t in range(T):
                        project(f"gt{n}{u}{t}.{l}", hnT, slot, KD, 512, t)
                slot = panel("branch")
                read_out(pe, f"yT{n}1.{l}")
                for u in range(2):
                    for t in range(T):
                        project(f"br{n}{u}{t}.{l}", yT[:, n % 2], slot, 4, 512, t, 512 * u, D)
            pe.wait_ge(s.merged_done, T * 2 * (l + 1))
            transpose_in("gT{}." + str(l), merged)
            read_out(pe, f"gT3.{l}")
            for u in range(2):
                slot = panel("o")
                for t in range(T):
                    project(f"o{u}{t}.{l}", gT, slot, KD, 512, t)
            pe.wait_ge(s.hn_ready, 2 * T * l + 2 * T)
            transpose_in("fT{}." + str(l), hn)
            read_out(pe, f"fT3.{l}")
            if l == 0:
                for j in range(7):
                    if j < 6:
                        for n, jobs in (("ffn_gate", "fg"), ("ffn_up", "fu")):
                            slot = panel(n)
                            for t in range(T):
                                project(f"{jobs}{j}{t}.0", hnT, slot, KD, FFN_COLS[j], t)
                    if j:
                        k = FFN_COLS[j - 1] // P
                        for t in range(T):
                            read_out(pe, f"fu{j - 1}{t}.0")
                            b = bank(f"hT{j - 1}{t}.0")
                            for c in range(k):
                                ins = TR(b[:, c * P:(c + 1) * P], hm[:, (j - 1) % 2, t, c:k * P:k], ident)
                            done(ins)
                outs = [(u, t, bank(f"fd{u}{t}.0")) for u in range(2) for t in range(T)]
                for j in range(6):
                    slot = panel("ffn_down")
                    read_out(pe, f"hT{j}1.0")
                    k = FFN_COLS[j] // P
                    w = slot[:, 0:k * D].rearrange("p (c n) -> p c n", c=k)
                    for u, t, b in outs:
                        for c in range(k):
                            ins = M(b[:], hmT[:, 4 * j + c, t * P:(t + 1) * P], w[:, c, 512 * u:512 * u + 512],
                                    start=j == 0 and c == 0, stop=j == 5 and c == k - 1, skip_group_check=True)
                        if j == 5:
                            done(ins)
                    if j < 5:
                        ins.then_inc(s.down_used, 1)
        pe.wait_ge(s.router_loaded, 16)
        b = bank("router.1")
        for t in range(T):
            for c in range(KD):
                ins = M(b[:, NE * t:NE * t + NE], hnT[:, c, t * P:(t + 1) * P], router[:, c, :], start=c == 0,
                        stop=c == KD - 1)
        done(ins)
        pe.wait_ge(s.mask_ready, 1)
        b = bank("rank.1")
        m0, m1_ = rt[:, 8, 0, :], rt[:, 8, 1, :]
        M(b[:, 0:NE], C("upto"), m0, start=True, stop=True)
        M(b[:, NE:2 * NE], C("ones"), m0, start=True, stop=False)
        M(b[:, NE:2 * NE], C("upto"), m1_, start=False, stop=True)
        M(b[:, 2 * NE:3 * NE], C("ones"), m0, start=True, stop=False)
        done(M(b[:, 2 * NE:3 * NE], C("ones"), m1_, start=False, stop=True))
        pe.wait_ge(s.freed_act, FR["act"])
        pe.wait_ge(s.freed_vec, FR["vec"])
        pe.wait_ge(s.items_ready, 1)
        n_items = pe.value_load(items[0:1, 24:25], min_val=SURE, max_val=SURE + 3)
        with pe.Fori(0, n_items) as item:
            def item_read_out(job):
                k = ITEM_AT[job]
                e = ITEM[k][1]
                pe.wait_ge(freed[e], item * IF[e] + (FR[e] + item_freed(k, e)))

            def item_bank(job):
                k = ITEM_AT[job]
                if k >= BANKS:
                    item_read_out(ITEM[k - BANKS][0])
                else:
                    p = max(m for m in range(len(ITEM)) if m % BANKS == k)
                    e = ITEM[p][1]
                    pe.wait_ge(freed[e], item * IF[e] + (FR[e] - IF[e] + item_freed(p, e)))
                return banks[k % BANKS]

            def item_panel(m):
                i = (NPAN + m) % RING
                before = 16 * sum(PANELS[n][3] for n in range(NPAN) if n % RING == i)
                nth = sum((NPAN + q) % RING == i for q in range(m + 1))
                pe.wait_ge(slot_loaded[i], item * (16 * EP // RING) + (before + 16 * nth))
                return ring[:, i, :]

            pe.wait_ge(s.sel_ready, item + 1)
            b = item_bank("csT")
            for t in range(T):
                ins = TR(b[:, t * P:(t + 1) * P], csel[:, t, :], ident)
            done(ins)
            for u in range(2):
                b = item_bank(f"gx{u}")
                for i in range(4):
                    for t in range(T):
                        ins = M(b[:, i * P:(i + 1) * P], hn[:, t, 4 * u + i:D:KD], sel[:, t, :], start=t == 0,
                                stop=t == T - 1)
                done(ins)
            item_read_out("gx1")
            for j in range(8):
                if j < 7:
                    for q, name in enumerate(("eg", "eu")):
                        w = item_panel(2 * j + q).rearrange("p (c n) -> p c n", c=KD)
                        b = item_bank(f"{name}{j}")
                        for c in range(KD):
                            ins = M(b[:], xg[:, c, :], w[:, c, :], start=c == 0, stop=c == KD - 1)
                        done(ins)
                if j:
                    item_read_out(f"eu{j - 1}")
                    b = item_bank(f"eT{j - 1}")
                    for c in range(4):
                        ins = TR(b[:, c * P:(c + 1) * P], ehm[:, (j - 1) % 2, c:512:4], ident)
                    done(ins)
            b0, b1 = item_bank("ed0"), item_bank("ed1")
            for j in range(7):
                w = item_panel(14 + j).rearrange("p (c n) -> p c n", c=4)
                item_read_out(f"eT{j}")
                for u, b in enumerate((b0, b1)):
                    for c in range(4):
                        ins = M(b[:], ehT[:, 4 * j + c, :], w[:, c, 512 * u:512 * u + 512],
                                start=j == 0 and c == 0, stop=j == 6 and c == 3, skip_group_check=True)
                    if j == 6:
                        done(ins)
                if j < 6:
                    ins.then_inc(s.down_used, 1)
            item_read_out("csT")
            for u in range(2):
                item_read_out(f"ed{u}")
                for t in range(T):
                    done(M(item_bank(f"sc{u}{t}")[:], cselT[:, t * P:(t + 1) * P], ey[:, 512 * u:512 * u + 512],
                           start=True, stop=True))

    @block.vector
    def _(dve):
        own = Own(dve, "vec", s.vec_step, s.freed_vec)
        V = nc.vector
        step, settle, free = own.step, own.settle, own.free

        def tt(out_, a, b, op):
            return V.tensor_tensor(out_, a, b, op)

        def normalise(m, dst):
            dve.wait_ge(s.sumsq_ready, T * (m + 1))
            step(V.tensor_scalar(stat[:, 0, 0:T], stat[:, 0, 0:T], 1.0 / D, EPS, ALU.mult, ALU.add), s.var_ready)
            dve.wait_ge(s.root_ready, m + 1)
            step(V.reciprocal(stat[:, 0, 0:T], stat[:, 0, 0:T]))
            settle()
            for t in range(T):
                step(V.tensor_scalar(dst[:, t, :], h[:, t, :], stat[:, 0, t:t + 1], None, ALU.mult), s.hn_ready)

        def group_stats(y, groups, width, eps, m):
            mean, var = stat[:, 3, 0:groups], stat[:, 4, 0:groups]
            v = y.rearrange("p t (g e) -> p (t g) e", e=width)
            sq = tmp[:].rearrange("p t (g e) -> p (t g) e", e=width)
            step(V.reduce_sum(mean, v, AX.X))
            settle()
            step(V.tensor_scalar(mean, mean, 1.0 / width, None, ALU.mult))
            settle()
            step(tt(v, v, wide(mean, width), ALU.subtract))
            settle()
            step(tt(sq, v, v, ALU.mult))
            settle()
            step(V.reduce_sum(var, sq, AX.X))
            settle()
            step(V.tensor_scalar(var, var, 1.0 / width, eps, ALU.mult, ALU.add), s.gn_var_ready)
            dve.wait_ge(s.gn_root_ready, m + 1)
            step(V.reciprocal(var, var))
            settle()
            step(tt(v, v, wide(var, width), ALU.mult))
            settle()

        dve.wait_ge(s.const_loaded, 16)
        dve.wait_ge(s.pos_loaded, 16 * T)
        step(V.tensor_copy(pos_f[:], pos_i[:]))
        settle()
        for t in range(T):
            step(V.tensor_scalar(sinT[:, t, :], C("inv_freq"), pos_f[:, t:t + 1], None, ALU.mult))
        settle()
        step(V.tensor_scalar(cosT[:], sinT[:], 1.0 / (2 * np.pi), ROUND, ALU.mult, ALU.add))
        settle()
        step(V.tensor_scalar(cosT[:], cosT[:], -ROUND, None, ALU.add))
        settle()
        for part in TWO_PI:
            step(V.scalar_tensor_tensor(out=sinT[:], in0=cosT[:], scalar=-part, in1=sinT[:], op0=ALU.mult,
                                        op1=ALU.add))
            settle()
        half_pi, pi = float(np.float32(np.pi / 2)), 3.1415925
        turn = gg[:, :, 0:80]
        step(V.tensor_scalar(turn, sinT[:], half_pi, -2 * np.pi, ALU.is_gt, ALU.mult))
        settle()
        step(V.scalar_tensor_tensor(out=cosT[:], in0=sinT[:], scalar=half_pi, in1=turn, op0=ALU.add, op1=ALU.add))
        settle()
        step(V.tensor_scalar(cosT[:], cosT[:], -pi, pi, ALU.max, ALU.min))
        step(V.tensor_scalar(sinT[:], sinT[:], -pi, pi, ALU.max, ALU.min), s.angles_ready)

        for l in range(DEPTH):
            normalise(2 * l, hn)
            dve.wait_ge(s.vec_loaded, 16 * 7 * (l + 1))
            dve.wait_ge(s.shift_loaded, 32 * (l + 1))
            for a, b_ in ((1536, RWCOLS), (0, 1536)):
                step(tt(prev[:, :, a:b_], prev[:, :, a:b_], pr[:, :, a:b_], ALU.subtract))
                settle()
                step(tt(prev[:, :, a:b_], prev[:, :, a:b_], each(VEC("mu", a, b_)), ALU.mult))
                settle()
                step(tt(pr[:, :, a:b_], pr[:, :, a:b_], prev[:, :, a:b_], ALU.add),
                     s.xs_ready if a else None)
            settle()
            r, k, v = (pr[:, :, 512 * i:512 * i + 512] for i in range(3))
            step(tt(kk[:], k, each(VEC("k_k")), ALU.mult))
            settle()
            step(tt(tmp[:], kk[:], kk[:], ALU.mult))
            settle()
            step(V.reduce_sum(stat[:, 1, :], tmp[:].rearrange("p t (g e) -> p (t g) e", e=HD), AX.X))
            settle()
            step(V.tensor_scalar(stat[:, 1, :], stat[:, 1, :], 1e-12, None, ALU.add))
            dve.wait_ge(s.qa_sumsq, 4 * (l + 1))
            lat = stat[:, 2, 0:4].rearrange("p (t q) -> p t q", t=T)
            step(V.tensor_scalar(lat[:, :, 0], lat[:, :, 0], 1.0 / 256, EPS, ALU.mult, ALU.add))
            step(V.tensor_scalar(lat[:, :, 1], lat[:, :, 1], 1.0 / 128, EPS, ALU.mult, ALU.add), s.knsq_ready)
            for t in range(T):
                b = product(dve, f"z{t}.{l}")
                free(tt(ld[:, t, :], b[:], VEC("w0"), ALU.add), f"z{t}.{l}")
                b = product(dve, f"a{t}.{l}")
                free(tt(ab[:, t, :], b[:], VEC("a0"), ALU.add), f"a{t}.{l}")
            dve.wait_ge(s.knroot_ready, l + 1)
            step(V.reciprocal(stat[:, 1, :], stat[:, 1, :]))
            step(V.reciprocal(stat[:, 2, 0:4], stat[:, 2, 0:4]))
            settle()
            kg = kk[:].rearrange("p t (g e) -> p (t g) e", e=HD)
            step(tt(kg, kg, wide(stat[:, 1, :], HD), ALU.mult))
            for t in range(T):
                step(V.tensor_scalar(qa[:, t, 0:256], qa[:, t, 0:256], stat[:, 2, 2 * t:2 * t + 1], None, ALU.mult))
                step(V.tensor_scalar(qa[:, t, 256:384], qa[:, t, 256:384], stat[:, 2, 2 * t + 1:2 * t + 2], None,
                                     ALU.mult), s.qa_ready if t else None)
            settle()
            dve.wait_ge(s.decay_sig_ready, l + 1)
            step(V.tensor_scalar(ld[:], ld[:], -DECAY, None, ALU.mult), s.logd_ready)
            dve.wait_ge(s.rate_sig_ready, l + 1)
            step(V.scalar_tensor_tensor(out=tmp[:], in0=ab[:], scalar=-1.0, in1=each(VEC("k_a")), op0=ALU.add,
                                        op1=ALU.mult))
            step(tt(ab[:], ab[:], kk[:], ALU.mult))
            settle()
            step(V.scalar_tensor_tensor(out=k, in0=tmp[:], scalar=1.0, in1=k, op0=ALU.add, op1=ALU.mult))
            settle()
            step(tt(tmp[:], r, k, ALU.mult))
            settle()
            step(tt(tmp[:], tmp[:], each(VEC("r_k")), ALU.mult))
            settle()
            step(V.reduce_sum(stat[:, 5, :], tmp[:].rearrange("p t (g e) -> p (t g) e", e=HD), AX.X))
            for i in range(RH):
                b = product(dve, f"sR{i}.{l}")
                step(tt(sR[:, i, 0:256], b[:, 0:256], C("ret_mask", 256 * i, 256 * i + 256), ALU.mult))
                free(tt(sR[:, i, 256:384], b[:, 256:384], C("ret_mask", 256 * i, 256 * i + 128), ALU.mult),
                     f"sR{i}.{l}")
            dve.wait_ge(s.product_ready, JOB_AT[f"pc.{l}"] + 1)
            for t in range(T):
                b = banks[JOB_AT[f"cum{t}.{l}"] % BANKS]
                dve.wait_ge(s.exps_ready, T * l + t + 1)
                step(tt(ld[:, t, :], b[:], ld[:, t, :], ALU.subtract), s.cex_ready)
            read_out(dve, f"cum1.{l}")
            step(tt(kk[:], kk[:], ld[:], ALU.mult))
            step(tt(r, r, ec[:], ALU.mult))
            step(tt(ab[:], ab[:], enc[:], ALU.mult))
            step(tt(k, k, enc[:], ALU.mult), s.scan_in_ready)
            read_out(dve, f"oR1.{l}")
            group_stats(y_ret[:], 8, P, 1e-5, 2 * l)
            dve.wait_ge(s.silu_g_ready, l + 1)
            step(tt(y_ret[:], y_ret[:], raw[:, :, 3, :], ALU.mult), s.ret_done)
            for i in range(NH + 2):
                if i < NH:
                    b = product(dve, f"sM{i}.{l}")
                    if i > 1:
                        dve.wait_ge(s.product_ready, JOB_AT[f"pT{i - 2}.{l}"] + 1)
                    sc = float(QK) ** -0.5
                    m = sm[:, i % 2, :]
                    step(V.scalar_tensor_tensor(out=m[:, 0:128], in0=b[:, 0:128], scalar=sc, in1=C("mla_mask"),
                                                op0=ALU.mult, op1=ALU.add))
                    step(V.tensor_scalar(m[:, 128:256], b[:, 128:256], sc, None, ALU.mult))
                    free(V.scalar_tensor_tensor(out=m[:, 256:384], in0=b[:, 256:384], scalar=sc, in1=C("mla_mask"),
                                                op0=ALU.mult, op1=ALU.add), f"sM{i}.{l}")
                    settle()
                    step(V.reduce_max(smax[:, i, 0:1], m[:, 0:128], AX.X))
                    step(V.reduce_max(smax[:, i, 1:2], m[:, 128:384], AX.X))
                    settle()
                    step(V.tensor_scalar(smax[:, i, :], smax[:, i, :], -1.0, None, ALU.mult), s.masked_ready)
                if i > 1:
                    j = i - 2
                    dve.wait_ge(s.prob_ready, NH * l + j + 1)
                    step(V.reciprocal(den[:, j, :], den[:, j, :]))
                    b = product(dve, f"oM{j}.{l}")
                    settle()
                    free(tt(y_mla[:, :, 64 * j:64 * j + 64], b[:, 0:128].rearrange("p (t e) -> p t e", t=T),
                            wide(den[:, j, :], HD), ALU.mult), f"oM{j}.{l}")
            for t in range(T):
                for i in range(NH):
                    b = product(dve, f"M{t}{i}.{l}")
                    free(tt(m1[:, i, :], b[:], C("pair_mask"), ALU.mult), f"M{t}{i}.{l}")
                for g in range(2):
                    four = slice(4 * g, 4 * g + 4)
                    b = product(dve, f"A{t}{g}.{l}")
                    quad = b[:].rearrange("p (i n) -> p i n", i=4)
                    free(tt(am[:, four, :], quad, each(C("a_mask"), 4), ALU.mult), f"A{t}{g}.{l}")
                    settle()
                    step(tt(xt[:, four, :], m1[:, four, 0:128], each(C("level0_t"), 4), ALU.mult))
                    settle()
                    step(tt(xi[:, four, :], am[:, four, :], each(C("levels", 0, P), 4), ALU.mult))
                    step(tt(xt[:, four, :], xt[:, four, :], each(C("ident"), 4), ALU.add))
                    settle()
                    step(tt(xi[:, four, :], xi[:, four, :], each(C("ident"), 4), ALU.add), s.x_ready)
                for lv in range(1, LEVELS):
                    for g in range(2):
                        four = slice(4 * g, 4 * g + 4)
                        b = product(dve, f"T{t}{lv}{g}.{l}")
                        free(tt(t1[:, four, :], b[:].rearrange("p (i n) -> p i n", i=4),
                                each(C("levels", lv * P, lv * P + P), 4), ALU.mult), f"T{t}{lv}{g}.{l}")
                    for g in range(2):
                        four = slice(4 * g, 4 * g + 4)
                        for x_, name in ((xi, "X"), (xt, "XT")):
                            if name == "X" and lv == LEVELS - 1:
                                continue
                            b = product(dve, f"{name}{t}{lv}{g}.{l}")
                            free(tt(x_[:, four, :], b[:].rearrange("p (i n) -> p i n", i=4), x_[:, four, :],
                                    ALU.add), f"{name}{t}{lv}{g}.{l}")
                for n in (2 * t, 2 * t + 1):
                    o = slice(64 * (n % 2), 64 * (n % 2) + 64)
                    if n == 2 * t:
                        read_out(dve, f"U{t}.{l}")
                    if n:
                        for e in range(2):
                            b = product(dve, f"dU{n}{e}.{l}")
                            u_ = uu[o, t, :].rearrange("p (a b d) -> p a b d", a=4, b=2)[:, :, e, :]
                            free(tt(u_, b[o, 0:256].rearrange("p (a d) -> p a d", a=4), u_, ALU.add),
                                 f"dU{n}{e}.{l}")
                    if n < 3:
                        b = product(dve, f"S{n + 1}.{l}")
                        sn = b[:, 0:256].rearrange("p (a d) -> p a d", a=4)
                        dec = wide(decay_end[:, t, :, n % 2], HD)
                        if n == 0:
                            free(V.tensor_copy(st[:, 0, :, :], sn), f"S{n + 1}.{l}")
                        else:
                            free(tt(st[:, n, :, :], sn, st[:, n - 1, :, :], ALU.add), f"S{n + 1}.{l}")
                        settle()
                        step(tt(st[:, n, :, :], st[:, n, :, :], dec, ALU.mult), s.state_ready)
            read_out(dve, f"Y11.{l}")
            group_stats(y_rwkv[:], 16, HD, 64e-5, 2 * l + 1)
            step(tt(y_rwkv[:], y_rwkv[:], each(VEC("lnx")), ALU.mult))
            step(tt(tmp[:].rearrange("p t (g e) -> p t g e", e=HD), v.rearrange("p t (g e) -> p t g e", e=HD),
                    wide(stat[:, 5, :].rearrange("p (t g) -> p t g", t=T), HD), ALU.mult))
            settle()
            step(tt(y_rwkv[:], y_rwkv[:], tmp[:], ALU.add))
            settle()
            step(tt(y_rwkv[:], y_rwkv[:], gg[:], ALU.mult), s.rwkv_done)
            for n in range(3):
                for u in range(2):
                    for t in range(T):
                        b = product(dve, f"br{n}{u}{t}.{l}")
                        read_out(dve, f"gt{n}{u}{t}.{l}")
                        m = merged[:, t, 512 * u:512 * u + 512]
                        gate = sig[:, n % 2, u, t, :]
                        if n == 0:
                            free(tt(m, b[:], gate, ALU.mult), f"br{n}{u}{t}.{l}")
                        else:
                            free(tt(gate, b[:], gate, ALU.mult), f"br{n}{u}{t}.{l}")
                            settle()
                            step(tt(m, m, gate, ALU.add), s.merged_done if n == 2 else None)
            for u in range(2):
                for t in range(T):
                    b = product(dve, f"o{u}{t}.{l}")
                    hs = h[:, t, 512 * u:512 * u + 512]
                    free(tt(hs, b[:], hs, ALU.add), f"o{u}{t}.{l}")
            normalise(2 * l + 1, hn)
            if l == 0:
                for j in range(6):
                    w_ = FFN_COLS[j]
                    for t in range(T):
                        b = product(dve, f"fu{j}{t}.0")
                        read_out(dve, f"fg{j}{t}.0")
                        free(tt(hm[:, j % 2, t, 0:w_], b[:, 0:w_], sg[:, j % 2, t, 0:w_], ALU.mult),
                             f"fu{j}{t}.0")
                for u in range(2):
                    for t in range(T):
                        b = product(dve, f"fd{u}{t}.0")
                        hs = h[:, t, 512 * u:512 * u + 512]
                        free(tt(hs, b[:], hs, ALU.add), f"fd{u}{t}.0")
        R = lambda i: rt[:, i, :, :]
        few = each(C("experts"), T)
        b = product(dve, "router.1")
        free(V.tensor_copy(R(0), b[:, 0:T * NE].rearrange("p (t e) -> p t e", t=T)), "router.1")
        step(V.tensor_scalar(R(1), few, -99.0, None, ALU.add))
        settle()
        top = stat[:, 7, :].rearrange("p (a t) -> p a t", t=T)
        for i in range(2):
            step(V.reduce_max(top[:, i, :], R(0), AX.X))
            settle()
            step(tt(R(4), R(0), wide(top[:, i, :], NE), ALU.is_equal))
            settle()
            step(tt(R(4), R(4), R(1), ALU.mult))
            settle()
            step(V.tensor_reduce(top[:, 2, :], R(4), AX.X, ALU.min))
            settle()
            step(tt(R(2 + i), R(1), wide(top[:, 2, :], NE), ALU.is_equal))
            settle()
            if i == 0:
                step(V.scalar_tensor_tensor(out=R(0), in0=R(2), scalar=-3e38, in1=R(0), op0=ALU.mult, op1=ALU.add))
                settle()
        step(tt(stat[:, 6, 0:2], top[:, 1, :], top[:, 0, :], ALU.subtract), s.route_diff)
        step(tt(R(8), R(2), R(3), ALU.add), s.mask_ready)
        dve.wait_ge(s.route_exp, 1)
        step(V.tensor_scalar(stat[:, 6, 2:4], stat[:, 6, 0:2], 1.0, None, ALU.add))
        settle()
        step(V.reciprocal(stat[:, 6, 2:4], stat[:, 6, 2:4]))
        settle()
        step(tt(stat[:, 6, 0:2], stat[:, 6, 0:2], stat[:, 6, 2:4], ALU.mult))
        settle()
        step(tt(R(2), R(2), wide(stat[:, 6, 2:4], NE), ALU.mult))
        step(tt(R(3), R(3), wide(stat[:, 6, 0:2], NE), ALU.mult))
        settle()
        for i in range(2):
            step(tt(comb[:, i, :, :], R(2), R(3), ALU.add))
        b = product(dve, "rank.1")
        step(tt(R(5), b[:, 0:T * NE].rearrange("p (t e) -> p t e", t=T), R(8), ALU.mult))
        settle()
        for i in range(2):
            step(V.tensor_scalar(spos[:, i, :, :], R(5), -1.0 - P * i, None, ALU.add))
        f = it_f[0:1, :]
        free(V.tensor_scalar(f[:, 0:8], b[0:1, 16:24], P + 0.5, None, ALU.is_gt), "rank.1")
        step(V.tensor_scalar(f[:, 8:16], C("experts")[0:1, :], -1.0, 8.0, ALU.mult, ALU.add))
        settle()
        step(tt(f[:, 8:16], f[:, 8:16], f[:, 0:8], ALU.mult))
        step(V.reduce_sum(f[:, 56:57], f[:, 0:8], AX.X))
        settle()
        step(V.max(f[:, 16:24], f[:, 8:16]))
        settle()
        step(V.tensor_scalar(f[:, 40:44], f[:, 16:20], -1.0, 24.0, ALU.mult, ALU.add))
        step(V.tensor_copy(f[:, 32:40], C("experts")[0:1, :]))
        step(V.tensor_copy(f[:, 44:52], C("experts")[0:1, :]))
        step(V.tensor_scalar(f[:, 52:56], f[:, 16:20], -1.0, 8.0, ALU.mult, ALU.add))
        step(V.tensor_scalar(f[:, 56:57], f[:, 56:57], float(NE), None, ALU.add))
        settle()
        step(V.tensor_scalar(f[:, 52:56], f[:, 52:56], float(NE - 1), None, ALU.min))
        step(V.tensor_scalar(f[:, 40:44], f[:, 40:44], float(2 * NE * T // 2 + NE - 1), None, ALU.min))
        settle()
        step(V.tensor_copy(items[0:1, 0:25], f[:, 32:57]), s.items_ready)
        settle()
        n_items = dve.value_load(items[0:1, 24:25], min_val=SURE, max_val=SURE + 3)
        with dve.Fori(0, n_items) as item:
            at_ = dve.value_load(items[0:1, bass.ds(item, 1)], min_val=0, max_val=NE * T + NE - 1)

            def item_product(job):
                dve.wait_ge(s.product_ready, item * len(ITEM) + (len(JOBS) + ITEM_AT[job] + 1))
                return banks[ITEM_AT[job] % BANKS]

            for t in range(T):
                sp_ = spos[:].rearrange("p i t e -> p (i t e)")[:, bass.ds(at_ + NE * t, 1)]
                cb_ = comb[:].rearrange("p i t e -> p (i t e)")[:, bass.ds(at_ + NE * t, 1)]
                V.tensor_scalar(sel[:, t, :], C("slots"), sp_, None, ALU.is_equal)
                ins = V.tensor_scalar(csel[:, t, :], C("slots"), sp_, cb_, ALU.is_equal, ALU.mult)
            ins.then_inc(s.sel_ready, 1)
            for j in range(7):
                b = item_product(f"eu{j}")
                k = ITEM_AT[f"eg{j}"]
                dve.wait_ge(s.freed_act, item * IF["act"] + (FR["act"] + item_freed(k, "act")))
                tt(ehm[:, j % 2, :], b[:], esg[:, j % 2, :], ALU.mult).then_inc(s.freed_vec, 1)
            for u in range(2):
                V.tensor_copy(ey[:, 512 * u:512 * u + 512], item_product(f"ed{u}")[:]).then_inc(s.freed_vec, 1)
            for u in range(2):
                for t in range(T):
                    hs = h[:, t, 512 * u:512 * u + 512]
                    tt(hs, item_product(f"sc{u}{t}")[:], hs, ALU.add).then_inc(s.freed_vec, 1)
            V.tensor_copy(smax[:, 0, :], smax[:, 0, :]).then_inc(s.item_step, 1)
            dve.wait_ge(s.item_step, item + 1)
        V.tensor_copy(smax[:, 0, :], smax[:, 0, :]).then_inc(s.items_done, 1)
        normalise(4, fin)
        dve.wait_ge(s.fgain_loaded, 16)
        for t in range(T):
            settle()
            own.step(tt(fin[:, t, :], fin[:, t, :], fgain[:], ALU.mult), s.fin_ready)

    blk.__exit__(None, None, None)


_INS = ["x", "positions", "attn_norm", "w_in", "rwkv_mu", "rwkv_w0", "rwkv_w2", "rwkv_a0", "rwkv_a2", "rwkv_g2",
        "rwkv_k_k", "rwkv_k_a", "rwkv_r_k", "rwkv_lnx_w", "mla_q_norm", "mla_w_qb", "mla_kv_norm", "mla_w_kvb",
        "w_branch", "w_o", "ffn_norm", "ffn_w_gate", "ffn_w_up", "ffn_w_down", "moe_router", "moe_w_gate",
        "moe_w_up", "moe_w_down", "final_norm"]


def kernel(**inputs):
    import concourse.bacc as bacc
    from concourse.bass_utils import run_bass_kernel_spmd

    nc = bacc.Bacc("TRN2", target_bir_lowering=False, num_devices=1)
    arrays, args = {}, []
    for name in _INS:
        a = np.ascontiguousarray(inputs[name])
        arrays[f"{name}_dram"] = a
        args.append(nc.dram_tensor(f"{name}_dram", a.shape, mybir.dt.from_np(a.dtype), kind="ExternalInput").ap())
    arrays["const_dram"] = CONST
    args.append(nc.dram_tensor("const_dram", CONST.shape, F32, kind="ExternalInput").ap())
    args.append(nc.dram_tensor("out_dram", (1, SEQ, D), F32, kind="ExternalOutput").ap())
    build(nc, *args)
    r = run_bass_kernel_spmd(nc, [arrays], core_ids=[0])
    return r.results[0]["out_dram"]
```

```python
import numpy as np
import concourse.bass as bass
from concourse import mybir

F32 = mybir.dt.float32
I32 = mybir.dt.int32
ALU = mybir.AluOpType
ACT = mybir.ActivationFunctionType
AX = mybir.AxisListType

P = 128
SEQ, D, DEPTH, CHUNK = 256, 1024, 2, 64
T = SEQ // P
KD = D // P
RH, RW = 4, 512
NH, HD, W = 8, 64, 512
LORA = 288
RWCOLS = 3 * W + LORA
NOPE, ROPE, QK = 64, 32, 96
MLAC = 256 + 160
DFF, NE, FE = 2816, 8, 3584
DECAY = float(np.exp(-0.5))
EPS = 1e-6
RING = 3
BANKS = 8
SLOT = 4096
F32R = mybir.dt.float32r
HALF = SLOT // 2
PARTS = 3

C_RET, C_RWKV, C_MLA, C_GATE = 0, 2048, 2048 + RWCOLS, 2048 + RWCOLS + MLAC


def constants():
    i = np.arange(P)
    same = (i[:, None] // CHUNK) == (i[None, :] // CHUNK)
    s, t = i[:, None], i[None, :]
    c = {"ident": np.eye(P)}
    c["ones"] = np.ones((P, P))
    c["upto"] = (s <= t)
    c["chunk_upto"] = (s <= t) & same
    c["chunk_sel"] = np.stack([i < CHUNK, i >= CHUNK], 1)
    strict = (s < t) & same
    incl = (s <= t) & same
    c["pair_mask"] = np.concatenate([-1.0 * strict, incl, -1.0 * strict, incl], 1)
    c["a_mask"] = -1.0 * ((s > t) & same)
    b = 1
    lv = []
    while b < CHUNK:
        lv.append((s // (2 * b) == t // (2 * b)) & ((s // b) % 2 == 1) & ((t // b) % 2 == 0))
        b *= 2
    c["levels"] = np.concatenate([x.astype(np.float64) for x in lv], 1)
    c["level0_t"] = lv[0].T
    g = np.arange(SEQ)
    lg = np.log(1.0 - 2.0 ** (-5.0 - np.arange(RH)))
    ret = []
    for h in range(RH):
        m = np.exp(lg[h] * np.abs(g[None, :] - i[:, None])) * 128 ** -0.5
        ret.append(m * (i[:, None] // CHUNK <= g[None, :] // CHUNK))
    c["ret_mask"] = np.concatenate(ret, 1)
    c["mla_mask"] = np.where(i[None, :] // CHUNK <= i[:, None] // CHUNK, 0.0, -1e30)
    c["slots"] = np.tile(np.arange(P, dtype=np.float64), (P, 1))
    f32 = np.float32
    inv = [f32(1.0) / (f32(10000.0) ** (np.arange(0, d, 2, dtype=f32) / f32(d))) for d in (128, ROPE)]
    c["inv_freq"] = np.tile(np.concatenate(inv), (P, 1))
    c["experts"] = np.tile(np.arange(NE, dtype=np.float64), (P, 1))
    out, at = {}, 0
    for k, v in c.items():
        v = v.astype(np.float32)
        out[k] = (at, v.shape[1])
        at += v.shape[1]
    return out, np.ascontiguousarray(np.concatenate([v.astype(np.float32) for v in c.values()], 1))


CONST_AT, CONST = constants()
LEVELS = 6
VECTORS = ["mu", "w0", "a0", "k_k", "k_a", "r_k", "lnx"]
VEC_AT = {"mu": (0, RWCOLS)}
for _n, _v in enumerate(VECTORS[1:]):
    VEC_AT[_v] = (RWCOLS + _n * W, W)
VEC_COLS = RWCOLS + 6 * W

TWO_PI = [6.28125]
_left = 2 * np.pi - TWO_PI[0]
_c2 = float(np.round(_left * 2 ** 20) / 2 ** 20)
TWO_PI += [_c2, float(np.float32(_left - _c2))]
ROUND = 1.5 * 2 ** 23


BRANCHES = (0, 2, 1)


def panels():
    out = []
    for l in range(DEPTH):
        out += [("in", l, j, 1) for j in range(9)]
        out += [("lora", l, 0, 4), ("mla", l, 0, 2)]
        out += [("gate", l, j, 1) for j in range(6)]
        out += [("branch", l, n, 1) for n in BRANCHES]
        out += [("o", l, 0, 1), ("o", l, 1, 1)]
        if l == 0:
            for j in range(6):
                out += [("ffn_gate", 0, j, 1), ("ffn_up", 0, j, 1)]
            out += [("ffn_down", 0, j, 1) for j in range(6)]
    return out


IN_PANELS = [(C_RWKV + 1536, LORA), (C_RWKV, 512), (C_RWKV + 512, 512), (C_RWKV + 1024, 512),
             (0, 512), (512, 512), (1024, 512), (1536, 512), (C_MLA, MLAC)]
FFN_COLS = [512] * 5 + [256]


GATED = (2, 4)


def layer_jobs(l):
    A, V = "act", "vec"
    out = [(f"nT{q}", A) for q in range(4)]
    out += [(f"in{j}_{t}", A) for j in range(8) for t in range(T)]
    out += [(f"loT{t}", A) for t in range(T)] + [(f"in8_{t}", A) for t in range(T)]
    out += [(f"{n}{t}", e) for t in range(T) for n, e in (("z", V), ("a", V), ("g", A))]
    out += [(f"rT{s}{t}", A) for t in range(T) for s in range(2)]
    out += [(f"cT{t}", A) for t in range(T)]
    out += [(f"mq{t}{u}", A) for t in range(T) for u in range(2)]
    out += [(f"mk{t}{u}", A) for t in range(T) for u in range(2)]
    out += [(f"sR{h}", V) for h in range(RH)]
    out += [(f"cum{t}", A) for t in range(T)] + [("pc", A)]
    out += [(f"oR{t}", A) for t in range(T)]
    out += [("gt0", A)] + [(f"mT0{u}", A) for u in range(4)] + [("gt1", A)] + [(f"mT1{u}", A) for u in range(4)]
    for i in range(NH + 2):
        out += [(f"sM{i}", V)] * (i < NH) + [(f"pT{i - 1}", A)] * (0 < i <= NH) + [(f"oM{i - 2}", V)] * (i > 1)
        out += [(f"gt{2 + i // 2}", A)] * (i % 2 and i < NH)
    for t in range(T):
        out += [(f"kT{t}{hp}", A) for hp in range(4)]
        out += [(f"M{t}{i}", V) for i in range(NH)] + [(f"A{t}{g}", V) for g in range(2)]
        for lv in range(1, LEVELS):
            out += [(f"T{t}{lv}{g}", V) for g in range(2)]
            for g in range(2):
                out += [(f"X{t}{lv}{g}", V)] * (lv < LEVELS - 1) + [(f"XT{t}{lv}{g}", V)]
            out += [(f"gt{6 + 3 * t + GATED.index(lv)}", A)] if lv in GATED else []
        out += [(f"W{t}", A), (f"Z{t}", A), (f"U{t}", A)]
        for n in (2 * t, 2 * t + 1):
            out += [(f"dU{n}{e}", V) for e in range(2)] * (n > 0)
            out += [(f"gt{8 + 3 * t}", A)] * (n == 2 * t)
            out += [(f"S{n + 1}", V)] * (n < 3)
        out += [(f"Y{t}{e}", A) for e in range(2)]
    for n in BRANCHES:
        out += [(f"yT{n}{u}", A) for u in range(2)]
        out += [(f"br{n}{u}{t}", V) for u in range(2) for t in range(T)]
    out += [(f"gT{q}", A) for q in range(4)]
    out += [(f"o{u}{t}", V) for u in range(2) for t in range(T)]
    out += [(f"fT{q}", A if l else V) for q in range(4)]
    if l == 0:
        for j in range(7):
            if j < 6:
                out += [(f"fg{j}{t}", A) for t in range(T)] + [(f"fu{j}{t}", V) for t in range(T)]
            if j > 0:
                out += [(f"hT{j - 1}{t}", V) for t in range(T)]
        out += [(f"fd{u}{t}", V) for u in range(2) for t in range(T)]
    else:
        out += [("router", V), ("rank", V)]
    return [(f"{n}.{l}", e) for n, e in out]


def moe_jobs():
    A, V = "act", "vec"
    out = [("csT", A), ("gx0", V), ("gx1", V)]
    for j in range(8):
        out += ([(f"eg{j}", A), (f"eu{j}", V)] if j < 7 else []) + ([(f"eT{j - 1}", V)] if j else [])
    out += [("ed0", V), ("ed1", V)]
    out += [(f"sc{u}{t}", V) for u in range(2) for t in range(T)]
    return out


JOBS = layer_jobs(0) + layer_jobs(1)
JOB_AT = {n: i for i, (n, _) in enumerate(JOBS)}
ITEM = moe_jobs()
ITEM_AT = {n: i for i, (n, _) in enumerate(ITEM)}
PANELS = panels()
EP = 21
HALVES = 14 + 13
SURE = NE


def freed_count(k, eng):
    return sum(e == eng for _, e in JOBS[:k + 1])


def item_freed(k, eng):
    return sum(e == eng for _, e in ITEM[:k + 1])


class Own:

    def __init__(self, eng, name, step_sem, freed_sem):
        self.eng, self.name, self.step_sem, self.freed_sem = eng, name, step_sem, freed_sem
        self.count, self.last = {}, None

    def step(self, ins, sem=None):
        sem = sem or self.step_sem
        self.count[id(sem)] = self.count.get(id(sem), 0) + 1
        ins.then_inc(sem, 1)
        self.last = (sem, self.count[id(sem)])

    def free(self, ins, job):
        self.step(ins, self.freed_sem)
        assert JOBS[JOB_AT[job]][1] == self.name
        assert self.count[id(self.freed_sem)] == freed_count(JOB_AT[job], self.name), job

    def settle(self):
        self.eng.wait_ge(*self.last)


class Signals:

    def __init__(self, nc):
        new = nc.alloc_semaphore
        self.const_loaded = new("const_loaded")
        self.pos_loaded = new("pos_loaded")
        self.x_loaded = new("x_loaded")
        self.vec_loaded = new("vec_loaded")
        self.gain_loaded = new("gain_loaded")
        self.router_loaded = new("router_loaded")
        self.fgain_loaded = new("fgain_loaded")
        self.f_hi_ready = new("f_hi_ready")
        self.f_lo_ready = new("f_lo_ready")
        self.f_half_used = new("f_half_used")
        self.f_x_hi_ready = new("f_x_hi_ready")
        self.hi_ready = new("hi_ready")
        self.lo_ready = new("lo_ready")
        self.half_used = new("half_used")
        self.x_hi_ready = new("x_hi_ready")
        self.product_ready = new("product_ready")
        self.freed_act = new("freed_act")
        self.freed_vec = new("freed_vec")
        self.act_step = new("act_step")
        self.vec_step = new("vec_step")
        self.pool_step = new("pool_step")
        self.out_stored = new("out_stored")
        self.angles_ready = new("angles_ready")
        self.trig_ready = new("trig_ready")
        self.sumsq_ready = new("sumsq_ready")
        self.var_ready = new("var_ready")
        self.root_ready = new("root_ready")
        self.hn_ready = new("hn_ready")
        self.shift_zero = new("shift_zero")
        self.shift_loaded = new("shift_loaded")
        self.xs_ready = new("xs_ready")
        self.lora_act_ready = new("lora_act_ready")
        self.knsq_ready = new("knsq_ready")
        self.knroot_ready = new("knroot_ready")
        self.decay_sig_ready = new("decay_sig_ready")
        self.rate_sig_ready = new("rate_sig_ready")
        self.logd_ready = new("logd_ready")
        self.exps_ready = new("exps_ready")
        self.cex_ready = new("cex_ready")
        self.scan_in_ready = new("scan_in_ready")
        self.rope_ready = new("rope_ready")
        self.silu_g_ready = new("silu_g_ready")
        self.gn_var_ready = new("gn_var_ready")
        self.gn_root_ready = new("gn_root_ready")
        self.ret_done = new("ret_done")
        self.qa_sumsq = new("qa_sumsq")
        self.qa_ready = new("qa_ready")
        self.mla_key_ready = new("mla_key_ready")
        self.masked_ready = new("masked_ready")
        self.prob_ready = new("prob_ready")
        self.merged_done = new("merged_done")
        self.x_ready = new("x_ready")
        self.state_ready = new("state_ready")
        self.rwkv_done = new("rwkv_done")
        self.route_exp = new("route_exp")
        self.route_diff = new("route_diff")
        self.mask_ready = new("mask_ready")
        self.items_ready = new("items_ready")
        self.sel_ready = new("sel_ready")
        self.item_step = new("item_step")
        self.fin_ready = new("fin_ready")
        self.items_done = new("items_done")


def build(nc, x, positions, attn_norm, w_in, rwkv_mu, rwkv_w0, rwkv_w2, rwkv_a0, rwkv_a2, rwkv_g2, rwkv_k_k,
          rwkv_k_a, rwkv_r_k, rwkv_lnx_w, mla_q_norm, mla_w_qb, mla_kv_norm, mla_w_kvb, w_branch, w_o, ffn_norm,
          ffn_w_gate, ffn_w_up, ffn_w_down, moe_router, moe_w_gate, moe_w_up, moe_w_down, final_norm, const, out):
    at = [-(-int(nc.sbuf_base) // 64) * 64]

    def sb(name, shape, dt=F32, where=None):
        size = -(-int(np.prod(shape[1:])) * 4 // 32) * 32
        if where is None:
            where = at[0]
            at[0] += size
        return nc.alloc_sbuf_tensor_at(name, shape, dt, offset=where)

    h = sb("h", [P, T, D])
    hnT_at = at[0]
    hnT = sb("hnT", [P, KD, SEQ])
    hn_at = at[0]
    hn = sb("hn", [P, T, D])
    y_ret = sb("y_ret", [P, T, W], where=hn_at)
    y_mla = sb("y_mla", [P, T, W], where=hn_at + 4096)
    ring = sb("ring", [P, RING, SLOT])
    cst = sb("cst", [P, CONST.shape[1]])
    gains = sb("gains", [P, DEPTH, 2, KD])
    mgain = sb("mgain", [P, DEPTH, 3])
    cosT = sb("cosT", [P, T, 80])
    sinT = sb("sinT", [P, T, 80])
    pos_i = sb("pos_i", [P, T], I32)
    pos_f = sb("pos_f", [P, T])
    stat = sb("stat", [P, 8, 16])
    den = sb("den", [P, NH, T])
    smax = sb("smax", [P, NH, T])
    decay_end = sb("decay_end", [P, T, 4, 2])
    E = at[0]
    vec = sb("vec", [P, VEC_COLS])
    pr_at = at[0]
    pr = sb("pr", [P, T, RWCOLS])
    scratch = at[0]
    prev = sb("prev", [P, T, RWCOLS])
    kk = sb("kk", [P, T, W], where=scratch)
    tmp = sb("tmp", [P, T, W], where=scratch + 4096)
    ab = sb("ab", [P, T, W], where=scratch + 8192)
    ld = sb("ld", [P, T, W])
    ec_at = at[0]
    ec = sb("ec", [P, T, W])
    enc = sb("enc", [P, T, W])
    gg = sb("gg", [P, T, W])
    y_rwkv = sb("y_rwkv", [P, T, W], where=ec_at - 4096)
    qa = sb("qa", [P, T, MLAC])
    B = at[0]
    raw = sb("raw", [P, 4, T, W], where=B)
    qkT = sb("qkT", [P, 2, RH, T, P], where=B + 16384)
    rope_tmp = sb("rope_tmp", [P, 2048], where=B + 16384)
    sR = sb("sR", [P, RH, 384], where=B + 24576)
    mqT = sb("mqT", [P, NH, SEQ], where=B)
    mkT = sb("mkT", [P, NH, SEQ], where=B + 8192)
    mq = sb("mq", [P, T, NH, QK], where=B + 30720)
    mk = sb("mk", [P, T, NH, QK], where=B + 36864)
    mv = sb("mv", [P, T, NH, NOPE], where=B + 43008)
    sm = sb("sm", [P, 2, 384], where=B + 47104)
    pT = sb("pT", [P, 2, 384], where=B + 50176)
    loT = sb("loT", [P, T, 384], where=B + 47104)
    cT = sb("cT", [P, 3, SEQ], where=B + 50176)
    mrope_tmp = sb("mrope_tmp", [P, 4, P], where=B + 47104)
    tT = sb("tT", [P, 4, 512], where=B)
    m1 = sb("m1", [P, NH, 512], where=B + 8192)
    am = sb("am", [P, NH, P], where=B + 24576)
    xi = sb("xi", [P, NH, P], where=B + 28672)
    xt = sb("xt", [P, NH, P], where=B + 32768)
    t1 = sb("t1", [P, NH, P], where=B + 36864)
    zz = sb("zz", [P, W], where=B + 40960)
    uu = sb("uu", [P, T, W], where=B + 43008)
    nw = sb("nw", [P, 4, P], where=B + 47104)
    st = sb("st", [P, 3, 4, HD], where=B + 49152)
    merged = sb("merged", [P, T, D], where=B)
    sigs = [sb(f"sig{n}", [P, 2, T, 512], where=w) for n, w in enumerate((E, E + 8192, ec_at))]
    assert VEC_AT["lnx"][0] * 4 >= 16384
    yT = sb("yT", [P, 2, 4, SEQ], where=B + 24576)
    gT = sb("gT", [P, KD, SEQ], where=B + 32768)
    hmT_hi = sb("hmT_hi", [P, 22, SEQ], F32R, where=B)
    hmT_lo = sb("hmT_lo", [P, 22, SEQ], F32R, where=B + 22528)
    hm = sb("hm", [P, 2, T, 512], where=B + 45056)
    sg = sb("sg", [P, 2, T, 512], where=hn_at)
    f_hi = sb("f_hi", [P, 2, HALF], F32R, where=pr_at)
    f_lo = sb("f_lo", [P, 2, HALF], F32R, where=pr_at + 16384)
    fx_hi = sb("fx_hi", [P, KD, SEQ], F32R, where=hnT_at)
    fx_lo = sb("fx_lo", [P, KD, SEQ], F32R, where=ec_at)
    X = E
    w_hi = sb("w_hi", [P, PARTS, HALF], F32R, where=X)
    w_lo = sb("w_lo", [P, PARTS, HALF], F32R, where=X + 24576)
    xg_hi = sb("xg_hi", [P, KD, P], F32R, where=X + 49152)
    xg_lo = sb("xg_lo", [P, KD, P], F32R, where=X + 53248)
    ehT_hi = sb("ehT_hi", [P, 28, P], F32R, where=X + 57344)
    ehT_lo = sb("ehT_lo", [P, 28, P], F32R, where=X + 71680)
    sel = sb("sel", [P, T, P], where=X + 86016)
    csel = sb("csel", [P, T, P], where=X + 87040)
    cselT = sb("cselT", [P, SEQ], where=X + 88064)
    ehm = sb("ehm", [P, 2, 512], where=X + 89088)
    esg = sb("esg", [P, 2, 512], where=X + 93184)
    ey = sb("ey", [P, D], where=X + 97280)
    rt = sb("rt", [P, 16, T, NE], where=X + 101376)
    router = sb("router", [P, KD, NE], where=X + 102400)
    it_f = sb("it_f", [1, 64], where=X + 102656)
    items = sb("items", [1, 32], I32, where=X + 102912)
    spos = sb("spos", [P, 2, T, NE], where=X + 103040)
    comb = sb("comb", [P, 2, T, NE], where=X + 103168)
    fin = sb("fin", [P, T, D], where=X)
    fgain = sb("fgain", [P, D], where=X + 104448)
    assert X + 104448 + 4096 <= B + 53248
    assert B + 53248 <= int(nc.sbuf_usable_end), (B, int(nc.sbuf_usable_end))

    def C(name, a=0, b=None):
        o, n = CONST_AT[name]
        return cst[:, o + a:o + (n if b is None else b)]

    def VEC(name, a=0, b=None):
        o, n = VEC_AT[name]
        return vec[:, o + a:o + (n if b is None else b)]

    def each(ap, n=T):
        return ap.unsqueeze(1).to_broadcast([ap.shape[0], n, ap.shape[1]])

    def wide(ap, n):
        return ap.unsqueeze(len(ap.shape)).to_broadcast(list(ap.shape) + [n])

    banks = [nc.alloc_psum_tensor(f"bank{i}", [P, 512], F32) for i in range(BANKS)]

    s = Signals(nc)
    slot_loaded = [nc.alloc_semaphore(f"slot{i}_loaded") for i in range(RING)]
    freed = {"act": s.freed_act, "vec": s.freed_vec}
    FR = {e: freed_count(len(JOBS) - 1, e) for e in freed}
    IF = {e: item_freed(len(ITEM) - 1, e) for e in freed}
    NPAN = len(PANELS)

    def product(eng, job):
        eng.wait_ge(s.product_ready, JOB_AT[job] + 1)
        return banks[JOB_AT[job] % BANKS]

    def read_out(eng, job):
        k = JOB_AT[job]
        eng.wait_ge(freed[JOBS[k][1]], freed_count(k, JOBS[k][1]))

    def used_up(n):
        kind, l, j, _ = PANELS[n]
        if kind.startswith("ffn"):
            return s.f_lo_ready, 2 * (n - FIRST_FFN + 1)
        job = {"in": f"in{j}_1.{l}", "lora": f"g1.{l}", "mla": f"mk11.{l}", "gate": f"gt{2 * j + 1}.{l}",
               "branch": f"br{j}11.{l}", "o": f"o{j}1.{l}"}[kind]
        return s.product_ready, JOB_AT[job] + 1

    FIRST_FFN = next(m for m, p in enumerate(PANELS) if p[0] == "ffn_gate")

    def ffn_half(q):
        width = FFN_COLS[q // 4] * 4 if q < 24 else FFN_COLS[(q - 24) // 2] // P * D // 2
        return ring[:, (FIRST_FFN + q // 2) % RING, width * (q % 2):width * (q % 2) + width], width

    def ffn_half_used(eng, q):
        if q < 24 and q % 2:
            eng.wait_ge(s.product_ready, JOB_AT[f"f{'gu'[q // 2 % 2]}{q // 4}1.0"] + 1)
        else:
            eng.wait_ge(s.f_half_used, q // 2 + 1 if q < 24 else q - 24 + 13)

    def half_used(q, item):
        before, q = (1, q + 2 * EP) if q < 0 else (0, q)
        if q == 2 * EP - 1 or (q < 28 and q % 2):
            job = "ed1" if q >= 28 else f"e{'gu'[q // 2 % 2]}{q // 4}"
            return s.product_ready, item * len(ITEM) + (len(JOBS) + ITEM_AT[job] + 1 - len(ITEM) * before)
        n = q // 2 + 1 if q < 28 else q - 28 + 15
        return s.half_used, item * HALVES + (HALVES + n - HALVES * before)

    def panel_loaded(n):
        return 16 * sum(PANELS[m][3] for m in range(n + 1) if m % RING == n % RING)

    def rows(w):
        return w.rearrange("(p c) n -> p c n", p=P)

    blk = nc.Block()
    block = blk.__enter__()

    @block.sync
    def _(sp):
        for t in range(T):
            sp.dma_start(h[:, t, :], x[0, t * P:(t + 1) * P, :]).then_inc(s.x_loaded, 16)
        sp.dma_start(cst[:], const).then_inc(s.const_loaded, 16)
        for n, (kind, l, j, _) in enumerate(PANELS):
            if n >= RING:
                sp.wait_ge(*used_up(n - RING))
            slot = ring[:, n % RING, :]
            sem = slot_loaded[n % RING]

            def cols(w, c0, width):
                k = w.shape[0] // P
                dst = slot[:, 0:k * width].rearrange("p (c n) -> p c n", c=k)
                sp.dma_start(dst, rows(w)[:, :, c0:c0 + width]).then_inc(sem, 16)

            if kind == "in":
                cols(w_in[l], *IN_PANELS[j])
            elif kind == "gate":
                cols(w_in[l], C_GATE + 512 * j, 512)
            elif kind == "lora":
                sp.dma_start(slot[0:64, 0:512], rwkv_w2[l]).then_inc(sem, 16)
                sp.dma_start(slot[64:128, 0:512], rwkv_a2[l]).then_inc(sem, 16)
                sp.dma_start(slot[:, 512:1024], rwkv_g2[l, 0:128, :]).then_inc(sem, 16)
                sp.dma_start(slot[0:32, 1024:1536], rwkv_g2[l, 128:160, :]).then_inc(sem, 16)
            elif kind == "mla":
                sp.dma_start(slot[:, 0:1536].rearrange("p (c n) -> p c n", c=2), rows(mla_w_qb[l])).then_inc(sem, 16)
                sp.dma_start(slot[:, 1536:2560], mla_w_kvb[l]).then_inc(sem, 16)
            elif kind == "branch":
                cols(w_branch[l, j], 0, D)
            elif kind == "o":
                cols(w_o[l], 512 * j, 512)
            elif kind == "ffn_gate":
                cols(ffn_w_gate[0], 512 * j, FFN_COLS[j])
            elif kind == "ffn_up":
                cols(ffn_w_up[0], 512 * j, FFN_COLS[j])
            else:
                cols(ffn_w_down[0, 512 * j:512 * j + FFN_COLS[j], :], 0, D)

        def expert_panels(e, item):
            for m in range(EP):
                i = (NPAN + m) % RING
                sp.wait_ge(s.lo_ready, item * (2 * EP) + (2 * RING + 2 * (m - RING + 1)))
                if m < 14:
                    w = (moe_w_gate, moe_w_up)[m % 2][0, bass.ds(e, 1), :, 512 * (m // 2):512 * (m // 2) + 512]
                    k = KD
                else:
                    w = moe_w_down[0, bass.ds(e, 1), 512 * (m - 14):512 * (m - 14) + 512, :]
                    k = 4
                sp.dma_start(ring[:, i, :].rearrange("p (c n) -> p c n", c=k),
                             w.rearrange("o (p c) n -> p (o c) n", p=P)).then_inc(slot_loaded[i], 16)

        sp.wait_ge(*used_up(NPAN - 1))
        with sp.Fori(0, SURE) as item:
            expert_panels(item, item)
        sp.wait_ge(s.items_ready, 1)
        n_items = sp.value_load(items[0:1, 24:25], min_val=SURE, max_val=SURE + 3)
        with sp.If(n_items > SURE):
            with sp.Fori(SURE, n_items) as item:
                e = sp.value_load(items[0:1, bass.ds(item + 12, 1)], min_val=0, max_val=NE - 1)
                expert_panels(e, item)
            sp.nop()
        with sp.Else():
            sp.nop()
        for t in range(T):
            sp.wait_ge(s.fin_ready, t + 1)
            sp.dma_start(out[0, t * P:(t + 1) * P, :], fin[:, t, :]).then_inc(s.out_stored, 16)
        sp.wait_ge(s.out_stored, 16 * T)

    @block.gpsimd
    def _(pool):
        for t in range(T):
            pool.dma_start(pos_i[:, t:t + 1], positions[:, t * P:(t + 1) * P].rearrange("a p -> p a"))\
                .then_inc(s.pos_loaded, 16)
        own = Own(pool, "pool", s.pool_step, None)
        G = nc.gpsimd

        def rotate(x1, x2, c, sn, f, ready):
            own.step(G.tensor_tensor(f[0], x1, sn, ALU.mult))
            own.step(G.tensor_tensor(f[1], x2, sn, ALU.mult))
            own.step(G.tensor_tensor(f[2], x1, c, ALU.mult))
            own.step(G.tensor_tensor(f[3], x2, c, ALU.mult))
            own.settle()
            own.step(G.tensor_tensor(x1, f[2], f[1], ALU.subtract))
            own.step(G.tensor_tensor(x2, f[0], f[3], ALU.add), ready)

        for l in range(DEPTH):
            if l:
                pool.wait_ge(s.merged_done, 2 * T * l)
            for name, w in (("mu", rwkv_mu[l]), ("w0", rwkv_w0[l]), ("a0", rwkv_a0[l]), ("k_k", rwkv_k_k[l]),
                            ("k_a", rwkv_k_a[l]), ("r_k", rwkv_r_k[l].rearrange("h d -> (h d)")),
                            ("lnx", rwkv_lnx_w[l])):
                pool.dma_start(VEC(name), w.partition_broadcast(P)).then_inc(s.vec_loaded, 16)
            if l:
                read_out(pool, f"fd11.{l - 1}")
            own.step(G.memset(prev[0:1, 0, :], 0.0), s.shift_zero)
            pool.wait_ge(s.trig_ready, 2)
            read_out(pool, f"in5_1.{l}")
            for t in range(T):
                qk = raw[:, 0:2, t, :].rearrange("p a (h e) -> p a h e", h=RH)
                c, sn = (x[:, t, 0:64].unsqueeze(1).unsqueeze(1).to_broadcast([P, 2, RH, 64]) for x in (cosT, sinT))
                f = [rope_tmp[:, 512 * i:512 * i + 512].rearrange("p (a h e) -> p a h e", a=2, h=RH)
                     for i in range(4)]
                if t:
                    own.settle()
                rotate(qk[:, :, :, 0:64], qk[:, :, :, 64:128], c, sn, f, s.rope_ready)
            read_out(pool, f"mk11.{l}")
            for t in range(T):
                own.settle()
                f = [mrope_tmp[:, i, :].rearrange("p (h e) -> p h e", h=8) for i in range(4)]
                rotate(mq[:, t, :, 64:80], mq[:, t, :, 80:96], each(cosT[:, t, 64:80], 8),
                       each(sinT[:, t, 64:80], 8), f, s.pool_step)
                own.settle()
                rotate(qa[:, t, 384:400], qa[:, t, 400:416], cosT[:, t, 64:80], sinT[:, t, 64:80],
                       [mrope_tmp[:, i, 0:16] for i in range(4)], s.pool_step)
                own.settle()
                own.step(G.tensor_copy(mk[:, t, :, 64:96], each(qa[:, t, 384:416], NH)), s.mla_key_ready)
        read_out(pool, "o11.1")
        pool.dma_start(router[:], moe_router[0].rearrange("(p c) n -> p c n", p=P)).then_inc(s.router_loaded, 16)
        pool.dma_start(fgain[:], final_norm.partition_broadcast(P)).then_inc(s.fgain_loaded, 16)

    @block.scalar
    def _(act):
        own = Own(act, "act", s.act_step, s.freed_act)
        A = nc.scalar

        def norm_sums(m):
            for t in range(T):
                own.step(A.activation(hn[:, t, :], h[:, t, :], ACT.Square, accum_out=stat[:, 0, t:t + 1]),
                         s.sumsq_ready)
            act.wait_ge(s.var_ready, m + 1)
            own.step(A.activation(stat[:, 0, 0:T], stat[:, 0, 0:T], ACT.Sqrt), s.root_ready)

        def norm_transposed(name, l, g):
            for q in range(4):
                b = product(act, f"{name}{q}.{l}")
                for i in range(2):
                    c = 2 * q + i
                    ins = A.activation(hnT[:, c, :], b[:, 256 * i:256 * i + 256], ACT.Copy,
                                       scale=gains[:, l, g, c:c + 1])
                    own.step(ins) if i == 0 else own.free(ins, f"{name}{q}.{l}")

        def copy_out(job, dst, cols=None, rows_=P, scale=1.0):
            b = product(act, job)
            src = b[0:rows_, 0:cols or 512]
            if len(dst.shape) == 3:
                src = src.rearrange("p (a b) -> p a b", a=dst.shape[1])
            own.free(A.activation(dst, src, ACT.Copy, scale=scale), job)

        for l in range(DEPTH):
            for g, w in enumerate((attn_norm, ffn_norm)):
                act.dma_start(gains[:, l, g, :], w[l].rearrange("(p c) -> p c", p=P)).then_inc(s.gain_loaded, 16)
            act.dma_start(mgain[:, l, 0:2], mla_q_norm[l].rearrange("(p c) -> p c", p=P)).then_inc(s.gain_loaded, 16)
            act.dma_start(mgain[:, l, 2:3], mla_kv_norm[l].rearrange("(p c) -> p c", p=P)).then_inc(s.gain_loaded, 16)
        act.wait_ge(s.gain_loaded, 16 * 4 * DEPTH)
        for l in range(DEPTH):
            if l:
                read_out(act, f"fd11.{l - 1}")
            else:
                act.wait_ge(s.x_loaded, 16 * T)
            norm_sums(2 * l)
            norm_transposed("nT", l, 0)
            if l == 0:
                act.wait_ge(s.angles_ready, 1)
                own.step(A.activation(sinT[:], sinT[:], ACT.Sin), s.trig_ready)
                own.step(A.activation(cosT[:], cosT[:], ACT.Sin), s.trig_ready)
            for j, (c0, width) in enumerate(IN_PANELS):
                for t in range(T):
                    if j < 4:
                        o = 1536 if j == 0 else 512 * (j - 1)
                        dst = pr[:, t, o:o + width]
                    elif j < 8:
                        dst = raw[:, j - 4, t, :]
                    else:
                        dst = qa[:, t, :]
                    copy_out(f"in{j}_{t}.{l}", dst, width)
                if j == 3:
                    own.settle()
                    act.wait_ge(s.shift_zero, l + 1)
                    act.dma_start(prev[1:P, :, :], pr[0:P - 1, :, :]).then_inc(s.shift_loaded, 16)
                    act.dma_start(prev[0:1, 1, :], pr[P - 1:P, 0, :]).then_inc(s.shift_loaded, 16)
                if j == 6:
                    act.wait_ge(s.xs_ready, l + 1)
                    own.step(A.activation(pr[:, :, 1536:1600], pr[:, :, 1536:1600], ACT.Tanh))
                    own.step(A.activation(pr[:, :, 1664:1824], pr[:, :, 1664:1824], ACT.Sigmoid), s.lora_act_ready)
                if j == 7:
                    own.settle()
                    own.step(A.activation(raw[:, 3, :, :], raw[:, 3, :, :], ACT.Silu), s.silu_g_ready)
                    for t in range(T):
                        b = product(act, f"loT{t}.{l}")
                        own.step(A.activation(loT[:, t, 0:256], b[:, 0:256], ACT.Copy))
                        own.free(A.activation(loT[0:32, t, 256:384], b[0:32, 256:384], ACT.Copy), f"loT{t}.{l}")
            own.settle()
            for t in range(T):
                own.step(A.activation(hn[:, t, 0:256], qa[:, t, 0:256], ACT.Square,
                                      accum_out=stat[:, 2, 2 * t:2 * t + 1]), s.qa_sumsq)
                own.step(A.activation(hn[:, t, 256:384], qa[:, t, 256:384], ACT.Square,
                                      accum_out=stat[:, 2, 2 * t + 1:2 * t + 2]), s.qa_sumsq)
            for t in range(T):
                copy_out(f"g{t}.{l}", gg[:, t, :])
            read_out(act, f"z1.{l}")
            own.step(A.activation(ld[:], ld[:], ACT.Sigmoid), s.decay_sig_ready)
            read_out(act, f"a1.{l}")
            own.step(A.activation(ab[:], ab[:], ACT.Sigmoid), s.rate_sig_ready)
            act.wait_ge(s.knsq_ready, l + 1)
            own.step(A.activation(stat[:, 1, :], stat[:, 1, :], ACT.Sqrt))
            own.step(A.activation(stat[:, 2, 0:4], stat[:, 2, 0:4], ACT.Sqrt), s.knroot_ready)
            act.wait_ge(s.rope_ready, T * (l + 1))
            for t in range(T):
                for q in range(2):
                    copy_out(f"rT{q}{t}.{l}", qkT[:, q, :, t, :])
            for t in range(T):
                b = product(act, f"cT{t}.{l}")
                for i in range(3):
                    ins = A.activation(cT[:, i, t * P:(t + 1) * P], b[:, i * P:(i + 1) * P], ACT.Copy,
                                       scale=mgain[:, l, i:i + 1])
                    own.step(ins) if i < 2 else own.free(ins, f"cT{t}.{l}")
            for t in range(T):
                for u in range(2):
                    copy_out(f"mq{t}{u}.{l}", mq[:, t, 4 * u:4 * u + 4, :], 384)
            for t in range(T):
                for u in range(2):
                    b = product(act, f"mk{t}{u}.{l}")
                    kv = b[:].rearrange("p (h e) -> p h e", h=4)
                    own.step(A.activation(mk[:, t, 4 * u:4 * u + 4, 0:64], kv[:, :, 0:64], ACT.Copy))
                    own.free(A.activation(mv[:, t, 4 * u:4 * u + 4, :], kv[:, :, 64:128], ACT.Copy),
                             f"mk{t}{u}.{l}")
            for t in range(T):
                b = product(act, f"cum{t}.{l}")
                own.step(A.activation(ec[:, t, :], b[:], ACT.Exp))
                own.step(A.activation(enc[:, t, :], b[:], ACT.Exp, scale=-1.0), s.exps_ready)
            for t in range(T):
                act.wait_ge(s.cex_ready, T * l + t + 1)
                own.free(A.activation(ld[:, t, :], ld[:, t, :], ACT.Exp), f"cum{t}.{l}")
            b = product(act, f"pc.{l}")
            own.free(A.activation(decay_end[:], b[:, 0:16].rearrange("p (t a c) -> p t a c", t=T, a=4), ACT.Exp),
                     f"pc.{l}")
            for t in range(T):
                copy_out(f"oR{t}.{l}", y_ret[:, t, :])
            act.wait_ge(s.gn_var_ready, 2 * l + 1)
            own.step(A.activation(stat[:, 4, 0:8], stat[:, 4, 0:8], ACT.Sqrt), s.gn_root_ready)
            def gate(g):
                n, u, t = g // 4, g // 2 % 2, g % 2
                b = product(act, f"gt{g}.{l}")
                own.free(A.activation(sigs[n][:, u, t, :], b[:], ACT.Sigmoid), f"gt{g}.{l}")

            for q, dst in enumerate((mqT, mkT)):
                gate(q)
                if q:
                    act.wait_ge(s.ret_done, l + 1)
                for u in range(4):
                    copy_out(f"mT{q}{u}.{l}", dst[0:QK, 2 * u:2 * u + 2, :], rows_=QK)
            for i in range(NH + 1):
                if i < NH:
                    act.wait_ge(s.masked_ready, NH * l + i + 1)
                    own.step(A.activation(sm[:, i % 2, 0:128], sm[:, i % 2, 0:128], ACT.Exp,
                                          bias=smax[:, i, 0:1], accum_out=den[:, i, 0:1]))
                    own.step(A.activation(sm[:, i % 2, 128:384], sm[:, i % 2, 128:384], ACT.Exp,
                                          bias=smax[:, i, 1:2], accum_out=den[:, i, 1:2]), s.prob_ready)
                if i:
                    copy_out(f"pT{i - 1}.{l}", pT[:, (i - 1) % 2, :], 384)
                if i % 2 and i < NH:
                    gate(2 + i // 2)

            for t in range(T):
                for hp in range(4):
                    copy_out(f"kT{t}{hp}.{l}", tT[:, hp, :])
                for g in range(len(GATED)):
                    gate(6 + 3 * t + g)
                copy_out(f"W{t}.{l}", nw[:], scale=-1.0)
                copy_out(f"Z{t}.{l}", zz[:])
                copy_out(f"U{t}.{l}", uu[:, t, :])
                gate(8 + 3 * t)
                for e in range(2):
                    copy_out(f"Y{t}{e}.{l}", y_rwkv[:, t, :].rearrange("p (a b d) -> p a b d", a=4, b=2)[:, :, e, :],
                             256)
            act.wait_ge(s.gn_var_ready, 2 * l + 2)
            own.step(A.activation(stat[:, 4, :], stat[:, 4, :], ACT.Sqrt), s.gn_root_ready)
            for i, n in enumerate(BRANCHES):
                for u in range(2):
                    copy_out(f"yT{n}{u}.{l}", yT[:, i % 2, 2 * u:2 * u + 2, :])
            for q in range(4):
                copy_out(f"gT{q}.{l}", gT[:, 2 * q:2 * q + 2, :])
            read_out(act, f"o11.{l}")
            norm_sums(2 * l + 1)
            if l:
                norm_transposed("fT", l, 1)
            else:
                for q in range(4):
                    b = product(act, f"fT{q}.0")
                    for i in range(2):
                        c = 2 * q + i
                        own.step(A.activation(fx_hi[:, c, :], b[:, 256 * i:256 * i + 256], ACT.Copy,
                                              scale=gains[:, 0, 1, c:c + 1]), s.f_x_hi_ready if i else None)
                for q in range(36):
                    src, width = ffn_half(q)
                    if q % 2 == 0:
                        n = FIRST_FFN + q // 2
                        act.wait_ge(slot_loaded[n % RING], panel_loaded(n))
                    if q > 1:
                        ffn_half_used(act, q - 2)
                    own.step(A.activation(f_hi[:, q % 2, 0:width], src, ACT.Copy), s.f_hi_ready)
                    if q % 4 == 3 and q < 24:
                        j = q // 4
                        w_ = FFN_COLS[j]
                        for t in range(T):
                            if j > 1:
                                read_out(act, f"fu{j - 2}{t}.0")
                            b = product(act, f"fg{j}{t}.0")
                            own.free(A.activation(sg[:, j % 2, t, 0:w_], b[:, 0:w_], ACT.Silu), f"fg{j}{t}.0")
                    if q % 4 == 1 and 9 <= q <= 29:
                        j = (q - 9) // 4
                        k = FFN_COLS[j] // P
                        for t in range(T):
                            b = product(act, f"hT{j}{t}.0")
                            own.step(A.activation(hmT_hi[:, 4 * j:4 * j + k, t * P:(t + 1) * P],
                                                  b[:, 0:k * P].rearrange("p (c n) -> p c n", c=k), ACT.Copy),
                                     s.f_x_hi_ready)
        act.wait_ge(s.route_diff, 1)
        own.step(A.activation(stat[:, 6, 0:2], stat[:, 6, 0:2], ACT.Exp), s.route_exp)
        act.wait_ge(s.items_ready, 1)
        n_items = act.value_load(items[0:1, 24:25], min_val=SURE, max_val=SURE + 3)
        with act.Fori(0, n_items) as item:
            def item_product(job):
                act.wait_ge(s.product_ready, item * len(ITEM) + (len(JOBS) + ITEM_AT[job] + 1))
                return banks[ITEM_AT[job] % BANKS]

            def hi(q):
                if q % 2 == 0:
                    m = q // 2
                    i = (NPAN + m) % RING
                    before = 16 * sum(PANELS[n][3] for n in range(NPAN) if n % RING == i)
                    nth = sum((NPAN + r) % RING == i for r in range(m + 1))
                    act.wait_ge(slot_loaded[i], item * (16 * EP // RING) + (before + 16 * nth))
                act.wait_ge(*half_used(q - PARTS, item))
                i, o = (NPAN + q // 2) % RING, HALF * (q % 2)
                A.activation(w_hi[:, q % PARTS, :], ring[:, i, o:o + HALF], ACT.Copy).then_inc(s.hi_ready, 1)

            for q in range(2 * EP):
                hi(q)
                if q == 2:
                    A.activation(cselT[:], item_product("csT")[:, 0:SEQ], ACT.Copy).then_inc(s.freed_act, 1)
                    for u in range(2):
                        b = item_product(f"gx{u}")
                        for i in range(4):
                            ins = A.activation(xg_hi[:, 4 * u + i, :], b[:, i * P:(i + 1) * P], ACT.Copy,
                                               scale=gains[:, 1, 1, 4 * u + i:4 * u + i + 1])
                        ins.then_inc(s.x_hi_ready, 1)
                if q % 4 == 3 and q < 28:
                    j = q // 4
                    if j > 1:
                        act.wait_ge(s.freed_vec,
                                    item * IF["vec"] + (FR["vec"] + item_freed(ITEM_AT[f"eu{j - 2}"], "vec")))
                    A.activation(esg[:, j % 2, :], item_product(f"eg{j}")[:], ACT.Silu).then_inc(s.freed_act, 1)
                if q % 4 == 1 and 9 <= q <= 33:
                    j = (q - 9) // 4
                    A.activation(ehT_hi[:, 4 * j:4 * j + 4, :],
                                 item_product(f"eT{j}")[:].rearrange("p (c n) -> p c n", c=4),
                                 ACT.Copy).then_inc(s.x_hi_ready, 1)
        act.wait_ge(s.items_done, 1)
        norm_sums(4)

    @block.tensor
    def _(pe):
        M, TR = nc.tensor.matmul, nc.tensor.transpose
        ident = C("ident")
        used = [0]

        def bank(job):
            k = JOB_AT[job]
            if k >= BANKS:
                e = JOBS[k - BANKS][1]
                pe.wait_ge(freed[e], freed_count(k - BANKS, e))
            return banks[k % BANKS]

        def panel(kind):
            n = used[0]
            assert PANELS[n][0] == kind, (n, PANELS[n], kind)
            pe.wait_ge(slot_loaded[n % RING], panel_loaded(n))
            used[0] += 1
            return ring[:, n % RING, :]

        def done(ins):
            ins.then_inc(s.product_ready, 1)

        def transpose_in(jobs, src):
            for q in range(4):
                b = bank(jobs.format(q))
                for i in range(2):
                    for t in range(T):
                        ins = TR(b[:, 256 * i + 128 * t:256 * i + 128 * t + 128], src[:, t, 2 * q + i:D:KD], ident)
                done(ins)

        def project(job, lhs, slot, k, width, t, c0=0, row=None):
            b = bank(job)
            w = slot[:, 0:k * (row or width)].rearrange("p (c n) -> p c n", c=k)
            for c in range(k):
                ins = M(b[:, 0:width], lhs[:, c, t * P:(t + 1) * P], w[:, c, c0:c0 + width], start=c == 0,
                        stop=c == k - 1)
            done(ins)

        pe.wait_ge(s.const_loaded, 16)
        for l in range(DEPTH):
            pe.wait_ge(s.hn_ready, 2 * T * l + T)
            transpose_in("nT{}." + str(l), hn)
            read_out(pe, f"nT3.{l}")
            for j, (_, width) in enumerate(IN_PANELS):
                if j == 8:
                    pe.wait_ge(s.lora_act_ready, l + 1)
                    for t in range(T):
                        b = bank(f"loT{t}.{l}")
                        TR(b[:, 0:128], pr[:, t, 1536:1664], ident)
                        TR(b[:, 128:256], pr[:, t, 1664:1792], ident)
                        done(TR(b[0:32, 256:384], pr[:, t, 1792:1824], ident))
                slot = panel("in")
                for t in range(T):
                    project(f"in{j}_{t}.{l}", hnT, slot, KD, width, t)
            slot = panel("lora")
            for t in range(T):
                read_out(pe, f"loT{t}.{l}")
                done(M(bank(f"z{t}.{l}")[:], loT[0:64, t, 0:128], slot[0:64, 0:512], start=True, stop=True))
                done(M(bank(f"a{t}.{l}")[:], loT[64:128, t, 0:128], slot[64:128, 0:512], start=True, stop=True))
                b = bank(f"g{t}.{l}")
                M(b[:], loT[:, t, 128:256], slot[:, 512:1024], start=True, stop=False)
                done(M(b[:], loT[0:32, t, 256:384], slot[0:32, 1024:1536], start=False, stop=True))
            for t in range(T):
                pe.wait_ge(s.rope_ready, T * l + t + 1)
                for q in range(2):
                    b = bank(f"rT{q}{t}.{l}")
                    for i in range(RH):
                        ins = TR(b[:, i * P:(i + 1) * P], raw[:, q, t, i * P:(i + 1) * P], ident)
                    done(ins)
            slot = panel("mla")
            pe.wait_ge(s.qa_ready, l + 1)
            for t in range(T):
                b = bank(f"cT{t}.{l}")
                for i in range(2):
                    TR(b[:, i * P:(i + 1) * P], qa[:, t, i:256:2], ident)
                done(TR(b[:, 256:384], qa[:, t, 256:384], ident))
            read_out(pe, f"cT1.{l}")
            for t in range(T):
                for u in range(2):
                    project(f"mq{t}{u}.{l}", cT, slot, 2, 384, t, 384 * u, 768)
            for t in range(T):
                for u in range(2):
                    done(M(bank(f"mk{t}{u}.{l}")[:], cT[:, 2, t * P:(t + 1) * P],
                           slot[:, 1536 + 512 * u:2048 + 512 * u], start=True, stop=True))
            read_out(pe, f"rT11.{l}")
            for i in range(RH):
                b = bank(f"sR{i}.{l}")
                M(b[:, 0:256], qkT[:, 1, i, 0, :], qkT[:, 0, i, :, :], start=True, stop=True)
                done(M(b[:, 256:384], qkT[:, 1, i, 1, :], qkT[:, 0, i, 1, :], start=True, stop=True))
            pe.wait_ge(s.logd_ready, l + 1)
            for t in range(T):
                done(M(bank(f"cum{t}.{l}")[:], C("chunk_upto"), ld[:, t, :], start=True, stop=True))
            b = bank(f"pc.{l}")
            for t in range(T):
                for hp in range(4):
                    o = 2 * (4 * t + hp)
                    ins = M(b[:, o:o + 2], ld[:, t, hp * P:(hp + 1) * P], C("chunk_sel"), start=True, stop=True)
            done(ins)
            read_out(pe, f"sR3.{l}")
            for t in range(T):
                b = bank(f"oR{t}.{l}")
                for i in range(RH):
                    o = b[:, i * P:(i + 1) * P]
                    cols = slice(i * P, (i + 1) * P)
                    if t == 0:
                        ins = M(o, sR[:, i, 0:128], raw[:, 2, 0, cols], start=True, stop=True)
                    else:
                        M(o, sR[:, i, 128:256], raw[:, 2, 0, cols], start=True, stop=False)
                        ins = M(o, sR[:, i, 256:384], raw[:, 2, 1, cols], start=False, stop=True)
                done(ins)
            gates = []

            def gate_part(g, a, b_):
                if a == 0:
                    if g % 2 == 0:
                        gates[:] = [panel("gate")]
                    bank(f"gt{g}.{l}")
                dst = banks[JOB_AT[f"gt{g}.{l}"] % BANKS]
                for c in range(a, b_):
                    ins = M(dst[:], hnT[:, c, (g % 2) * P:(g % 2) * P + P],
                            gates[0][:, 512 * c:512 * c + 512], start=c == 0, stop=c == KD - 1,
                            skip_group_check=True)
                if b_ == KD:
                    done(ins)

            gate_part(0, 0, 8)
            pe.wait_ge(s.mla_key_ready, T * (l + 1))
            for q, src in enumerate((mq, mk)):
                for u in range(4):
                    b = bank(f"mT{q}{u}.{l}")
                    for i in range(2):
                        for t in range(T):
                            ins = TR(b[0:QK, 256 * i + 128 * t:256 * i + 128 * t + 128], src[:, t, 2 * u + i, :],
                                     ident)
                    done(ins)
                if q == 0:
                    gate_part(1, 0, 8)
            read_out(pe, f"mT13.{l}")
            for i in range(NH + 2):
                if i < NH:
                    b = bank(f"sM{i}.{l}")
                    M(b[:, 0:128], mqT[0:QK, i, 0:128], mkT[0:QK, i, 0:128], start=True, stop=True)
                    done(M(b[:, 128:384], mqT[0:QK, i, 128:256], mkT[0:QK, i, :], start=True, stop=True))
                if i < NH:
                    gate_part(2 + i // 2, 4 * (i % 2), 3 + 4 * (i % 2))
                if 0 < i <= NH:
                    pe.wait_ge(s.prob_ready, NH * l + i)
                    b = bank(f"pT{i - 1}.{l}")
                    for c in range(3):
                        ins = TR(b[:, c * P:(c + 1) * P], sm[:, (i - 1) % 2, c * P:(c + 1) * P], ident)
                    done(ins)
                if i > 1:
                    k = i - 2
                    read_out(pe, f"pT{k}.{l}")
                    b = bank(f"oM{k}.{l}")
                    M(b[:, 0:64], pT[:, k % 2, 0:128], mv[:, 0, k, :], start=True, stop=True)
                    M(b[:, 64:128], pT[:, k % 2, 128:256], mv[:, 0, k, :], start=True, stop=False)
                    done(M(b[:, 64:128], pT[:, k % 2, 256:384], mv[:, 1, k, :], start=False, stop=True))
                if i < NH:
                    gate_part(2 + i // 2, 3 + 4 * (i % 2), 4 + 4 * (i % 2))
            pe.wait_ge(s.scan_in_ready, l + 1)
            scan_in = ((kk, 0), (pr, 0), (ab, 0), (pr, 512))
            for t in range(T):
                for hp in range(4):
                    b = bank(f"kT{t}{hp}.{l}")
                    for i, (src, c0) in enumerate(scan_in):
                        ins = TR(b[:, i * P:(i + 1) * P], src[:, t, c0 + hp * P:c0 + (hp + 1) * P], ident)
                    done(ins)
                for i in range(NH):
                    e, hp = i // 4, i % 4
                    half = slice(64 * e, 64 * e + 64)
                    if e == 0:
                        read_out(pe, f"kT{t}{hp}.{l}")
                    b = bank(f"M{t}{i}.{l}")
                    M(b[:, 0:256], tT[half, hp, 256:384], tT[half, hp, 0:256], start=True, stop=True)
                    done(M(b[:, 256:512], tT[half, hp, 384:512], tT[half, hp, 0:256], start=True, stop=True))
                for g in range(2):
                    b = bank(f"A{t}{g}.{l}")
                    half = slice(64 * g, 64 * g + 64)
                    for hp in range(4):
                        ins = M(b[:, hp * P:(hp + 1) * P], tT[half, hp, 0:128], tT[half, hp, 256:384], start=True,
                                stop=True)
                    done(ins)
                for lv in range(1, LEVELS):
                    gt = 6 + 3 * t + (GATED.index(lv) if lv in GATED else 0)
                    for g in range(2):
                        pe.wait_ge(s.x_ready, 2 * (T * l + t) + g + 1) if lv == 1 else \
                            read_out(pe, f"XT{t}{lv - 1}{g}.{l}")
                        b = bank(f"T{t}{lv}{g}.{l}")
                        for i in range(4):
                            ins = M(b[:, i * P:(i + 1) * P], m1[:, 4 * g + i, 0:128], xi[:, 4 * g + i, :],
                                    start=True, stop=True)
                        done(ins)
                    if lv in GATED:
                        gate_part(gt, 0, 3)
                    for g in range(2):
                        read_out(pe, f"T{t}{lv}{g}.{l}")
                        if lv < LEVELS - 1:
                            b = bank(f"X{t}{lv}{g}.{l}")
                            for i in range(4):
                                ins = M(b[:, i * P:(i + 1) * P], xt[:, 4 * g + i, :], t1[:, 4 * g + i, :],
                                        start=True, stop=True)
                            done(ins)
                        b = bank(f"XT{t}{lv}{g}.{l}")
                        for i in range(4):
                            ins = M(b[:, i * P:(i + 1) * P], t1[:, 4 * g + i, :], xt[:, 4 * g + i, :],
                                    start=True, stop=True)
                        done(ins)
                        if lv in GATED:
                            gate_part(gt, 3 + 2 * g, 5 + 3 * g)
                read_out(pe, f"XT{t}{LEVELS - 1}1.{l}")
                vcol = pr[:, t, 1024:1536]
                b = bank(f"W{t}.{l}")
                for hp in range(4):
                    for e in range(2):
                        ins = M(b[64 * e:64 * e + 64, hp * P:(hp + 1) * P],
                                kk[:, t, (2 * hp + e) * 64:(2 * hp + e) * 64 + 64], xt[:, 4 * e + hp, :],
                                start=True, stop=True)
                done(ins)
                b = bank(f"Z{t}.{l}")
                for i in range(NH):
                    hh = slice(64 * i, 64 * i + 64)
                    ins = M(b[:, hh], m1[:, 4 * (i % 2) + i // 2, 256:384], vcol[:, hh], start=True, stop=True)
                done(ins)
                gate_part(8 + 3 * t, 0, 2)
                read_out(pe, f"Z{t}.{l}")
                b = bank(f"U{t}.{l}")
                for i in range(NH):
                    hh = slice(64 * i, 64 * i + 64)
                    ins = M(b[:, hh], xt[:, 4 * (i % 2) + i // 2, :], zz[:, hh], start=True, stop=True)
                done(ins)
                gate_part(8 + 3 * t, 2, 5)
                read_out(pe, f"U{t}.{l}")
                for n in (2 * t, 2 * t + 1):
                    o = slice(64 * (n % 2), 64 * (n % 2) + 64)
                    if n:
                        pe.wait_ge(s.state_ready, 3 * l + n)
                        for e in range(2):
                            b = bank(f"dU{n}{e}.{l}")
                            half = slice(64 * e, 64 * e + 64)
                            for hp in range(4):
                                ins = M(b[o, 64 * hp:64 * hp + 64], nw[half, hp, o], st[half, n - 1, hp, :],
                                        start=True, stop=True)
                            done(ins)
                    if n == 2 * t:
                        gate_part(8 + 3 * t, 5, 8)
                    if n:
                        read_out(pe, f"dU{n}1.{l}")
                    if n < 3:
                        b = bank(f"S{n + 1}.{l}")
                        for hp in range(4):
                            for e in range(2):
                                hh = slice((2 * hp + e) * 64, (2 * hp + e) * 64 + 64)
                                dst = b[64 * e:64 * e + 64, 64 * hp:64 * hp + 64]
                                M(dst, ab[o, t, hh], uu[o, t, hh], start=True, stop=False)
                                ins = M(dst, pr[o, t, 512 + hh.start:512 + hh.stop],
                                        pr[o, t, 1024 + hh.start:1024 + hh.stop], start=False, stop=True)
                        done(ins)
                for e in range(2):
                    b = bank(f"Y{t}{e}.{l}")
                    half = slice(64 * e, 64 * e + 64)
                    for hp in range(4):
                        hh = slice((2 * hp + e) * 64, (2 * hp + e) * 64 + 64)
                        dst = slice(64 * hp, 64 * hp + 64)
                        M(b[:, dst], m1[:, 4 * e + hp, 384:512], vcol[:, hh], start=True, stop=False)
                        for n in (2 * t, 2 * t + 1):
                            if n:
                                o = 64 * (n % 2)
                                M(b[o:o + 64, dst], tT[half, hp, 128 + o:192 + o], st[half, n - 1, hp, :],
                                  start=False, stop=False)
                        ins = M(b[:, dst], m1[:, 4 * e + hp, 128:256], uu[:, t, hh], start=False, stop=True)
                    done(ins)
            for i_, n in enumerate(BRANCHES):
                y = (y_ret, y_rwkv, y_mla)[n]
                if n == 2:
                    read_out(pe, f"oM{NH - 1}.{l}")
                else:
                    pe.wait_ge((s.ret_done, s.rwkv_done)[n], l + 1)
                for u in range(2):
                    b = bank(f"yT{n}{u}.{l}")
                    for i in range(2):
                        for t in range(T):
                            ins = TR(b[:, 256 * i + 128 * t:256 * i + 128 * t + 128], y[:, t, 2 * u + i:W:4], ident)
                    done(ins)
                slot = panel("branch")
                read_out(pe, f"yT{n}1.{l}")
                for u in range(2):
                    for t in range(T):
                        project(f"br{n}{u}{t}.{l}", yT[:, i_ % 2], slot, 4, 512, t, 512 * u, D)
            pe.wait_ge(s.merged_done, T * 2 * (l + 1))
            transpose_in("gT{}." + str(l), merged)
            read_out(pe, f"gT3.{l}")
            for u in range(2):
                slot = panel("o")
                for t in range(T):
                    project(f"o{u}{t}.{l}", gT, slot, KD, 512, t)
            pe.wait_ge(s.hn_ready, 2 * T * l + 2 * T)
            transpose_in("fT{}." + str(l), hn)
            read_out(pe, f"fT3.{l}")
            if l == 0:
                def ffn_split(q):
                    pe.wait_ge(s.f_lo_ready, q + 1)
                    used[0] += q % 2

                def three(dst, x, c, t, b, cols, start, stop):
                    tok = slice(t * P, (t + 1) * P)
                    for n, (a, w) in enumerate(((x[0], f_hi), (x[0], f_lo), (x[1], f_hi))):
                        ins = M(dst, a[:, c, tok], w[:, b, cols], start=start and n == 0, stop=stop and n == 2,
                                skip_group_check=True)
                    return ins

                for j in range(7):
                    if j < 6:
                        w_ = FFN_COLS[j]
                        for g, jobs in enumerate(("fg", "fu")):
                            bs = [bank(f"{jobs}{j}{t}.0") for t in range(T)]
                            for r in range(2):
                                q = 4 * j + 2 * g + r
                                ffn_split(q)
                                for t in range(T):
                                    for c in range(4):
                                        x = 4 * r + c
                                        ins = three(bs[t][:, 0:w_], (fx_hi, fx_lo), x, t, q % 2,
                                                    slice(w_ * c, w_ * c + w_), x == 0, x == KD - 1)
                                    if r:
                                        done(ins)
                                if r == 0:
                                    ins.then_inc(s.f_half_used, 1)
                    if j:
                        k = FFN_COLS[j - 1] // P
                        for t in range(T):
                            read_out(pe, f"fu{j - 1}{t}.0")
                            b = bank(f"hT{j - 1}{t}.0")
                            for c in range(k):
                                ins = TR(b[:, c * P:(c + 1) * P], hm[:, (j - 1) % 2, t, c:k * P:k], ident)
                            done(ins)
                outs = [(u, t, bank(f"fd{u}{t}.0")) for u in range(2) for t in range(T)]
                for j in range(6):
                    read_out(pe, f"hT{j}1.0")
                    k = FFN_COLS[j] // P
                    for r in range(2):
                        q = 24 + 2 * j + r
                        ffn_split(q)
                        for u, t, b in outs:
                            for c in range(k // 2):
                                x = 4 * j + k // 2 * r + c
                                ins = three(b[:], (hmT_hi, hmT_lo), x, t, q % 2,
                                            slice(D * c + 512 * u, D * c + 512 * u + 512), x == 0, x == 21)
                            if x == 21:
                                done(ins)
                        if x < 21:
                            ins.then_inc(s.f_half_used, 1)
        pe.wait_ge(s.router_loaded, 16)
        b = bank("router.1")
        for t in range(T):
            for c in range(KD):
                ins = M(b[:, NE * t:NE * t + NE], hnT[:, c, t * P:(t + 1) * P], router[:, c, :], start=c == 0,
                        stop=c == KD - 1)
        done(ins)
        pe.wait_ge(s.mask_ready, 1)
        b = bank("rank.1")
        m0, m1_ = rt[:, 8, 0, :], rt[:, 8, 1, :]
        M(b[:, 0:NE], C("upto"), m0, start=True, stop=True)
        M(b[:, NE:2 * NE], C("ones"), m0, start=True, stop=False)
        M(b[:, NE:2 * NE], C("upto"), m1_, start=False, stop=True)
        M(b[:, 2 * NE:3 * NE], C("ones"), m0, start=True, stop=False)
        done(M(b[:, 2 * NE:3 * NE], C("ones"), m1_, start=False, stop=True))
        pe.wait_ge(s.freed_act, FR["act"])
        pe.wait_ge(s.freed_vec, FR["vec"])
        pe.wait_ge(s.items_ready, 1)
        n_items = pe.value_load(items[0:1, 24:25], min_val=SURE, max_val=SURE + 3)
        with pe.Fori(0, n_items) as item:
            def item_read_out(job):
                k = ITEM_AT[job]
                e = ITEM[k][1]
                pe.wait_ge(freed[e], item * IF[e] + (FR[e] + item_freed(k, e)))

            def item_bank(job):
                k = ITEM_AT[job]
                if k >= BANKS:
                    item_read_out(ITEM[k - BANKS][0])
                else:
                    p = max(m for m in range(len(ITEM)) if m % BANKS == k)
                    e = ITEM[p][1]
                    pe.wait_ge(freed[e], item * IF[e] + (FR[e] - IF[e] + item_freed(p, e)))
                return banks[k % BANKS]

            def three(dst, x_hi, x_lo, b, k, start, stop):
                pairs = ((x_hi, w_hi[:, b, k]), (x_hi, w_lo[:, b, k]), (x_lo, w_hi[:, b, k]))
                for n, (a, w) in enumerate(pairs):
                    ins = M(dst, a, w, start=start and n == 0, stop=stop and n == 2, skip_group_check=True)
                return ins

            def half(q):
                pe.wait_ge(s.lo_ready, item * (2 * EP) + (2 * RING + q + 1))

            pe.wait_ge(s.sel_ready, item + 1)
            b = item_bank("csT")
            for t in range(T):
                ins = TR(b[:, t * P:(t + 1) * P], csel[:, t, :], ident)
            done(ins)
            for u in range(2):
                b = item_bank(f"gx{u}")
                for i in range(4):
                    for t in range(T):
                        ins = M(b[:, i * P:(i + 1) * P], hn[:, t, 4 * u + i:D:KD], sel[:, t, :], start=t == 0,
                                stop=t == T - 1)
                done(ins)
            item_read_out("gx1")
            for j in range(8):
                if j < 7:
                    for g, name in enumerate(("eg", "eu")):
                        b = item_bank(f"{name}{j}")
                        for r in range(2):
                            q = 4 * j + 2 * g + r
                            half(q)
                            for c in range(4):
                                x = 4 * r + c
                                ins = three(b[:], xg_hi[:, x, :], xg_lo[:, x, :], q % PARTS,
                                            slice(512 * c, 512 * c + 512), x == 0, x == KD - 1)
                            if r == 0:
                                ins.then_inc(s.half_used, 1)
                        done(ins)
                if j:
                    item_read_out(f"eu{j - 1}")
                    b = item_bank(f"eT{j - 1}")
                    for c in range(4):
                        ins = TR(b[:, c * P:(c + 1) * P], ehm[:, (j - 1) % 2, c:512:4], ident)
                    done(ins)
            b0, b1 = item_bank("ed0"), item_bank("ed1")
            for j in range(7):
                item_read_out(f"eT{j}")
                for r in range(2):
                    q = 28 + 2 * j + r
                    half(q)
                    for u, b in enumerate((b0, b1)):
                        for c in range(2):
                            x = 4 * j + 2 * r + c
                            ins = three(b[:], ehT_hi[:, x, :], ehT_lo[:, x, :], q % PARTS,
                                        slice(D * c + 512 * u, D * c + 512 * u + 512), x == 0, x == 27)
                        if x == 27:
                            done(ins)
                    if x < 27:
                        ins.then_inc(s.half_used, 1)
            item_read_out("csT")
            for u in range(2):
                item_read_out(f"ed{u}")
                for t in range(T):
                    done(M(item_bank(f"sc{u}{t}")[:], cselT[:, t * P:(t + 1) * P], ey[:, 512 * u:512 * u + 512],
                           start=True, stop=True))

    @block.vector
    def _(dve):
        own = Own(dve, "vec", s.vec_step, s.freed_vec)
        V = nc.vector
        step, settle, free = own.step, own.settle, own.free

        def tt(out_, a, b, op):
            return V.tensor_tensor(out_, a, b, op)

        def normalise(m, dst):
            dve.wait_ge(s.sumsq_ready, T * (m + 1))
            step(V.tensor_scalar(stat[:, 0, 0:T], stat[:, 0, 0:T], 1.0 / D, EPS, ALU.mult, ALU.add), s.var_ready)
            dve.wait_ge(s.root_ready, m + 1)
            step(V.reciprocal(stat[:, 0, 0:T], stat[:, 0, 0:T]))
            settle()
            for t in range(T):
                step(V.tensor_scalar(dst[:, t, :], h[:, t, :], stat[:, 0, t:t + 1], None, ALU.mult), s.hn_ready)

        def group_stats(y, groups, width, eps, m):
            mean, var = stat[:, 3, 0:groups], stat[:, 4, 0:groups]
            v = y.rearrange("p t (g e) -> p (t g) e", e=width)
            sq = tmp[:].rearrange("p t (g e) -> p (t g) e", e=width)
            step(V.reduce_sum(mean, v, AX.X))
            settle()
            step(V.tensor_scalar(mean, mean, 1.0 / width, None, ALU.mult))
            settle()
            step(tt(v, v, wide(mean, width), ALU.subtract))
            settle()
            step(tt(sq, v, v, ALU.mult))
            settle()
            step(V.reduce_sum(var, sq, AX.X))
            settle()
            step(V.tensor_scalar(var, var, 1.0 / width, eps, ALU.mult, ALU.add), s.gn_var_ready)
            dve.wait_ge(s.gn_root_ready, m + 1)
            step(V.reciprocal(var, var))
            settle()
            step(tt(v, v, wide(var, width), ALU.mult))
            settle()

        for l in range(DEPTH):
            normalise(2 * l, hn)
            if l == 0:
                dve.wait_ge(s.const_loaded, 16)
                dve.wait_ge(s.pos_loaded, 16 * T)
                step(V.tensor_copy(pos_f[:], pos_i[:]))
                settle()
                for t in range(T):
                    step(V.tensor_scalar(sinT[:, t, :], C("inv_freq"), pos_f[:, t:t + 1], None, ALU.mult))
                settle()
                step(V.tensor_scalar(cosT[:], sinT[:], 1.0 / (2 * np.pi), ROUND, ALU.mult, ALU.add))
                settle()
                step(V.tensor_scalar(cosT[:], cosT[:], -ROUND, None, ALU.add))
                settle()
                for part in TWO_PI:
                    step(V.scalar_tensor_tensor(out=sinT[:], in0=cosT[:], scalar=-part, in1=sinT[:], op0=ALU.mult,
                                                op1=ALU.add))
                    settle()
                half_pi, pi = float(np.float32(np.pi / 2)), 3.1415925
                turn = gg[:, :, 0:80]
                step(V.tensor_scalar(turn, sinT[:], half_pi, -2 * np.pi, ALU.is_gt, ALU.mult))
                settle()
                step(V.scalar_tensor_tensor(out=cosT[:], in0=sinT[:], scalar=half_pi, in1=turn, op0=ALU.add, op1=ALU.add))
                settle()
                step(V.tensor_scalar(cosT[:], cosT[:], -pi, pi, ALU.max, ALU.min))
                step(V.tensor_scalar(sinT[:], sinT[:], -pi, pi, ALU.max, ALU.min), s.angles_ready)
            dve.wait_ge(s.vec_loaded, 16 * 7 * (l + 1))
            dve.wait_ge(s.shift_loaded, 32 * (l + 1))
            for a, b_ in ((1536, RWCOLS), (0, 1536)):
                step(tt(prev[:, :, a:b_], prev[:, :, a:b_], pr[:, :, a:b_], ALU.subtract))
                settle()
                step(tt(prev[:, :, a:b_], prev[:, :, a:b_], each(VEC("mu", a, b_)), ALU.mult))
                settle()
                step(tt(pr[:, :, a:b_], pr[:, :, a:b_], prev[:, :, a:b_], ALU.add),
                     s.xs_ready if a else None)
            settle()
            r, k, v = (pr[:, :, 512 * i:512 * i + 512] for i in range(3))
            step(tt(kk[:], k, each(VEC("k_k")), ALU.mult))
            settle()
            step(tt(tmp[:], kk[:], kk[:], ALU.mult))
            settle()
            step(V.reduce_sum(stat[:, 1, :], tmp[:].rearrange("p t (g e) -> p (t g) e", e=HD), AX.X))
            settle()
            step(V.tensor_scalar(stat[:, 1, :], stat[:, 1, :], 1e-12, None, ALU.add))
            dve.wait_ge(s.qa_sumsq, 4 * (l + 1))
            lat = stat[:, 2, 0:4].rearrange("p (t q) -> p t q", t=T)
            step(V.tensor_scalar(lat[:, :, 0], lat[:, :, 0], 1.0 / 256, EPS, ALU.mult, ALU.add))
            step(V.tensor_scalar(lat[:, :, 1], lat[:, :, 1], 1.0 / 128, EPS, ALU.mult, ALU.add), s.knsq_ready)
            for t in range(T):
                b = product(dve, f"z{t}.{l}")
                free(tt(ld[:, t, :], b[:], VEC("w0"), ALU.add), f"z{t}.{l}")
                b = product(dve, f"a{t}.{l}")
                free(tt(ab[:, t, :], b[:], VEC("a0"), ALU.add), f"a{t}.{l}")
            dve.wait_ge(s.knroot_ready, l + 1)
            step(V.reciprocal(stat[:, 1, :], stat[:, 1, :]))
            step(V.reciprocal(stat[:, 2, 0:4], stat[:, 2, 0:4]))
            settle()
            kg = kk[:].rearrange("p t (g e) -> p (t g) e", e=HD)
            step(tt(kg, kg, wide(stat[:, 1, :], HD), ALU.mult))
            for t in range(T):
                step(V.tensor_scalar(qa[:, t, 0:256], qa[:, t, 0:256], stat[:, 2, 2 * t:2 * t + 1], None, ALU.mult))
                step(V.tensor_scalar(qa[:, t, 256:384], qa[:, t, 256:384], stat[:, 2, 2 * t + 1:2 * t + 2], None,
                                     ALU.mult), s.qa_ready if t else None)
            settle()
            dve.wait_ge(s.decay_sig_ready, l + 1)
            step(V.tensor_scalar(ld[:], ld[:], -DECAY, None, ALU.mult), s.logd_ready)
            dve.wait_ge(s.rate_sig_ready, l + 1)
            step(V.scalar_tensor_tensor(out=tmp[:], in0=ab[:], scalar=-1.0, in1=each(VEC("k_a")), op0=ALU.add,
                                        op1=ALU.mult))
            step(tt(ab[:], ab[:], kk[:], ALU.mult))
            settle()
            step(V.scalar_tensor_tensor(out=k, in0=tmp[:], scalar=1.0, in1=k, op0=ALU.add, op1=ALU.mult))
            settle()
            step(tt(tmp[:], r, k, ALU.mult))
            settle()
            step(tt(tmp[:], tmp[:], each(VEC("r_k")), ALU.mult))
            settle()
            step(V.reduce_sum(stat[:, 5, :], tmp[:].rearrange("p t (g e) -> p (t g) e", e=HD), AX.X))
            for i in range(RH):
                b = product(dve, f"sR{i}.{l}")
                step(tt(sR[:, i, 0:256], b[:, 0:256], C("ret_mask", 256 * i, 256 * i + 256), ALU.mult))
                free(tt(sR[:, i, 256:384], b[:, 256:384], C("ret_mask", 256 * i, 256 * i + 128), ALU.mult),
                     f"sR{i}.{l}")
            dve.wait_ge(s.product_ready, JOB_AT[f"pc.{l}"] + 1)
            for t in range(T):
                b = banks[JOB_AT[f"cum{t}.{l}"] % BANKS]
                dve.wait_ge(s.exps_ready, T * l + t + 1)
                step(tt(ld[:, t, :], b[:], ld[:, t, :], ALU.subtract), s.cex_ready)
            read_out(dve, f"cum1.{l}")
            step(tt(kk[:], kk[:], ld[:], ALU.mult))
            step(tt(r, r, ec[:], ALU.mult))
            step(tt(ab[:], ab[:], enc[:], ALU.mult))
            step(tt(k, k, enc[:], ALU.mult), s.scan_in_ready)
            read_out(dve, f"oR1.{l}")
            group_stats(y_ret[:], 8, P, 1e-5, 2 * l)
            dve.wait_ge(s.silu_g_ready, l + 1)
            step(tt(y_ret[:], y_ret[:], raw[:, 3, :, :], ALU.mult), s.ret_done)
            for i in range(NH + 2):
                if i < NH:
                    b = product(dve, f"sM{i}.{l}")
                    if i > 1:
                        dve.wait_ge(s.product_ready, JOB_AT[f"pT{i - 2}.{l}"] + 1)
                    sc = float(QK) ** -0.5
                    m = sm[:, i % 2, :]
                    step(V.scalar_tensor_tensor(out=m[:, 0:128], in0=b[:, 0:128], scalar=sc, in1=C("mla_mask"),
                                                op0=ALU.mult, op1=ALU.add))
                    step(V.tensor_scalar(m[:, 128:256], b[:, 128:256], sc, None, ALU.mult))
                    free(V.scalar_tensor_tensor(out=m[:, 256:384], in0=b[:, 256:384], scalar=sc, in1=C("mla_mask"),
                                                op0=ALU.mult, op1=ALU.add), f"sM{i}.{l}")
                    settle()
                    step(V.reduce_max(smax[:, i, 0:1], m[:, 0:128], AX.X))
                    step(V.reduce_max(smax[:, i, 1:2], m[:, 128:384], AX.X))
                    settle()
                    step(V.tensor_scalar(smax[:, i, :], smax[:, i, :], -1.0, None, ALU.mult), s.masked_ready)
                if i > 1:
                    j = i - 2
                    dve.wait_ge(s.prob_ready, NH * l + j + 1)
                    step(V.reciprocal(den[:, j, :], den[:, j, :]))
                    b = product(dve, f"oM{j}.{l}")
                    settle()
                    free(tt(y_mla[:, :, 64 * j:64 * j + 64], b[:, 0:128].rearrange("p (t e) -> p t e", t=T),
                            wide(den[:, j, :], HD), ALU.mult), f"oM{j}.{l}")
            for t in range(T):
                for i in range(NH):
                    b = product(dve, f"M{t}{i}.{l}")
                    free(tt(m1[:, i, :], b[:], C("pair_mask"), ALU.mult), f"M{t}{i}.{l}")
                for g in range(2):
                    four = slice(4 * g, 4 * g + 4)
                    b = product(dve, f"A{t}{g}.{l}")
                    quad = b[:].rearrange("p (i n) -> p i n", i=4)
                    free(tt(am[:, four, :], quad, each(C("a_mask"), 4), ALU.mult), f"A{t}{g}.{l}")
                    settle()
                    step(tt(xt[:, four, :], m1[:, four, 0:128], each(C("level0_t"), 4), ALU.mult))
                    settle()
                    step(tt(xi[:, four, :], am[:, four, :], each(C("levels", 0, P), 4), ALU.mult))
                    step(tt(xt[:, four, :], xt[:, four, :], each(C("ident"), 4), ALU.add))
                    settle()
                    step(tt(xi[:, four, :], xi[:, four, :], each(C("ident"), 4), ALU.add), s.x_ready)
                for lv in range(1, LEVELS):
                    for g in range(2):
                        four = slice(4 * g, 4 * g + 4)
                        b = product(dve, f"T{t}{lv}{g}.{l}")
                        free(tt(t1[:, four, :], b[:].rearrange("p (i n) -> p i n", i=4),
                                each(C("levels", lv * P, lv * P + P), 4), ALU.mult), f"T{t}{lv}{g}.{l}")
                    for g in range(2):
                        four = slice(4 * g, 4 * g + 4)
                        for x_, name in ((xi, "X"), (xt, "XT")):
                            if name == "X" and lv == LEVELS - 1:
                                continue
                            b = product(dve, f"{name}{t}{lv}{g}.{l}")
                            free(tt(x_[:, four, :], b[:].rearrange("p (i n) -> p i n", i=4), x_[:, four, :],
                                    ALU.add), f"{name}{t}{lv}{g}.{l}")
                for n in (2 * t, 2 * t + 1):
                    o = slice(64 * (n % 2), 64 * (n % 2) + 64)
                    if n == 2 * t:
                        read_out(dve, f"U{t}.{l}")
                    if n:
                        for e in range(2):
                            b = product(dve, f"dU{n}{e}.{l}")
                            u_ = uu[o, t, :].rearrange("p (a b d) -> p a b d", a=4, b=2)[:, :, e, :]
                            free(tt(u_, b[o, 0:256].rearrange("p (a d) -> p a d", a=4), u_, ALU.add),
                                 f"dU{n}{e}.{l}")
                    if n < 3:
                        b = product(dve, f"S{n + 1}.{l}")
                        sn = b[:, 0:256].rearrange("p (a d) -> p a d", a=4)
                        dec = wide(decay_end[:, t, :, n % 2], HD)
                        if n == 0:
                            free(V.tensor_copy(st[:, 0, :, :], sn), f"S{n + 1}.{l}")
                        else:
                            free(tt(st[:, n, :, :], sn, st[:, n - 1, :, :], ALU.add), f"S{n + 1}.{l}")
                        settle()
                        step(tt(st[:, n, :, :], st[:, n, :, :], dec, ALU.mult), s.state_ready)
            read_out(dve, f"Y11.{l}")
            group_stats(y_rwkv[:], 16, HD, 64e-5, 2 * l + 1)
            step(tt(y_rwkv[:], y_rwkv[:], each(VEC("lnx")), ALU.mult))
            step(tt(tmp[:].rearrange("p t (g e) -> p t g e", e=HD), v.rearrange("p t (g e) -> p t g e", e=HD),
                    wide(stat[:, 5, :].rearrange("p (t g) -> p t g", t=T), HD), ALU.mult))
            settle()
            step(tt(y_rwkv[:], y_rwkv[:], tmp[:], ALU.add))
            settle()
            step(tt(y_rwkv[:], y_rwkv[:], gg[:], ALU.mult), s.rwkv_done)
            for n in BRANCHES:
                for u in range(2):
                    for t in range(T):
                        b = product(dve, f"br{n}{u}{t}.{l}")
                        read_out(dve, f"gt11.{l}")
                        m = merged[:, t, 512 * u:512 * u + 512]
                        gate = sigs[n][:, u, t, :]
                        if n == 0:
                            free(tt(m, b[:], gate, ALU.mult), f"br{n}{u}{t}.{l}")
                        else:
                            free(tt(gate, b[:], gate, ALU.mult), f"br{n}{u}{t}.{l}")
                            settle()
                            step(tt(m, m, gate, ALU.add), s.merged_done if n == BRANCHES[-1] else None)
            for u in range(2):
                for t in range(T):
                    b = product(dve, f"o{u}{t}.{l}")
                    hs = h[:, t, 512 * u:512 * u + 512]
                    free(tt(hs, b[:], hs, ALU.add), f"o{u}{t}.{l}")
            normalise(2 * l + 1, hn)
            if l == 0:
                for q in range(4):
                    b = product(dve, f"fT{q}.0")
                    dve.wait_ge(s.f_x_hi_ready, q + 1)
                    for i in range(2):
                        c = 2 * q + i
                        ins = V.scalar_tensor_tensor(out=fx_lo[:, c, :], in0=b[:, 256 * i:256 * i + 256],
                                                     scalar=gains[:, 0, 1, c:c + 1],
                                                     in1=fx_hi[:, c, :].bitcast(F32), op0=ALU.mult,
                                                     op1=ALU.subtract)
                        step(ins) if i == 0 else free(ins, f"fT{q}.0")
                for q in range(36):
                    src, width = ffn_half(q)
                    dve.wait_ge(s.f_hi_ready, q + 1)
                    step(tt(f_lo[:, q % 2, 0:width], src, f_hi[:, q % 2, 0:width].bitcast(F32), ALU.subtract),
                         s.f_lo_ready)
                    if q % 4 == 1 and 5 <= q <= 25:
                        j = (q - 5) // 4
                        w_ = FFN_COLS[j]
                        for t in range(T):
                            b = product(dve, f"fu{j}{t}.0")
                            read_out(dve, f"fg{j}{t}.0")
                            free(tt(hm[:, j % 2, t, 0:w_], b[:, 0:w_], sg[:, j % 2, t, 0:w_], ALU.mult),
                                 f"fu{j}{t}.0")
                    if q % 4 == 2 and 10 <= q <= 30:
                        j = (q - 10) // 4
                        k = FFN_COLS[j] // P
                        for t in range(T):
                            b = product(dve, f"hT{j}{t}.0")
                            dve.wait_ge(s.f_x_hi_ready, 4 + T * j + t + 1)
                            tok = slice(t * P, (t + 1) * P)
                            free(tt(hmT_lo[:, 4 * j:4 * j + k, tok],
                                    b[:, 0:k * P].rearrange("p (c n) -> p c n", c=k),
                                    hmT_hi[:, 4 * j:4 * j + k, tok].bitcast(F32), ALU.subtract), f"hT{j}{t}.0")
                for u in range(2):
                    for t in range(T):
                        b = product(dve, f"fd{u}{t}.0")
                        hs = h[:, t, 512 * u:512 * u + 512]
                        free(tt(hs, b[:], hs, ALU.add), f"fd{u}{t}.0")
        R = lambda i: rt[:, i, :, :]
        few = each(C("experts"), T)
        b = product(dve, "router.1")
        free(V.tensor_copy(R(0), b[:, 0:T * NE].rearrange("p (t e) -> p t e", t=T)), "router.1")
        step(V.tensor_scalar(R(1), few, -99.0, None, ALU.add))
        settle()
        top = stat[:, 7, :].rearrange("p (a t) -> p a t", t=T)
        for i in range(2):
            step(V.reduce_max(top[:, i, :], R(0), AX.X))
            settle()
            step(tt(R(4), R(0), wide(top[:, i, :], NE), ALU.is_equal))
            settle()
            step(tt(R(4), R(4), R(1), ALU.mult))
            settle()
            step(V.tensor_reduce(top[:, 2, :], R(4), AX.X, ALU.min))
            settle()
            step(tt(R(2 + i), R(1), wide(top[:, 2, :], NE), ALU.is_equal))
            settle()
            if i == 0:
                step(V.scalar_tensor_tensor(out=R(0), in0=R(2), scalar=-3e38, in1=R(0), op0=ALU.mult, op1=ALU.add))
                settle()
        step(tt(stat[:, 6, 0:2], top[:, 1, :], top[:, 0, :], ALU.subtract), s.route_diff)
        step(tt(R(8), R(2), R(3), ALU.add), s.mask_ready)
        dve.wait_ge(s.route_exp, 1)
        step(V.tensor_scalar(stat[:, 6, 2:4], stat[:, 6, 0:2], 1.0, None, ALU.add))
        settle()
        step(V.reciprocal(stat[:, 6, 2:4], stat[:, 6, 2:4]))
        settle()
        step(tt(stat[:, 6, 0:2], stat[:, 6, 0:2], stat[:, 6, 2:4], ALU.mult))
        settle()
        step(tt(R(2), R(2), wide(stat[:, 6, 2:4], NE), ALU.mult))
        step(tt(R(3), R(3), wide(stat[:, 6, 0:2], NE), ALU.mult))
        settle()
        for i in range(2):
            step(tt(comb[:, i, :, :], R(2), R(3), ALU.add))
        b = product(dve, "rank.1")
        step(tt(R(5), b[:, 0:T * NE].rearrange("p (t e) -> p t e", t=T), R(8), ALU.mult))
        settle()
        for i in range(2):
            step(V.tensor_scalar(spos[:, i, :, :], R(5), -1.0 - P * i, None, ALU.add))
        f = it_f[0:1, :]
        free(V.tensor_scalar(f[:, 0:8], b[0:1, 16:24], P + 0.5, None, ALU.is_gt), "rank.1")
        step(V.tensor_scalar(f[:, 8:16], C("experts")[0:1, :], -1.0, 8.0, ALU.mult, ALU.add))
        settle()
        step(tt(f[:, 8:16], f[:, 8:16], f[:, 0:8], ALU.mult))
        step(V.reduce_sum(f[:, 56:57], f[:, 0:8], AX.X))
        settle()
        step(V.max(f[:, 16:24], f[:, 8:16]))
        settle()
        step(V.tensor_scalar(f[:, 40:44], f[:, 16:20], -1.0, 24.0, ALU.mult, ALU.add))
        step(V.tensor_copy(f[:, 32:40], C("experts")[0:1, :]))
        step(V.tensor_copy(f[:, 44:52], C("experts")[0:1, :]))
        step(V.tensor_scalar(f[:, 52:56], f[:, 16:20], -1.0, 8.0, ALU.mult, ALU.add))
        step(V.tensor_scalar(f[:, 56:57], f[:, 56:57], float(NE), None, ALU.add))
        settle()
        step(V.tensor_scalar(f[:, 52:56], f[:, 52:56], float(NE - 1), None, ALU.min))
        step(V.tensor_scalar(f[:, 40:44], f[:, 40:44], float(2 * NE * T // 2 + NE - 1), None, ALU.min))
        settle()
        step(V.tensor_copy(items[0:1, 0:25], f[:, 32:57]), s.items_ready)
        settle()
        V.tensor_copy(smax[:, 1, :], smax[:, 0, :]).then_inc(s.lo_ready, 2 * RING)
        V.tensor_copy(smax[:, 2, :], smax[:, 0, :]).then_inc(s.half_used, HALVES)
        n_items = dve.value_load(items[0:1, 24:25], min_val=SURE, max_val=SURE + 3)
        with dve.Fori(0, n_items) as item:
            at_ = dve.value_load(items[0:1, bass.ds(item, 1)], min_val=0, max_val=NE * T + NE - 1)

            def item_product(job):
                dve.wait_ge(s.product_ready, item * len(ITEM) + (len(JOBS) + ITEM_AT[job] + 1))
                return banks[ITEM_AT[job] % BANKS]

            for t in range(T):
                sp_ = spos[:].rearrange("p i t e -> p (i t e)")[:, bass.ds(at_ + NE * t, 1)]
                cb_ = comb[:].rearrange("p i t e -> p (i t e)")[:, bass.ds(at_ + NE * t, 1)]
                V.tensor_scalar(sel[:, t, :], C("slots"), sp_, None, ALU.is_equal)
                ins = V.tensor_scalar(csel[:, t, :], C("slots"), sp_, cb_, ALU.is_equal, ALU.mult)
            ins.then_inc(s.sel_ready, 1)
            def lo(q):
                dve.wait_ge(s.hi_ready, item * (2 * EP) + (q + 1))
                i, o = (NPAN + q // 2) % RING, HALF * (q % 2)
                tt(w_lo[:, q % PARTS, :], ring[:, i, o:o + HALF], w_hi[:, q % PARTS, :].bitcast(F32),
                   ALU.subtract).then_inc(s.lo_ready, 1)

            for q in range(2 * EP):
                lo(q)
                if q == 2:
                    for u in range(2):
                        b = item_product(f"gx{u}")
                        dve.wait_ge(s.x_hi_ready, item * 9 + (u + 1))
                        for i in range(4):
                            c = 4 * u + i
                            ins = V.scalar_tensor_tensor(out=xg_lo[:, c, :], in0=b[:, i * P:(i + 1) * P],
                                                         scalar=gains[:, 1, 1, c:c + 1],
                                                         in1=xg_hi[:, c, :].bitcast(F32), op0=ALU.mult,
                                                         op1=ALU.subtract)
                        ins.then_inc(s.freed_vec, 1)
                if q % 4 == 1 and 5 <= q <= 29:
                    j = (q - 5) // 4
                    b = item_product(f"eu{j}")
                    k = ITEM_AT[f"eg{j}"]
                    dve.wait_ge(s.freed_act, item * IF["act"] + (FR["act"] + item_freed(k, "act")))
                    tt(ehm[:, j % 2, :], b[:], esg[:, j % 2, :], ALU.mult).then_inc(s.freed_vec, 1)
                if q % 4 == 2 and 10 <= q <= 34:
                    j = (q - 10) // 4
                    b = item_product(f"eT{j}")
                    dve.wait_ge(s.x_hi_ready, item * 9 + (j + 3))
                    tt(ehT_lo[:, 4 * j:4 * j + 4, :], b[:].rearrange("p (c n) -> p c n", c=4),
                       ehT_hi[:, 4 * j:4 * j + 4, :].bitcast(F32), ALU.subtract).then_inc(s.freed_vec, 1)
            for u in range(2):
                V.tensor_copy(ey[:, 512 * u:512 * u + 512], item_product(f"ed{u}")[:]).then_inc(s.freed_vec, 1)
            for u in range(2):
                for t in range(T):
                    hs = h[:, t, 512 * u:512 * u + 512]
                    tt(hs, item_product(f"sc{u}{t}")[:], hs, ALU.add).then_inc(s.freed_vec, 1)
            V.tensor_copy(smax[:, 0, :], smax[:, 0, :]).then_inc(s.item_step, 1)
            dve.wait_ge(s.item_step, item + 1)
        V.tensor_copy(smax[:, 0, :], smax[:, 0, :]).then_inc(s.items_done, 1)
        normalise(4, fin)
        dve.wait_ge(s.fgain_loaded, 16)
        for t in range(T):
            settle()
            own.step(tt(fin[:, t, :], fin[:, t, :], fgain[:], ALU.mult), s.fin_ready)

    blk.__exit__(None, None, None)


_INS = ["x", "positions", "attn_norm", "w_in", "rwkv_mu", "rwkv_w0", "rwkv_w2", "rwkv_a0", "rwkv_a2", "rwkv_g2",
        "rwkv_k_k", "rwkv_k_a", "rwkv_r_k", "rwkv_lnx_w", "mla_q_norm", "mla_w_qb", "mla_kv_norm", "mla_w_kvb",
        "w_branch", "w_o", "ffn_norm", "ffn_w_gate", "ffn_w_up", "ffn_w_down", "moe_router", "moe_w_gate",
        "moe_w_up", "moe_w_down", "final_norm"]


def kernel(**inputs):
    import concourse.bacc as bacc
    from concourse.bass_utils import run_bass_kernel_spmd

    nc = bacc.Bacc("TRN2", target_bir_lowering=False, num_devices=1)
    arrays, args = {}, []
    for name in _INS:
        a = np.ascontiguousarray(inputs[name])
        arrays[f"{name}_dram"] = a
        args.append(nc.dram_tensor(f"{name}_dram", a.shape, mybir.dt.from_np(a.dtype), kind="ExternalInput").ap())
    arrays["const_dram"] = CONST
    args.append(nc.dram_tensor("const_dram", CONST.shape, F32, kind="ExternalInput").ap())
    args.append(nc.dram_tensor("out_dram", (1, SEQ, D), F32, kind="ExternalOutput").ap())
    build(nc, *args)
    r = run_bass_kernel_spmd(nc, [arrays], core_ids=[0])
    return r.results[0]["out_dram"]
```

```python
import numpy as np
import concourse.bass as bass
from concourse import mybir

F32 = mybir.dt.float32
I32 = mybir.dt.int32
ALU = mybir.AluOpType
ACT = mybir.ActivationFunctionType
AX = mybir.AxisListType

P = 128
SEQ, D, DEPTH, CHUNK = 256, 1024, 2, 64
T = SEQ // P
KD = D // P
RH, RW = 4, 512
NH, HD, W = 8, 64, 512
LORA = 288
RWCOLS = 3 * W + LORA
NOPE, ROPE, QK = 64, 32, 96
MLAC = 256 + 160
DFF, NE, FE = 2816, 8, 3584
DECAY = float(np.exp(-0.5))
EPS = 1e-6
RING = 3
BANKS = 8
SLOT = 4096
F32R = mybir.dt.float32r
HALF = SLOT // 2
PARTS = 3

C_RET, C_RWKV, C_MLA, C_GATE = 0, 2048, 2048 + RWCOLS, 2048 + RWCOLS + MLAC


def constants():
    i = np.arange(P)
    same = (i[:, None] // CHUNK) == (i[None, :] // CHUNK)
    s, t = i[:, None], i[None, :]
    c = {"ident": np.eye(P)}
    c["ones"] = np.ones((P, P))
    c["upto"] = (s <= t)
    c["chunk_upto"] = (s <= t) & same
    c["chunk_sel"] = np.stack([i < CHUNK, i >= CHUNK], 1)
    strict = (s < t) & same
    incl = (s <= t) & same
    c["pair_mask"] = np.concatenate([-1.0 * strict, incl, -1.0 * strict, incl], 1)
    c["a_mask"] = -1.0 * ((s > t) & same)
    b = 1
    lv = []
    while b < CHUNK:
        lv.append((s // (2 * b) == t // (2 * b)) & ((s // b) % 2 == 1) & ((t // b) % 2 == 0))
        b *= 2
    c["levels"] = np.concatenate([x.astype(np.float64) for x in lv], 1)
    c["level0_t"] = lv[0].T
    g = np.arange(SEQ)
    lg = np.log(1.0 - 2.0 ** (-5.0 - np.arange(RH)))
    ret = []
    for h in range(RH):
        m = np.exp(lg[h] * np.abs(g[None, :] - i[:, None])) * 128 ** -0.5
        ret.append(m * (i[:, None] // CHUNK <= g[None, :] // CHUNK))
    c["ret_mask"] = np.concatenate(ret, 1)
    c["mla_mask"] = np.where(i[None, :] // CHUNK <= i[:, None] // CHUNK, 0.0, -1e30)
    c["slots"] = np.tile(np.arange(P, dtype=np.float64), (P, 1))
    f32 = np.float32
    inv = [f32(1.0) / (f32(10000.0) ** (np.arange(0, d, 2, dtype=f32) / f32(d))) for d in (128, ROPE)]
    c["inv_freq"] = np.tile(np.concatenate(inv), (P, 1))
    c["experts"] = np.tile(np.arange(NE, dtype=np.float64), (P, 1))
    out, at = {}, 0
    for k, v in c.items():
        v = v.astype(np.float32)
        out[k] = (at, v.shape[1])
        at += v.shape[1]
    return out, np.ascontiguousarray(np.concatenate([v.astype(np.float32) for v in c.values()], 1))


CONST_AT, CONST = constants()
LEVELS = 6
VECTORS = ["mu", "w0", "a0", "k_k", "k_a", "r_k", "lnx"]
VEC_AT = {"mu": (0, RWCOLS)}
for _n, _v in enumerate(VECTORS[1:]):
    VEC_AT[_v] = (RWCOLS + _n * W, W)
VEC_COLS = RWCOLS + 6 * W

TWO_PI = [6.28125]
_left = 2 * np.pi - TWO_PI[0]
_c2 = float(np.round(_left * 2 ** 20) / 2 ** 20)
TWO_PI += [_c2, float(np.float32(_left - _c2))]
ROUND = 1.5 * 2 ** 23


BRANCHES = (0, 2, 1)


def panels():
    out = []
    for l in range(DEPTH):
        out += [("in", l, j, 1) for j in range(9)]
        out += [("lora", l, 0, 4), ("mla", l, 0, 2)]
        out += [("gate", l, j, 1) for j in range(3)] + [("branch", l, 0, 1)]
        out += [("gate", l, j, 1) for j in range(3, 6)] + [("branch", l, n, 1) for n in BRANCHES[1:]]
        out += [("o", l, 0, 1), ("o", l, 1, 1)]
        if l == 0:
            for j in range(6):
                out += [("ffn_gate", 0, j, 1), ("ffn_up", 0, j, 1)]
            out += [("ffn_down", 0, j, 1) for j in range(6)]
    return out


IN_PANELS = [(C_RWKV + 1536, LORA), (C_RWKV, 512), (C_RWKV + 512, 512), (C_RWKV + 1024, 512),
             (0, 512), (512, 512), (1024, 512), (1536, 512), (C_MLA, MLAC)]
FFN_COLS = [512] * 5 + [256]


GATED = (2, 4)


def layer_jobs(l):
    A, V = "act", "vec"
    out = [(f"nT{q}", A) for q in range(4)]
    out += [(f"in{j}_{t}", A) for j in range(8) for t in range(T)]
    out += [(f"loT{t}", A) for t in range(T)] + [(f"in8_{t}", A) for t in range(T)]
    out += [(f"{n}{t}", e) for t in range(T) for n, e in (("z", V), ("a", V), ("g", A))]
    out += [(f"rT{s}{t}", A) for t in range(T) for s in range(2)]
    out += [(f"sR{h}", V) for h in range(RH)]
    out += [(f"cT{t}", A) for t in range(T)]
    out += [(f"mq{t}{u}", A) for t in range(T) for u in range(2)]
    out += [(f"mk{t}{u}", A) for t in range(T) for u in range(2)]
    out += [(f"cum{t}", A) for t in range(T)] + [("pc", A)]
    out += [(f"oR{t}", A) for t in range(T)]
    out += [("gt0", A)] + [(f"mT0{u}", A) for u in range(4)] + [("gt1", A)] + [(f"mT1{u}", A) for u in range(4)]
    for i in range(NH + 2):
        out += [(f"sM{i}", V)] * (i < NH) + [(f"pT{i - 1}", A)] * (0 < i <= NH) + [(f"oM{i - 2}", V)] * (i > 1)
        out += [(f"gt{2 + i // 2}", A)] * (i % 2 and i < NH)
    for t in range(T):
        out += [(f"kT{t}{hp}", A) for hp in range(4)]
        out += [(f"M{t}{i}", V) for i in range(NH)] + [(f"A{t}{g}", V) for g in range(2)]
        out += [("br011", V)] if t else [("yT00", A), ("yT01", A), ("br000", V)]
        for lv in range(1, LEVELS):
            out += [(f"T{t}{lv}{g}", V) for g in range(2)]
            for g in range(2):
                out += [(f"X{t}{lv}{g}", V)] * (lv < LEVELS - 1) + [(f"XT{t}{lv}{g}", V)]
            out += [(f"gt{6 + 3 * t + GATED.index(lv)}", A)] if lv in GATED else []
        out += [(f"W{t}", A), (f"Z{t}", A), (f"U{t}", A)]
        for n in (2 * t, 2 * t + 1):
            out += [(f"dU{n}{e}", V) for e in range(2)] * (n > 0) + [("br010", V)] * (n == 1)
            out += [(f"gt{8 + 3 * t}", A)] * (n == 2 * t)
            out += [(f"S{n + 1}", V)] * (n < 3) + [("br001", V)] * (n == 0)
        out += [(f"Y{t}{e}", A) for e in range(2)]
    for n in BRANCHES[1:]:
        out += [(f"yT{n}{u}", A) for u in range(2)]
        out += [(f"br{n}{u}{t}", V) for u in range(2) for t in range(T)]
    out += [(f"gT{q}", A) for q in range(4)]
    out += [(f"o{u}{t}", V) for u in range(2) for t in range(T)]
    out += [(f"fT{q}", A if l else V) for q in range(4)]
    if l == 0:
        for j in range(7):
            if j < 6:
                out += [(f"fg{j}{t}", A) for t in range(T)] + [(f"fu{j}{t}", V) for t in range(T)]
            if j > 0:
                out += [(f"hT{j - 1}{t}", V) for t in range(T)]
        out += [(f"fd{u}{t}", V) for u in range(2) for t in range(T)]
    else:
        out += [("router", V), ("rank", V)]
    return [(f"{n}.{l}", e) for n, e in out]


def moe_jobs():
    A, V = "act", "vec"
    out = [("eg0", A)] + [(f"sc{u}{t}", V) for u in range(2) for t in range(T)] + [("csT", A), ("eu0", V)]
    for j in range(1, 7):
        out += [(f"eg{j}", A), (f"eu{j}", V), (f"eT{j - 1}", V)]
    out += [("eT6", V), ("gx0", V), ("gx1", V), ("ed0", V), ("ed1", V)]
    return out


JOBS = layer_jobs(0) + layer_jobs(1)
JOB_AT = {n: i for i, (n, _) in enumerate(JOBS)}
ITEM = moe_jobs()
ITEM_AT = {n: i for i, (n, _) in enumerate(ITEM)}
PANELS = panels()
AHEAD = 4
EP = 21
HALVES = 14 + 13
SURE = NE


def freed_count(k, eng):
    return sum(e == eng for _, e in JOBS[:k + 1])


def item_freed(k, eng):
    return sum(e == eng for _, e in ITEM[:k + 1])


class Own:

    def __init__(self, eng, name, step_sem, freed_sem):
        self.eng, self.name, self.step_sem, self.freed_sem = eng, name, step_sem, freed_sem
        self.count, self.last = {}, None

    def step(self, ins, sem=None):
        sem = sem or self.step_sem
        self.count[id(sem)] = self.count.get(id(sem), 0) + 1
        ins.then_inc(sem, 1)
        self.last = (sem, self.count[id(sem)])

    def free(self, ins, job):
        self.step(ins, self.freed_sem)
        assert JOBS[JOB_AT[job]][1] == self.name
        assert self.count[id(self.freed_sem)] == freed_count(JOB_AT[job], self.name), job

    def settle(self):
        self.eng.wait_ge(*self.last)


class Signals:

    def __init__(self, nc):
        new = nc.alloc_semaphore
        self.ident_loaded = new("ident_loaded")
        self.const_loaded = new("const_loaded")
        self.pos_loaded = new("pos_loaded")
        self.x_loaded = new("x_loaded")
        self.mu_loaded = new("mu_loaded")
        self.vec_loaded = new("vec_loaded")
        self.gain_loaded = new("gain_loaded")
        self.router_loaded = new("router_loaded")
        self.fgain_loaded = new("fgain_loaded")
        self.i_hi_ready = new("i_hi_ready")
        self.i_lo_ready = new("i_lo_ready")
        self.i_half_used = new("i_half_used")
        self.i_x_hi_ready = new("i_x_hi_ready")
        self.i_x_lo_ready = new("i_x_lo_ready")
        self.f_hi_ready = new("f_hi_ready")
        self.f_lo_ready = new("f_lo_ready")
        self.f_half_used = new("f_half_used")
        self.f_x_hi_ready = new("f_x_hi_ready")
        self.hi_ready = new("hi_ready")
        self.lo_ready = new("lo_ready")
        self.half_used = new("half_used")
        self.x_hi_ready = new("x_hi_ready")
        self.product_ready = new("product_ready")
        self.freed_act = new("freed_act")
        self.freed_vec = new("freed_vec")
        self.act_step = new("act_step")
        self.vec_step = new("vec_step")
        self.pool_step = new("pool_step")
        self.out_stored = new("out_stored")
        self.angles_ready = new("angles_ready")
        self.trig_ready = new("trig_ready")
        self.sumsq_ready = new("sumsq_ready")
        self.var_ready = new("var_ready")
        self.root_ready = new("root_ready")
        self.hn_ready = new("hn_ready")
        self.shift_zero = new("shift_zero")
        self.xs_ready = new("xs_ready")
        self.lora_act_ready = new("lora_act_ready")
        self.knsq_ready = new("knsq_ready")
        self.knroot_ready = new("knroot_ready")
        self.decay_sig_ready = new("decay_sig_ready")
        self.rate_sig_ready = new("rate_sig_ready")
        self.logd_ready = new("logd_ready")
        self.exps_ready = new("exps_ready")
        self.cex_ready = new("cex_ready")
        self.scan_in_ready = new("scan_in_ready")
        self.rope_ready = new("rope_ready")
        self.silu_g_ready = new("silu_g_ready")
        self.gn_var_ready = new("gn_var_ready")
        self.gn_root_ready = new("gn_root_ready")
        self.ret_done = new("ret_done")
        self.qa_sumsq = new("qa_sumsq")
        self.qa_ready = new("qa_ready")
        self.mla_key_ready = new("mla_key_ready")
        self.masked_ready = new("masked_ready")
        self.prob_ready = new("prob_ready")
        self.merged_done = new("merged_done")
        self.x_ready = new("x_ready")
        self.state_ready = new("state_ready")
        self.rwkv_done = new("rwkv_done")
        self.route_exp = new("route_exp")
        self.route_diff = new("route_diff")
        self.mask_ready = new("mask_ready")
        self.items_ready = new("items_ready")
        self.sel_ready = new("sel_ready")
        self.fin_ready = new("fin_ready")
        self.items_done = new("items_done")


def build(nc, x, positions, attn_norm, w_in, rwkv_mu, rwkv_w0, rwkv_w2, rwkv_a0, rwkv_a2, rwkv_g2, rwkv_k_k,
          rwkv_k_a, rwkv_r_k, rwkv_lnx_w, mla_q_norm, mla_w_qb, mla_kv_norm, mla_w_kvb, w_branch, w_o, ffn_norm,
          ffn_w_gate, ffn_w_up, ffn_w_down, moe_router, moe_w_gate, moe_w_up, moe_w_down, final_norm, const, out):
    at = [-(-int(nc.sbuf_base) // 64) * 64]

    def sb(name, shape, dt=F32, where=None):
        size = -(-int(np.prod(shape[1:])) * 4 // 32) * 32
        if where is None:
            where = at[0]
            at[0] += size
        return nc.alloc_sbuf_tensor_at(name, shape, dt, offset=where)

    h = sb("h", [P, T, D])
    hnT_at = at[0]
    hnT = sb("hnT", [P, KD, SEQ])
    hn_at = at[0]
    hn = sb("hn", [P, T, D])
    y_ret = sb("y_ret", [P, T, W], where=hn_at)
    y_mla = sb("y_mla", [P, T, W], where=hn_at + 4096)
    ring = sb("ring", [P, RING, SLOT])
    cst = sb("cst", [P, CONST.shape[1]])
    gains = sb("gains", [P, DEPTH, 2, KD])
    mgain = sb("mgain", [P, DEPTH, 3])
    cosT = sb("cosT", [P, T, 80])
    sinT = sb("sinT", [P, T, 80])
    pos_i = sb("pos_i", [P, T], I32)
    pos_f = sb("pos_f", [P, T])
    stat = sb("stat", [P, 8, 16])
    den = sb("den", [P, NH, T])
    smax = sb("smax", [P, NH, T])
    decay_end = sb("decay_end", [P, T, 4, 2])
    E = at[0]
    vec = sb("vec", [P, VEC_COLS])
    pr_at = at[0]
    pr = sb("pr", [P, T, RWCOLS])
    scratch = at[0]
    prev = sb("prev", [P, T, RWCOLS])
    kk = sb("kk", [P, T, W], where=scratch)
    tmp = sb("tmp", [P, T, W], where=scratch + 4096)
    ab = sb("ab", [P, T, W], where=scratch + 8192)
    ld = sb("ld", [P, T, W])
    ec_at = at[0]
    ec = sb("ec", [P, T, W])
    enc = sb("enc", [P, T, W])
    gg = sb("gg", [P, T, W])
    y_rwkv = sb("y_rwkv", [P, T, W], where=ec_at - 4096)
    qa = sb("qa", [P, T, MLAC])
    B = at[0]
    raw = sb("raw", [P, 4, T, W], where=B)
    qkT = sb("qkT", [P, 2, RH, T, P], where=B + 16384)
    rope_tmp = sb("rope_tmp", [P, 1024], where=B + 49152)
    ix_hi = sb("ix_hi", [P, KD, SEQ], F32R, where=ec_at - 4096)
    ix_lo = sb("ix_lo", [P, KD, SEQ], F32R, where=ec_at + 4096)
    i_hi = sb("i_hi", [P, 2, HALF], F32R, where=B + 16384)
    i_lo = sb("i_lo", [P, 2, HALF], F32R, where=B + 32768)
    sR = sb("sR", [P, RH, 384], where=B + 24576)
    mqT = sb("mqT", [P, NH, SEQ], where=B)
    mkT = sb("mkT", [P, NH, SEQ], where=B + 8192)
    mq = sb("mq", [P, T, NH, QK], where=B + 30720)
    mk = sb("mk", [P, T, NH, QK], where=B + 36864)
    mv = sb("mv", [P, T, NH, NOPE], where=B + 43008)
    sm = sb("sm", [P, 2, 384], where=B + 47104)
    pT = sb("pT", [P, 2, 384], where=B + 50176)
    loT = sb("loT", [P, T, 384], where=hn_at + 4096)
    cT = sb("cT", [P, 3, SEQ], where=B + 50176)
    mrope_tmp = sb("mrope_tmp", [P, 4, P], where=B + 47104)
    tT = sb("tT", [P, 4, 512], where=B)
    m1 = sb("m1", [P, NH, 512], where=B + 8192)
    am = sb("am", [P, NH, P], where=B + 24576)
    xi = sb("xi", [P, NH, P], where=B + 28672)
    xt = sb("xt", [P, NH, P], where=B + 32768)
    t1 = sb("t1", [P, NH, P], where=B + 36864)
    zz = sb("zz", [P, W], where=B + 40960)
    uu = sb("uu", [P, T, W], where=B + 43008)
    nw = sb("nw", [P, 4, P], where=B + 47104)
    st = sb("st", [P, 3, 4, HD], where=B + 49152)
    merged = sb("merged", [P, T, D], where=B)
    sigs = [sb(f"sig{n}", [P, 2, T, 512], where=w) for n, w in enumerate((E, E + 8192, ec_at))]
    assert VEC_AT["lnx"][0] * 4 >= 16384
    yT = [sb(f"yT{n}", [P, 4, SEQ], where=w) for n, w in enumerate((scratch + 4096, B + 24576, hn_at))]
    gT = sb("gT", [P, KD, SEQ], where=B + 32768)
    hmT_hi = sb("hmT_hi", [P, 22, SEQ], F32R, where=B)
    hmT_lo = sb("hmT_lo", [P, 22, SEQ], F32R, where=B + 22528)
    hm = sb("hm", [P, 2, T, 512], where=B + 45056)
    sg = sb("sg", [P, 2, T, 512], where=hn_at)
    f_hi = sb("f_hi", [P, 2, HALF], F32R, where=pr_at)
    f_lo = sb("f_lo", [P, 2, HALF], F32R, where=pr_at + 16384)
    fx_hi = sb("fx_hi", [P, KD, SEQ], F32R, where=hnT_at)
    fx_lo = sb("fx_lo", [P, KD, SEQ], F32R, where=ec_at)
    X = E
    w_hi = sb("w_hi", [P, PARTS, HALF], F32R, where=X)
    w_lo = sb("w_lo", [P, PARTS, HALF], F32R, where=X + 24576)
    xg_hi = sb("xg_hi", [P, KD, P], F32R, where=X + 49152)
    xg_lo = sb("xg_lo", [P, KD, P], F32R, where=X + 53248)
    ehT_hi = sb("ehT_hi", [P, 28, P], F32R, where=X + 57344)
    ehT_lo = sb("ehT_lo", [P, 28, P], F32R, where=X + 71680)
    sel = sb("sel", [P, T, P], where=X + 86016)
    csel = sb("csel", [P, T, P], where=X + 87040)
    cselT = sb("cselT", [P, SEQ], where=X + 88064)
    ehm = sb("ehm", [P, 2, 512], where=X + 89088)
    esg = sb("esg", [P, 2, 512], where=X + 93184)
    ey = sb("ey", [P, D], where=X + 97280)
    rt = sb("rt", [P, 16, T, NE], where=X + 101376)
    router = sb("router", [P, KD, NE], where=X + 102400)
    it_f = sb("it_f", [1, 64], where=X + 102656)
    items = sb("items", [1, 32], I32, where=X + 102912)
    spos = sb("spos", [P, 2, T, NE], where=X + 103040)
    comb = sb("comb", [P, 2, T, NE], where=X + 103168)
    fin = sb("fin", [P, T, D], where=X)
    fgain = sb("fgain", [P, D], where=X + 104448)
    assert X + 104448 + 4096 <= B + 53248
    assert B + 53248 <= int(nc.sbuf_usable_end), (B, int(nc.sbuf_usable_end))

    def C(name, a=0, b=None):
        o, n = CONST_AT[name]
        return cst[:, o + a:o + (n if b is None else b)]

    def VEC(name, a=0, b=None):
        o, n = VEC_AT[name]
        return vec[:, o + a:o + (n if b is None else b)]

    def each(ap, n=T):
        return ap.unsqueeze(1).to_broadcast([ap.shape[0], n, ap.shape[1]])

    def wide(ap, n):
        return ap.unsqueeze(len(ap.shape)).to_broadcast(list(ap.shape) + [n])

    banks = [nc.alloc_psum_tensor(f"bank{i}", [P, 512], F32) for i in range(BANKS)]

    s = Signals(nc)
    slot_loaded = [nc.alloc_semaphore(f"slot{i}_loaded") for i in range(RING)]
    shift_loaded = [nc.alloc_semaphore(f"shift{j}_loaded") for j in range(4)]
    freed = {"act": s.freed_act, "vec": s.freed_vec}
    FR = {e: freed_count(len(JOBS) - 1, e) for e in freed}
    IF = {e: item_freed(len(ITEM) - 1, e) for e in freed}
    LOOP_FR = {"act": FR["act"], "vec": FR["vec"] + AHEAD}
    NPAN = len(PANELS)

    def product(eng, job):
        eng.wait_ge(s.product_ready, JOB_AT[job] + 1)
        return banks[JOB_AT[job] % BANKS]

    def read_out(eng, job):
        k = JOB_AT[job]
        eng.wait_ge(freed[JOBS[k][1]], freed_count(k, JOBS[k][1]))

    def used_up(n):
        kind, l, j, _ = PANELS[n]
        if kind.startswith("ffn"):
            return s.f_lo_ready, 2 * (n - FIRST_FFN + 1)
        if kind == "in":
            return s.i_lo_ready, 2 * (9 * l + j + 1)
        job = {"lora": f"g1.{l}", "mla": f"mk11.{l}", "gate": f"gt{2 * j + 1}.{l}",
               "branch": f"br{j}11.{l}", "o": f"o{j}1.{l}"}[kind]
        return s.product_ready, JOB_AT[job] + 1

    FIRST_FFN = next(m for m, p in enumerate(PANELS) if p[0] == "ffn_gate")

    def ffn_half(q):
        width = FFN_COLS[q // 4] * 4 if q < 24 else FFN_COLS[(q - 24) // 2] // P * D // 2
        return ring[:, (FIRST_FFN + q // 2) % RING, width * (q % 2):width * (q % 2) + width], width

    NIN = 2 * len(IN_PANELS)

    def in_half(l, q):
        width = IN_PANELS[q // 2][1] * KD // 2
        return ring[:, (PANELS.index(("in", l, q // 2, 1))) % RING, width * (q % 2):width * (q % 2) + width], width

    def in_half_used(eng, l, q):
        if q % 2:
            eng.wait_ge(s.product_ready, JOB_AT[f"in{q // 2}_1.{l}"] + 1)
        else:
            eng.wait_ge(s.i_half_used, NIN // 2 * l + q // 2 + 1)

    def ffn_half_used(eng, q):
        if q < 24 and q % 2:
            eng.wait_ge(s.product_ready, JOB_AT[f"f{'gu'[q // 2 % 2]}{q // 4}1.0"] + 1)
        else:
            eng.wait_ge(s.f_half_used, q // 2 + 1 if q < 24 else q - 24 + 13)

    def ahead(eng, job):
        eng.wait_ge(s.product_ready, len(JOBS) + AHEAD - (len(ITEM) - 1 - ITEM_AT[job]))
        return banks[ITEM_AT[job] % BANKS]

    def half_used(q, item):
        before, q = (1, q + 2 * EP) if q < 0 else (0, q)
        if q == 2 * EP - 1 or (q < 28 and q % 2):
            job = "ed1" if q >= 28 else f"e{'gu'[q // 2 % 2]}{q // 4}"
            return s.product_ready, item * len(ITEM) + (len(JOBS) + AHEAD + ITEM_AT[job] + 1 - len(ITEM) * before)
        n = q // 2 + 1 if q < 28 else q - 28 + 15
        return s.half_used, item * HALVES + (HALVES + n - HALVES * before)

    def panel_loaded(n):
        return 16 * sum(PANELS[m][3] for m in range(n + 1) if m % RING == n % RING)

    def rows(w):
        return w.rearrange("(p c) n -> p c n", p=P)

    blk = nc.Block()
    block = blk.__enter__()

    @block.sync
    def _(sp):
        sp.dma_start(cst[:, 0:P], const[:, 0:P]).then_inc(s.ident_loaded, 16)
        for t in range(T):
            sp.dma_start(h[:, t, :], x[0, t * P:(t + 1) * P, :]).then_inc(s.x_loaded, 16)
        sp.wait_ge(s.x_loaded, 16 * T)
        for n, (kind, l, j, _) in enumerate(PANELS):
            if n == 2:
                sp.dma_start(cst[:, P:], const[:, P:]).then_inc(s.const_loaded, 16)
            if n >= RING:
                sp.wait_ge(*used_up(n - RING))
            slot = ring[:, n % RING, :]
            sem = slot_loaded[n % RING]

            def cols(w, c0, width):
                k = w.shape[0] // P
                dst = slot[:, 0:k * width].rearrange("p (c n) -> p c n", c=k)
                sp.dma_start(dst, rows(w)[:, :, c0:c0 + width]).then_inc(sem, 16)

            if kind == "in":
                cols(w_in[l], *IN_PANELS[j])
            elif kind == "gate":
                cols(w_in[l], C_GATE + D * BRANCHES[j // 2] + 512 * (j % 2), 512)
            elif kind == "lora":
                sp.dma_start(slot[0:64, 0:512], rwkv_w2[l]).then_inc(sem, 16)
                sp.dma_start(slot[64:128, 0:512], rwkv_a2[l]).then_inc(sem, 16)
                sp.dma_start(slot[:, 512:1024], rwkv_g2[l, 0:128, :]).then_inc(sem, 16)
                sp.dma_start(slot[0:32, 1024:1536], rwkv_g2[l, 128:160, :]).then_inc(sem, 16)
            elif kind == "mla":
                sp.dma_start(slot[:, 0:1536].rearrange("p (c n) -> p c n", c=2), rows(mla_w_qb[l])).then_inc(sem, 16)
                sp.dma_start(slot[:, 1536:2560], mla_w_kvb[l]).then_inc(sem, 16)
            elif kind == "branch":
                cols(w_branch[l, j], 0, D)
            elif kind == "o":
                cols(w_o[l], 512 * j, 512)
            elif kind == "ffn_gate":
                cols(ffn_w_gate[0], 512 * j, FFN_COLS[j])
            elif kind == "ffn_up":
                cols(ffn_w_up[0], 512 * j, FFN_COLS[j])
            else:
                cols(ffn_w_down[0, 512 * j:512 * j + FFN_COLS[j], :], 0, D)

        def expert_panels(e, item):
            for m in range(EP):
                i = (NPAN + m) % RING
                sp.wait_ge(s.lo_ready, item * (2 * EP) + (2 * RING + 2 * (m - RING + 1)))
                if m < 14:
                    w = (moe_w_gate, moe_w_up)[m % 2][0, bass.ds(e, 1), :, 512 * (m // 2):512 * (m // 2) + 512]
                    k = KD
                else:
                    w = moe_w_down[0, bass.ds(e, 1), 512 * (m - 14):512 * (m - 14) + 512, :]
                    k = 4
                sp.dma_start(ring[:, i, :].rearrange("p (c n) -> p c n", c=k),
                             w.rearrange("o (p c) n -> p (o c) n", p=P)).then_inc(slot_loaded[i], 16)

        sp.wait_ge(*used_up(NPAN - 1))
        with sp.Fori(0, SURE) as item:
            expert_panels(item, item)
        sp.wait_ge(s.items_ready, 1)
        n_items = sp.value_load(items[0:1, 24:25], min_val=SURE, max_val=SURE + 3)
        with sp.If(n_items > SURE):
            with sp.Fori(SURE, n_items) as item:
                e = sp.value_load(items[0:1, bass.ds(item + 12, 1)], min_val=0, max_val=NE - 1)
                expert_panels(e, item)
            sp.nop()
        with sp.Else():
            sp.nop()
        for t in range(T):
            sp.wait_ge(s.fin_ready, t + 1)
            sp.dma_start(out[0, t * P:(t + 1) * P, :], fin[:, t, :]).then_inc(s.out_stored, 16)
        sp.wait_ge(s.out_stored, 16 * T)

    @block.gpsimd
    def _(pool):
        for t in range(T):
            pool.dma_start(pos_i[:, t:t + 1], positions[:, t * P:(t + 1) * P].rearrange("a p -> p a"))\
                .then_inc(s.pos_loaded, 16)
        own = Own(pool, "pool", s.pool_step, None)
        G = nc.gpsimd

        def rotate(x1, x2, c, sn, f, ready):
            own.step(G.tensor_tensor(f[0], x1, sn, ALU.mult))
            own.step(G.tensor_tensor(f[1], x2, sn, ALU.mult))
            own.step(G.tensor_tensor(f[2], x1, c, ALU.mult))
            own.step(G.tensor_tensor(f[3], x2, c, ALU.mult))
            own.settle()
            own.step(G.tensor_tensor(x1, f[2], f[1], ALU.subtract))
            own.step(G.tensor_tensor(x2, f[0], f[3], ALU.add), ready)

        pool.wait_ge(s.const_loaded, 16)
        for l in range(DEPTH):
            if l:
                pool.wait_ge(s.merged_done, 2 * T * l)
            for name, w in (("mu", rwkv_mu[l]), ("w0", rwkv_w0[l]), ("a0", rwkv_a0[l]), ("k_k", rwkv_k_k[l]),
                            ("k_a", rwkv_k_a[l]), ("r_k", rwkv_r_k[l].rearrange("h d -> (h d)")),
                            ("lnx", rwkv_lnx_w[l])):
                pool.dma_start(VEC(name), w.partition_broadcast(P)).then_inc(
                    s.mu_loaded if name == "mu" else s.vec_loaded, 16)
            if l:
                read_out(pool, f"fd11.{l - 1}")
            own.step(G.memset(prev[0:1, 0, :], 0.0), s.shift_zero)
            pool.wait_ge(s.trig_ready, 2)
            read_out(pool, f"in5_1.{l}")
            f = [rope_tmp[:, 256 * i:256 * i + 256].rearrange("p (h e) -> p h e", h=RH) for i in range(4)]
            for t in range(T):
                for a in range(2):
                    qk = raw[:, a, t, :].rearrange("p (h e) -> p h e", h=RH)
                    if t or a:
                        own.settle()
                    rotate(qk[:, :, 0:64], qk[:, :, 64:128], each(cosT[:, t, 0:64], RH), each(sinT[:, t, 0:64], RH),
                           f, s.rope_ready if a else s.pool_step)
            read_out(pool, f"mk11.{l}")
            for t in range(T):
                own.settle()
                f = [mrope_tmp[:, i, :].rearrange("p (h e) -> p h e", h=8) for i in range(4)]
                rotate(mq[:, t, :, 64:80], mq[:, t, :, 80:96], each(cosT[:, t, 64:80], 8),
                       each(sinT[:, t, 64:80], 8), f, s.pool_step)
                own.settle()
                rotate(qa[:, t, 384:400], qa[:, t, 400:416], cosT[:, t, 64:80], sinT[:, t, 64:80],
                       [mrope_tmp[:, i, 0:16] for i in range(4)], s.pool_step)
                own.settle()
                own.step(G.tensor_copy(mk[:, t, :, 64:96], each(qa[:, t, 384:416], NH)), s.mla_key_ready)
        read_out(pool, "o11.1")
        pool.dma_start(router[:], moe_router[0].rearrange("(p c) n -> p c n", p=P)).then_inc(s.router_loaded, 16)
        pool.dma_start(fgain[:], final_norm.partition_broadcast(P)).then_inc(s.fgain_loaded, 16)

    @block.scalar
    def _(act):
        own = Own(act, "act", s.act_step, s.freed_act)
        A = nc.scalar

        def norm_sums(m):
            for t in range(T):
                own.step(A.activation(hn[:, t, :], h[:, t, :], ACT.Square, accum_out=stat[:, 0, t:t + 1]),
                         s.sumsq_ready)
            act.wait_ge(s.var_ready, m + 1)
            own.step(A.activation(stat[:, 0, 0:T], stat[:, 0, 0:T], ACT.Sqrt), s.root_ready)

        def norm_transposed(name, l, g, quarters=range(4)):
            for q in quarters:
                b = product(act, f"{name}{q}.{l}")
                for i in range(2):
                    c = 2 * q + i
                    ins = A.activation(hnT[:, c, :], b[:, 256 * i:256 * i + 256], ACT.Copy,
                                       scale=gains[:, l, g, c:c + 1])
                    own.step(ins) if i == 0 else own.free(ins, f"{name}{q}.{l}")

        def copy_out(job, dst, cols=None, rows_=P, scale=1.0):
            b = product(act, job)
            src = b[0:rows_, 0:cols or 512]
            if len(dst.shape) == 3:
                src = src.rearrange("p (a b) -> p a b", a=dst.shape[1])
            own.free(A.activation(dst, src, ACT.Copy, scale=scale), job)

        for l in range(DEPTH):
            for g, w in enumerate((attn_norm, ffn_norm)):
                act.dma_start(gains[:, l, g, :], w[l].rearrange("(p c) -> p c", p=P)).then_inc(s.gain_loaded, 16)
            act.dma_start(mgain[:, l, 0:2], mla_q_norm[l].rearrange("(p c) -> p c", p=P)).then_inc(s.gain_loaded, 16)
            act.dma_start(mgain[:, l, 2:3], mla_kv_norm[l].rearrange("(p c) -> p c", p=P)).then_inc(s.gain_loaded, 16)
        act.wait_ge(s.gain_loaded, 16 * 4 * DEPTH)
        for l in range(DEPTH):
            if l:
                read_out(act, f"fd11.{l - 1}")
            else:
                act.wait_ge(s.x_loaded, 16 * T)
            norm_sums(2 * l)

            def in_hi(q):
                src, width = in_half(l, q)
                if q % 2 == 0:
                    n = PANELS.index(("in", l, q // 2, 1))
                    act.wait_ge(slot_loaded[n % RING], panel_loaded(n))
                if q > 1:
                    in_half_used(act, l, q - 2)
                own.step(A.activation(i_hi[:, q % 2, 0:width], src, ACT.Copy), s.i_hi_ready)

            in_hi(0)
            in_hi(1)
            for r in range(2):
                norm_transposed("nT", l, 0, (2 * r, 2 * r + 1))
                own.settle()
                own.step(A.activation(ix_hi[:, 4 * r:4 * r + 4, :], hnT[:, 4 * r:4 * r + 4, :], ACT.Copy),
                         s.i_x_hi_ready)
            for j, (c0, width) in enumerate(IN_PANELS):
                if j < 8:
                    in_hi(2 * j + 2)
                    in_hi(2 * j + 3)
                for t in range(T):
                    if j < 4:
                        o = 1536 if j == 0 else 512 * (j - 1)
                        dst = pr[:, t, o:o + width]
                    elif j < 8:
                        dst = raw[:, j - 4, t, :]
                    else:
                        dst = qa[:, t, :]
                    copy_out(f"in{j}_{t}.{l}", dst, width)
                if l == 0 and j == 2:
                    act.wait_ge(s.angles_ready, 1)
                    own.step(A.activation(sinT[:], sinT[:], ACT.Sin), s.trig_ready)
                    own.step(A.activation(cosT[:], cosT[:], ACT.Sin), s.trig_ready)
                if j < 4:
                    own.settle()
                    if j == 0:
                        act.wait_ge(s.shift_zero, l + 1)
                    act.dma_start(prev[1:P, :, o:o + width], pr[0:P - 1, :, o:o + width])\
                        .then_inc(shift_loaded[j], 16)
                    act.dma_start(prev[0:1, 1, o:o + width], pr[P - 1:P, 0, o:o + width])\
                        .then_inc(shift_loaded[j], 16)
                if j == 6:
                    act.wait_ge(s.xs_ready, l + 1)
                    own.step(A.activation(pr[:, :, 1536:1600], pr[:, :, 1536:1600], ACT.Tanh))
                    own.step(A.activation(pr[:, :, 1664:1824], pr[:, :, 1664:1824], ACT.Sigmoid), s.lora_act_ready)
                if j == 7:
                    own.settle()
                    own.step(A.activation(raw[:, 3, :, :], raw[:, 3, :, :], ACT.Silu), s.silu_g_ready)
                    for t in range(T):
                        b = product(act, f"loT{t}.{l}")
                        own.step(A.activation(loT[:, t, 0:256], b[:, 0:256], ACT.Copy))
                        own.free(A.activation(loT[0:32, t, 256:384], b[0:32, 256:384], ACT.Copy), f"loT{t}.{l}")
            own.settle()
            for t in range(T):
                own.step(A.activation(hn[:, 0, 384 * t:384 * t + 256], qa[:, t, 0:256], ACT.Square,
                                      accum_out=stat[:, 2, 2 * t:2 * t + 1]), s.qa_sumsq)
                own.step(A.activation(hn[:, 0, 384 * t + 256:384 * t + 384], qa[:, t, 256:384], ACT.Square,
                                      accum_out=stat[:, 2, 2 * t + 1:2 * t + 2]), s.qa_sumsq)
            act.wait_ge(s.knsq_ready, l + 1)
            own.step(A.activation(stat[:, 1, :], stat[:, 1, :], ACT.Sqrt))
            own.step(A.activation(stat[:, 2, 0:4], stat[:, 2, 0:4], ACT.Sqrt), s.knroot_ready)
            for t in range(T):
                copy_out(f"g{t}.{l}", gg[:, t, :])
            for t in range(T):
                for q in range(2):
                    copy_out(f"rT{q}{t}.{l}", qkT[:, q, :, t, :])
            read_out(act, f"z1.{l}")
            own.step(A.activation(ld[:], ld[:], ACT.Sigmoid), s.decay_sig_ready)
            read_out(act, f"a1.{l}")
            own.step(A.activation(ab[:], ab[:], ACT.Sigmoid), s.rate_sig_ready)
            for t in range(T):
                b = product(act, f"cT{t}.{l}")
                for i in range(3):
                    ins = A.activation(cT[:, i, t * P:(t + 1) * P], b[:, i * P:(i + 1) * P], ACT.Copy,
                                       scale=mgain[:, l, i:i + 1])
                    own.step(ins) if i < 2 else own.free(ins, f"cT{t}.{l}")
            for t in range(T):
                for u in range(2):
                    copy_out(f"mq{t}{u}.{l}", mq[:, t, 4 * u:4 * u + 4, :], 384)
            for t in range(T):
                for u in range(2):
                    b = product(act, f"mk{t}{u}.{l}")
                    kv = b[:].rearrange("p (h e) -> p h e", h=4)
                    own.step(A.activation(mk[:, t, 4 * u:4 * u + 4, 0:64], kv[:, :, 0:64], ACT.Copy))
                    own.free(A.activation(mv[:, t, 4 * u:4 * u + 4, :], kv[:, :, 64:128], ACT.Copy),
                             f"mk{t}{u}.{l}")
            for t in range(T):
                b = product(act, f"cum{t}.{l}")
                own.step(A.activation(ec[:, t, :], b[:], ACT.Exp))
                own.step(A.activation(enc[:, t, :], b[:], ACT.Exp, scale=-1.0), s.exps_ready)
            for t in range(T):
                act.wait_ge(s.cex_ready, T * l + t + 1)
                own.free(A.activation(ld[:, t, :], ld[:, t, :], ACT.Exp), f"cum{t}.{l}")
            b = product(act, f"pc.{l}")
            own.free(A.activation(decay_end[:], b[:, 0:16].rearrange("p (t a c) -> p t a c", t=T, a=4), ACT.Exp),
                     f"pc.{l}")
            for t in range(T):
                copy_out(f"oR{t}.{l}", y_ret[:, t, :])
            act.wait_ge(s.gn_var_ready, 2 * l + 1)
            own.step(A.activation(stat[:, 4, 0:8], stat[:, 4, 0:8], ACT.Sqrt), s.gn_root_ready)
            def gate(g):
                n, u, t = BRANCHES[g // 4], g // 2 % 2, g % 2
                b = product(act, f"gt{g}.{l}")
                own.free(A.activation(sigs[n][:, u, t, :], b[:], ACT.Sigmoid), f"gt{g}.{l}")

            for q, dst in enumerate((mqT, mkT)):
                gate(q)
                if q:
                    act.wait_ge(s.ret_done, l + 1)
                for u in range(4):
                    copy_out(f"mT{q}{u}.{l}", dst[0:QK, 2 * u:2 * u + 2, :], rows_=QK)
            for i in range(NH + 1):
                if i < NH:
                    act.wait_ge(s.masked_ready, NH * l + i + 1)
                    own.step(A.activation(sm[:, i % 2, 0:128], sm[:, i % 2, 0:128], ACT.Exp,
                                          bias=smax[:, i, 0:1], accum_out=den[:, i, 0:1]))
                    own.step(A.activation(sm[:, i % 2, 128:384], sm[:, i % 2, 128:384], ACT.Exp,
                                          bias=smax[:, i, 1:2], accum_out=den[:, i, 1:2]), s.prob_ready)
                if i:
                    copy_out(f"pT{i - 1}.{l}", pT[:, (i - 1) % 2, :], 384)
                if i % 2 and i < NH:
                    gate(2 + i // 2)

            for t in range(T):
                for hp in range(4):
                    copy_out(f"kT{t}{hp}.{l}", tT[:, hp, :])
                for u in range(2 if t == 0 else 0):
                    copy_out(f"yT0{u}.{l}", yT[0][:, 2 * u:2 * u + 2, :])
                for g in range(len(GATED)):
                    gate(6 + 3 * t + g)
                copy_out(f"W{t}.{l}", nw[:], scale=-1.0)
                copy_out(f"Z{t}.{l}", zz[:])
                copy_out(f"U{t}.{l}", uu[:, t, :])
                gate(8 + 3 * t)
                for e in range(2):
                    copy_out(f"Y{t}{e}.{l}", y_rwkv[:, t, :].rearrange("p (a b d) -> p a b d", a=4, b=2)[:, :, e, :],
                             256)
            for n in BRANCHES[1:]:
                if n == 1:
                    act.wait_ge(s.gn_var_ready, 2 * l + 2)
                    own.step(A.activation(stat[:, 4, :], stat[:, 4, :], ACT.Sqrt), s.gn_root_ready)
                for u in range(2):
                    copy_out(f"yT{n}{u}.{l}", yT[n][:, 2 * u:2 * u + 2, :])
            for q in range(4):
                copy_out(f"gT{q}.{l}", gT[:, 2 * q:2 * q + 2, :])

            def ffn_high(q):
                src, width = ffn_half(q)
                if q % 2 == 0:
                    n = FIRST_FFN + q // 2
                    act.wait_ge(slot_loaded[n % RING], panel_loaded(n))
                if q > 1:
                    ffn_half_used(act, q - 2)
                own.step(A.activation(f_hi[:, q % 2, 0:width], src, ACT.Copy), s.f_hi_ready)

            if l == 0:
                ffn_high(0)
                ffn_high(1)
            read_out(act, f"o11.{l}")
            norm_sums(2 * l + 1)
            if l:
                norm_transposed("fT", l, 1)
            else:
                for q in range(4):
                    b = product(act, f"fT{q}.0")
                    for i in range(2):
                        c = 2 * q + i
                        own.step(A.activation(fx_hi[:, c, :], b[:, 256 * i:256 * i + 256], ACT.Copy,
                                              scale=gains[:, 0, 1, c:c + 1]), s.f_x_hi_ready if i else None)
                for q in range(2, 36):
                    ffn_high(q)
                    if q % 4 == 3 and q < 24:
                        j = q // 4
                        w_ = FFN_COLS[j]
                        for t in range(T):
                            if j > 1:
                                read_out(act, f"fu{j - 2}{t}.0")
                            b = product(act, f"fg{j}{t}.0")
                            own.free(A.activation(sg[:, j % 2, t, 0:w_], b[:, 0:w_], ACT.Silu), f"fg{j}{t}.0")
                    if q % 4 == 1 and 9 <= q <= 29:
                        j = (q - 9) // 4
                        k = FFN_COLS[j] // P
                        for t in range(T):
                            b = product(act, f"hT{j}{t}.0")
                            own.step(A.activation(hmT_hi[:, 4 * j:4 * j + k, t * P:(t + 1) * P],
                                                  b[:, 0:k * P].rearrange("p (c n) -> p c n", c=k), ACT.Copy),
                                     s.f_x_hi_ready)
        act.wait_ge(s.route_diff, 1)
        own.step(A.activation(stat[:, 6, 0:2], stat[:, 6, 0:2], ACT.Exp), s.route_exp)
        def gathered_hi(eng_wait):
            for u in range(2):
                b = eng_wait(f"gx{u}")
                for i in range(4):
                    ins = A.activation(xg_hi[:, 4 * u + i, :], b[:, i * P:(i + 1) * P], ACT.Copy,
                                       scale=gains[:, 1, 1, 4 * u + i:4 * u + i + 1])
                ins.then_inc(s.x_hi_ready, 1)

        gathered_hi(lambda job: ahead(act, job))
        act.wait_ge(s.items_ready, 1)
        n_items = act.value_load(items[0:1, 24:25], min_val=SURE, max_val=SURE + 3)
        with act.Fori(0, n_items) as item:
            def item_product(job):
                act.wait_ge(s.product_ready, item * len(ITEM) + (len(JOBS) + AHEAD + ITEM_AT[job] + 1))
                return banks[ITEM_AT[job] % BANKS]

            def hi(q):
                if q % 2 == 0:
                    m = q // 2
                    i = (NPAN + m) % RING
                    before = 16 * sum(PANELS[n][3] for n in range(NPAN) if n % RING == i)
                    nth = sum((NPAN + r) % RING == i for r in range(m + 1))
                    act.wait_ge(slot_loaded[i], item * (16 * EP // RING) + (before + 16 * nth))
                act.wait_ge(*half_used(q - PARTS, item))
                i, o = (NPAN + q // 2) % RING, HALF * (q % 2)
                A.activation(w_hi[:, q % PARTS, :], ring[:, i, o:o + HALF], ACT.Copy).then_inc(s.hi_ready, 1)

            for q in range(2 * EP):
                hi(q)
                if q % 4 == 3 and q < 28:
                    j = q // 4
                    if j > 1:
                        act.wait_ge(s.freed_vec,
                                    item * IF["vec"] + (LOOP_FR["vec"] + item_freed(ITEM_AT[f"eu{j - 2}"], "vec")))
                    A.activation(esg[:, j % 2, :], item_product(f"eg{j}")[:], ACT.Silu).then_inc(s.freed_act, 1)
                    if j == 0:
                        A.activation(cselT[:], item_product("csT")[:, 0:SEQ], ACT.Copy).then_inc(s.freed_act, 1)
                if q % 4 == 1 and 9 <= q <= 33:
                    j = (q - 9) // 4
                    A.activation(ehT_hi[:, 4 * j:4 * j + 4, :],
                                 item_product(f"eT{j}")[:].rearrange("p (c n) -> p c n", c=4),
                                 ACT.Copy).then_inc(s.x_hi_ready, 1)
                if q == 35:
                    gathered_hi(item_product)
        act.wait_ge(s.items_done, 1)
        norm_sums(4)

    @block.tensor
    def _(pe):
        M, TR = nc.tensor.matmul, nc.tensor.transpose
        ident = C("ident")
        used = [0]

        def bank(job):
            k = JOB_AT[job]
            if k >= BANKS:
                e = JOBS[k - BANKS][1]
                pe.wait_ge(freed[e], freed_count(k - BANKS, e))
            return banks[k % BANKS]

        def panel(kind):
            n = used[0]
            assert PANELS[n][0] == kind, (n, PANELS[n], kind)
            pe.wait_ge(slot_loaded[n % RING], panel_loaded(n))
            used[0] += 1
            return ring[:, n % RING, :]

        def done(ins):
            ins.then_inc(s.product_ready, 1)

        def transpose_in(jobs, src):
            for q in range(4):
                b = bank(jobs.format(q))
                for i in range(2):
                    for t in range(T):
                        ins = TR(b[:, 256 * i + 128 * t:256 * i + 128 * t + 128], src[:, t, 2 * q + i:D:KD], ident)
                done(ins)

        def project(job, lhs, slot, k, width, t, c0=0, row=None):
            b = bank(job)
            w = slot[:, 0:k * (row or width)].rearrange("p (c n) -> p c n", c=k)
            for c in range(k):
                ins = M(b[:, 0:width], lhs[:, c, t * P:(t + 1) * P], w[:, c, c0:c0 + width], start=c == 0,
                        stop=c == k - 1)
            done(ins)

        def three(dst, x, w, c, t, b, cols, start, stop):
            tok = slice(t * P, (t + 1) * P)
            for n, (a, v) in enumerate(((x[0], w[0]), (x[0], w[1]), (x[1], w[0]))):
                ins = M(dst, a[:, c, tok], v[:, b, cols], start=start and n == 0, stop=stop and n == 2,
                        skip_group_check=True)
            return ins

        pe.wait_ge(s.ident_loaded, 16)
        for l in range(DEPTH):
            pe.wait_ge(s.hn_ready, 2 * T * l + T)
            transpose_in("nT{}." + str(l), hn)
            for j, (_, width) in enumerate(IN_PANELS):
                if j == 8:
                    pe.wait_ge(s.lora_act_ready, l + 1)
                    for t in range(T):
                        b = bank(f"loT{t}.{l}")
                        TR(b[:, 0:128], pr[:, t, 1536:1664], ident)
                        TR(b[:, 128:256], pr[:, t, 1664:1792], ident)
                        done(TR(b[0:32, 256:384], pr[:, t, 1792:1824], ident))
                used[0] += 1
                bs = [bank(f"in{j}_{t}.{l}") for t in range(T)]
                for r in range(2):
                    q = 2 * j + r
                    if j == 0:
                        pe.wait_ge(s.i_x_lo_ready, 2 * l + r + 1)
                    pe.wait_ge(s.i_lo_ready, NIN * l + q + 1)
                    for t in range(T):
                        for c in range(4):
                            ins = three(bs[t][:, 0:width], (ix_hi, ix_lo), (i_hi, i_lo), 4 * r + c, t, q % 2,
                                        slice(width * c, width * c + width), r + c == 0, r == 1 and c == 3)
                        if r:
                            done(ins)
                    if r == 0:
                        ins.then_inc(s.i_half_used, 1)
            slot = panel("lora")
            for t in range(T):
                read_out(pe, f"loT{t}.{l}")
                done(M(bank(f"z{t}.{l}")[:], loT[0:64, t, 0:128], slot[0:64, 0:512], start=True, stop=True))
                done(M(bank(f"a{t}.{l}")[:], loT[64:128, t, 0:128], slot[64:128, 0:512], start=True, stop=True))
                b = bank(f"g{t}.{l}")
                M(b[:], loT[:, t, 128:256], slot[:, 512:1024], start=True, stop=False)
                done(M(b[:], loT[0:32, t, 256:384], slot[0:32, 1024:1536], start=False, stop=True))
            for t in range(T):
                pe.wait_ge(s.rope_ready, T * l + t + 1)
                for q in range(2):
                    b = bank(f"rT{q}{t}.{l}")
                    for i in range(RH):
                        ins = TR(b[:, i * P:(i + 1) * P], raw[:, q, t, i * P:(i + 1) * P], ident)
                    done(ins)
            read_out(pe, f"rT11.{l}")
            for i in range(RH):
                b = bank(f"sR{i}.{l}")
                M(b[:, 0:256], qkT[:, 1, i, 0, :], qkT[:, 0, i, :, :], start=True, stop=True)
                done(M(b[:, 256:384], qkT[:, 1, i, 1, :], qkT[:, 0, i, 1, :], start=True, stop=True))
            slot = panel("mla")
            pe.wait_ge(s.qa_ready, l + 1)
            for t in range(T):
                b = bank(f"cT{t}.{l}")
                for i in range(2):
                    TR(b[:, i * P:(i + 1) * P], qa[:, t, i:256:2], ident)
                done(TR(b[:, 256:384], qa[:, t, 256:384], ident))
            read_out(pe, f"cT1.{l}")
            for t in range(T):
                for u in range(2):
                    project(f"mq{t}{u}.{l}", cT, slot, 2, 384, t, 384 * u, 768)
            for t in range(T):
                for u in range(2):
                    done(M(bank(f"mk{t}{u}.{l}")[:], cT[:, 2, t * P:(t + 1) * P],
                           slot[:, 1536 + 512 * u:2048 + 512 * u], start=True, stop=True))
            pe.wait_ge(s.logd_ready, l + 1)
            pe.wait_ge(s.const_loaded, 16)
            for t in range(T):
                done(M(bank(f"cum{t}.{l}")[:], C("chunk_upto"), ld[:, t, :], start=True, stop=True))
            b = bank(f"pc.{l}")
            for t in range(T):
                for hp in range(4):
                    o = 2 * (4 * t + hp)
                    ins = M(b[:, o:o + 2], ld[:, t, hp * P:(hp + 1) * P], C("chunk_sel"), start=True, stop=True)
            done(ins)
            read_out(pe, f"sR3.{l}")
            for t in range(T):
                b = bank(f"oR{t}.{l}")
                for i in range(RH):
                    o = b[:, i * P:(i + 1) * P]
                    cols = slice(i * P, (i + 1) * P)
                    if t == 0:
                        ins = M(o, sR[:, i, 0:128], raw[:, 2, 0, cols], start=True, stop=True)
                    else:
                        M(o, sR[:, i, 128:256], raw[:, 2, 0, cols], start=True, stop=False)
                        ins = M(o, sR[:, i, 256:384], raw[:, 2, 1, cols], start=False, stop=True)
                done(ins)
            gates = []

            def gate_part(g, a, b_):
                if a == 0:
                    if g % 2 == 0:
                        gates[:] = [panel("gate")]
                    bank(f"gt{g}.{l}")
                dst = banks[JOB_AT[f"gt{g}.{l}"] % BANKS]
                for c in range(a, b_):
                    ins = M(dst[:], hnT[:, c, (g % 2) * P:(g % 2) * P + P],
                            gates[0][:, 512 * c:512 * c + 512], start=c == 0, stop=c == KD - 1,
                            skip_group_check=True)
                if b_ == KD:
                    done(ins)

            gate_part(0, 0, 8)
            pe.wait_ge(s.mla_key_ready, T * (l + 1))
            for q, src in enumerate((mq, mk)):
                for u in range(4):
                    b = bank(f"mT{q}{u}.{l}")
                    for i in range(2):
                        for t in range(T):
                            ins = TR(b[0:QK, 256 * i + 128 * t:256 * i + 128 * t + 128], src[:, t, 2 * u + i, :],
                                     ident)
                    done(ins)
                if q == 0:
                    gate_part(1, 0, 8)
            read_out(pe, f"mT13.{l}")
            for i in range(NH + 2):
                if i < NH:
                    b = bank(f"sM{i}.{l}")
                    M(b[:, 0:128], mqT[0:QK, i, 0:128], mkT[0:QK, i, 0:128], start=True, stop=True)
                    done(M(b[:, 128:384], mqT[0:QK, i, 128:256], mkT[0:QK, i, :], start=True, stop=True))
                if i < NH:
                    gate_part(2 + i // 2, 4 * (i % 2), 3 + 4 * (i % 2))
                if 0 < i <= NH:
                    pe.wait_ge(s.prob_ready, NH * l + i)
                    b = bank(f"pT{i - 1}.{l}")
                    for c in range(3):
                        ins = TR(b[:, c * P:(c + 1) * P], sm[:, (i - 1) % 2, c * P:(c + 1) * P], ident)
                    done(ins)
                if i > 1:
                    k = i - 2
                    read_out(pe, f"pT{k}.{l}")
                    b = bank(f"oM{k}.{l}")
                    M(b[:, 0:64], pT[:, k % 2, 0:128], mv[:, 0, k, :], start=True, stop=True)
                    M(b[:, 64:128], pT[:, k % 2, 128:256], mv[:, 0, k, :], start=True, stop=False)
                    done(M(b[:, 64:128], pT[:, k % 2, 256:384], mv[:, 1, k, :], start=False, stop=True))
                if i < NH:
                    gate_part(2 + i // 2, 3 + 4 * (i % 2), 4 + 4 * (i % 2))
            pe.wait_ge(s.scan_in_ready, l + 1)
            scan_in = ((kk, 0), (pr, 0), (ab, 0), (pr, 512))

            def branch_in(n):
                y = (y_ret, y_rwkv, y_mla)[n]
                if n == 2:
                    read_out(pe, f"oM{NH - 1}.{l}")
                else:
                    pe.wait_ge((s.ret_done, s.rwkv_done)[n], l + 1)
                for u in range(2):
                    b = bank(f"yT{n}{u}.{l}")
                    for i in range(2):
                        for t in range(T):
                            ins = TR(b[:, 256 * i + 128 * t:256 * i + 128 * t + 128], y[:, t, 2 * u + i:W:4], ident)
                    done(ins)
                slot = panel("branch")
                read_out(pe, f"yT{n}1.{l}")
                return slot

            def branch(n, slot, u, t):
                project(f"br{n}{u}{t}.{l}", yT[n], slot, 4, 512, t, 512 * u, D)
            for t in range(T):
                for hp in range(4):
                    b = bank(f"kT{t}{hp}.{l}")
                    for i, (src, c0) in enumerate(scan_in):
                        ins = TR(b[:, i * P:(i + 1) * P], src[:, t, c0 + hp * P:c0 + (hp + 1) * P], ident)
                    done(ins)
                for i in range(NH):
                    e, hp = i // 4, i % 4
                    half = slice(64 * e, 64 * e + 64)
                    if e == 0:
                        read_out(pe, f"kT{t}{hp}.{l}")
                    b = bank(f"M{t}{i}.{l}")
                    M(b[:, 0:256], tT[half, hp, 256:384], tT[half, hp, 0:256], start=True, stop=True)
                    done(M(b[:, 256:512], tT[half, hp, 384:512], tT[half, hp, 0:256], start=True, stop=True))
                for g in range(2):
                    b = bank(f"A{t}{g}.{l}")
                    half = slice(64 * g, 64 * g + 64)
                    for hp in range(4):
                        ins = M(b[:, hp * P:(hp + 1) * P], tT[half, hp, 0:128], tT[half, hp, 256:384], start=True,
                                stop=True)
                    done(ins)
                if t == 0:
                    ret_slot = branch_in(0)
                branch(0, ret_slot, t, t)
                for lv in range(1, LEVELS):
                    gt = 6 + 3 * t + (GATED.index(lv) if lv in GATED else 0)
                    for g in range(2):
                        pe.wait_ge(s.x_ready, 2 * (T * l + t) + g + 1) if lv == 1 else \
                            read_out(pe, f"XT{t}{lv - 1}{g}.{l}")
                        b = bank(f"T{t}{lv}{g}.{l}")
                        for i in range(4):
                            ins = M(b[:, i * P:(i + 1) * P], m1[:, 4 * g + i, 0:128], xi[:, 4 * g + i, :],
                                    start=True, stop=True)
                        done(ins)
                    if lv in GATED:
                        gate_part(gt, 0, 3)
                    for g in range(2):
                        read_out(pe, f"T{t}{lv}{g}.{l}")
                        if lv < LEVELS - 1:
                            b = bank(f"X{t}{lv}{g}.{l}")
                            for i in range(4):
                                ins = M(b[:, i * P:(i + 1) * P], xt[:, 4 * g + i, :], t1[:, 4 * g + i, :],
                                        start=True, stop=True)
                            done(ins)
                        b = bank(f"XT{t}{lv}{g}.{l}")
                        for i in range(4):
                            ins = M(b[:, i * P:(i + 1) * P], t1[:, 4 * g + i, :], xt[:, 4 * g + i, :],
                                    start=True, stop=True)
                        done(ins)
                        if lv in GATED:
                            gate_part(gt, 3 + 2 * g, 5 + 3 * g)
                read_out(pe, f"XT{t}{LEVELS - 1}1.{l}")
                vcol = pr[:, t, 1024:1536]
                b = bank(f"W{t}.{l}")
                for hp in range(4):
                    for e in range(2):
                        ins = M(b[64 * e:64 * e + 64, hp * P:(hp + 1) * P],
                                kk[:, t, (2 * hp + e) * 64:(2 * hp + e) * 64 + 64], xt[:, 4 * e + hp, :],
                                start=True, stop=True)
                done(ins)
                b = bank(f"Z{t}.{l}")
                for i in range(NH):
                    hh = slice(64 * i, 64 * i + 64)
                    ins = M(b[:, hh], m1[:, 4 * (i % 2) + i // 2, 256:384], vcol[:, hh], start=True, stop=True)
                done(ins)
                gate_part(8 + 3 * t, 0, 2)
                read_out(pe, f"Z{t}.{l}")
                b = bank(f"U{t}.{l}")
                for i in range(NH):
                    hh = slice(64 * i, 64 * i + 64)
                    ins = M(b[:, hh], xt[:, 4 * (i % 2) + i // 2, :], zz[:, hh], start=True, stop=True)
                done(ins)
                gate_part(8 + 3 * t, 2, 5)
                read_out(pe, f"U{t}.{l}")
                for n in (2 * t, 2 * t + 1):
                    o = slice(64 * (n % 2), 64 * (n % 2) + 64)
                    if n:
                        pe.wait_ge(s.state_ready, 3 * l + n)
                        for e in range(2):
                            b = bank(f"dU{n}{e}.{l}")
                            half = slice(64 * e, 64 * e + 64)
                            for hp in range(4):
                                ins = M(b[o, 64 * hp:64 * hp + 64], nw[half, hp, o], st[half, n - 1, hp, :],
                                        start=True, stop=True)
                            done(ins)
                    if n == 1:
                        branch(0, ret_slot, 1, 0)
                    if n == 2 * t:
                        gate_part(8 + 3 * t, 5, 8)
                    if n:
                        read_out(pe, f"dU{n}1.{l}")
                    if n < 3:
                        b = bank(f"S{n + 1}.{l}")
                        for hp in range(4):
                            for e in range(2):
                                hh = slice((2 * hp + e) * 64, (2 * hp + e) * 64 + 64)
                                dst = b[64 * e:64 * e + 64, 64 * hp:64 * hp + 64]
                                M(dst, ab[o, t, hh], uu[o, t, hh], start=True, stop=False)
                                ins = M(dst, pr[o, t, 512 + hh.start:512 + hh.stop],
                                        pr[o, t, 1024 + hh.start:1024 + hh.stop], start=False, stop=True)
                        done(ins)
                    if n == 0:
                        branch(0, ret_slot, 0, 1)
                for e in range(2):
                    b = bank(f"Y{t}{e}.{l}")
                    half = slice(64 * e, 64 * e + 64)
                    for hp in range(4):
                        hh = slice((2 * hp + e) * 64, (2 * hp + e) * 64 + 64)
                        dst = slice(64 * hp, 64 * hp + 64)
                        M(b[:, dst], m1[:, 4 * e + hp, 384:512], vcol[:, hh], start=True, stop=False)
                        for n in (2 * t, 2 * t + 1):
                            if n:
                                o = 64 * (n % 2)
                                M(b[o:o + 64, dst], tT[half, hp, 128 + o:192 + o], st[half, n - 1, hp, :],
                                  start=False, stop=False)
                        ins = M(b[:, dst], m1[:, 4 * e + hp, 128:256], uu[:, t, hh], start=False, stop=True)
                    done(ins)
            for n in BRANCHES[1:]:
                slot = branch_in(n)
                for u in range(2):
                    for t in range(T):
                        branch(n, slot, u, t)
            pe.wait_ge(s.merged_done, T * 2 * (l + 1))
            transpose_in("gT{}." + str(l), merged)
            read_out(pe, f"gT3.{l}")
            for u in range(2):
                slot = panel("o")
                for t in range(T):
                    project(f"o{u}{t}.{l}", gT, slot, KD, 512, t)
            pe.wait_ge(s.hn_ready, 2 * T * l + 2 * T)
            transpose_in("fT{}." + str(l), hn)
            read_out(pe, f"fT3.{l}")
            if l == 0:
                def ffn_split(q):
                    pe.wait_ge(s.f_lo_ready, q + 1)
                    used[0] += q % 2

                for j in range(7):
                    if j < 6:
                        w_ = FFN_COLS[j]
                        for g, jobs in enumerate(("fg", "fu")):
                            bs = [bank(f"{jobs}{j}{t}.0") for t in range(T)]
                            for r in range(2):
                                q = 4 * j + 2 * g + r
                                ffn_split(q)
                                for t in range(T):
                                    for c in range(4):
                                        x = 4 * r + c
                                        ins = three(bs[t][:, 0:w_], (fx_hi, fx_lo), (f_hi, f_lo), x, t, q % 2,
                                                    slice(w_ * c, w_ * c + w_), x == 0, x == KD - 1)
                                    if r:
                                        done(ins)
                                if r == 0:
                                    ins.then_inc(s.f_half_used, 1)
                    if j:
                        k = FFN_COLS[j - 1] // P
                        for t in range(T):
                            read_out(pe, f"fu{j - 1}{t}.0")
                            b = bank(f"hT{j - 1}{t}.0")
                            for c in range(k):
                                ins = TR(b[:, c * P:(c + 1) * P], hm[:, (j - 1) % 2, t, c:k * P:k], ident)
                            done(ins)
                outs = [(u, t, bank(f"fd{u}{t}.0")) for u in range(2) for t in range(T)]
                for j in range(6):
                    read_out(pe, f"hT{j}1.0")
                    k = FFN_COLS[j] // P
                    for r in range(2):
                        q = 24 + 2 * j + r
                        ffn_split(q)
                        for u, t, b in outs:
                            for c in range(k // 2):
                                x = 4 * j + k // 2 * r + c
                                ins = three(b[:], (hmT_hi, hmT_lo), (f_hi, f_lo), x, t, q % 2,
                                            slice(D * c + 512 * u, D * c + 512 * u + 512), x == 0, x == 21)
                            if x == 21:
                                done(ins)
                        if x < 21:
                            ins.then_inc(s.f_half_used, 1)
        pe.wait_ge(s.router_loaded, 16)
        b = bank("router.1")
        for t in range(T):
            for c in range(KD):
                ins = M(b[:, NE * t:NE * t + NE], hnT[:, c, t * P:(t + 1) * P], router[:, c, :], start=c == 0,
                        stop=c == KD - 1)
        done(ins)
        pe.wait_ge(s.mask_ready, 1)
        b = bank("rank.1")
        m0, m1_ = rt[:, 8, 0, :], rt[:, 8, 1, :]
        M(b[:, 0:NE], C("upto"), m0, start=True, stop=True)
        M(b[:, NE:2 * NE], C("ones"), m0, start=True, stop=False)
        M(b[:, NE:2 * NE], C("upto"), m1_, start=False, stop=True)
        M(b[:, 2 * NE:3 * NE], C("ones"), m0, start=True, stop=False)
        done(M(b[:, 2 * NE:3 * NE], C("ones"), m1_, start=False, stop=True))
        pe.wait_ge(s.freed_act, FR["act"])
        pe.wait_ge(s.freed_vec, FR["vec"])
        def gather(b_of):
            for u in range(2):
                b = b_of(f"gx{u}")
                for i in range(4):
                    for t in range(T):
                        ins = M(b[:, i * P:(i + 1) * P], hn[:, t, 4 * u + i:D:KD], sel[:, t, :], start=t == 0,
                                stop=t == T - 1)
                done(ins)

        pe.wait_ge(s.sel_ready, 1)
        gather(lambda job: banks[ITEM_AT[job] % BANKS])
        for u in range(2):
            done(M(banks[ITEM_AT[f"ed{u}"] % BANKS][:], ident, cst[:, 0:512], start=True, stop=True))
        pe.wait_ge(s.items_ready, 1)
        n_items = pe.value_load(items[0:1, 24:25], min_val=SURE, max_val=SURE + 3)
        def scatter(item, b_of):
            for u in range(2):
                pe.wait_ge(s.freed_vec, item * IF["vec"] + (LOOP_FR["vec"] - 1 + u))
                for t in range(T):
                    done(M(b_of(f"sc{u}{t}")[:], cselT[:, t * P:(t + 1) * P], ey[:, 512 * u:512 * u + 512],
                           start=True, stop=True))

        with pe.Fori(0, n_items) as item:
            def item_read_out(job):
                k = ITEM_AT[job]
                e = ITEM[k][1]
                pe.wait_ge(freed[e], item * IF[e] + (LOOP_FR[e] + item_freed(k, e)))

            def item_read_out_before(job):
                k = ITEM_AT[job]
                e = ITEM[k][1]
                pe.wait_ge(freed[e], item * IF[e] + (LOOP_FR[e] - IF[e] + item_freed(k, e)))

            def item_bank(job):
                k = ITEM_AT[job]
                if k >= BANKS:
                    item_read_out(ITEM[k - BANKS][0])
                else:
                    p = max(m for m in range(len(ITEM)) if m % BANKS == k)
                    e = ITEM[p][1]
                    pe.wait_ge(freed[e], item * IF[e] + (LOOP_FR[e] - IF[e] + item_freed(p, e)))
                return banks[k % BANKS]

            def three(dst, x_hi, x_lo, b, k, start, stop):
                pairs = ((x_hi, w_hi[:, b, k]), (x_hi, w_lo[:, b, k]), (x_lo, w_hi[:, b, k]))
                for n, (a, w) in enumerate(pairs):
                    ins = M(dst, a, w, start=start and n == 0, stop=stop and n == 2, skip_group_check=True)
                return ins

            def half(q):
                pe.wait_ge(s.lo_ready, item * (2 * EP) + (2 * RING + q + 1))

            item_read_out_before("gx1")
            for j in range(8):
                if j < 7:
                    for g, name in enumerate(("eg", "eu")):
                        b = item_bank(f"{name}{j}")
                        for r in range(2):
                            q = 4 * j + 2 * g + r
                            half(q)
                            for c in range(4):
                                x = 4 * r + c
                                ins = three(b[:], xg_hi[:, x, :], xg_lo[:, x, :], q % PARTS,
                                            slice(512 * c, 512 * c + 512), x == 0, x == KD - 1)
                            if r == 0:
                                ins.then_inc(s.half_used, 1)
                        done(ins)
                        if j == g == 0:
                            scatter(item, item_bank)
                            b = item_bank("csT")
                            for t in range(T):
                                ins = TR(b[:, t * P:(t + 1) * P], csel[:, t, :], ident)
                            done(ins)
                if j:
                    item_read_out(f"eu{j - 1}")
                    b = item_bank(f"eT{j - 1}")
                    for c in range(4):
                        ins = TR(b[:, c * P:(c + 1) * P], ehm[:, (j - 1) % 2, c:512:4], ident)
                    done(ins)
            b0, b1 = item_bank("ed0"), item_bank("ed1")
            for j in range(7):
                item_read_out(f"eT{j}")
                for r in range(2):
                    q = 28 + 2 * j + r
                    half(q)
                    for u, b in enumerate((b0, b1)):
                        for c in range(2):
                            x = 4 * j + 2 * r + c
                            ins = three(b[:], ehT_hi[:, x, :], ehT_lo[:, x, :], q % PARTS,
                                        slice(D * c + 512 * u, D * c + 512 * u + 512), x == 0, x == 27)
                        if x == 27:
                            done(ins)
                    if x < 27:
                        ins.then_inc(s.half_used, 1)
                    if q == 32:
                        pe.wait_ge(s.sel_ready, item + 2)
                        gather(item_bank)
        scatter(n_items, lambda job: banks[ITEM_AT[job] % BANKS])

    @block.vector
    def _(dve):
        own = Own(dve, "vec", s.vec_step, s.freed_vec)
        V = nc.vector
        step, settle, free = own.step, own.settle, own.free

        def tt(out_, a, b, op):
            return V.tensor_tensor(out_, a, b, op)

        def normalise(m, dst):
            dve.wait_ge(s.sumsq_ready, T * (m + 1))
            step(V.tensor_scalar(stat[:, 0, 0:T], stat[:, 0, 0:T], 1.0 / D, EPS, ALU.mult, ALU.add), s.var_ready)
            dve.wait_ge(s.root_ready, m + 1)
            step(V.reciprocal(stat[:, 0, 0:T], stat[:, 0, 0:T]))
            settle()
            for t in range(T):
                step(V.tensor_scalar(dst[:, t, :], h[:, t, :], stat[:, 0, t:t + 1], None, ALU.mult), s.hn_ready)

        def group_stats(y, groups, width, eps, m):
            mean, var = stat[:, 3, 0:groups], stat[:, 4, 0:groups]
            v = y.rearrange("p t (g e) -> p (t g) e", e=width)
            sq = tmp[:].rearrange("p t (g e) -> p (t g) e", e=width)
            step(V.reduce_sum(mean, v, AX.X))
            settle()
            step(V.tensor_scalar(mean, mean, 1.0 / width, None, ALU.mult))
            settle()
            step(tt(v, v, wide(mean, width), ALU.subtract))
            settle()
            step(tt(sq, v, v, ALU.mult))
            settle()
            step(V.reduce_sum(var, sq, AX.X))
            settle()
            step(V.tensor_scalar(var, var, 1.0 / width, eps, ALU.mult, ALU.add), s.gn_var_ready)
            dve.wait_ge(s.gn_root_ready, m + 1)
            step(V.reciprocal(var, var))
            settle()
            step(tt(v, v, wide(var, width), ALU.mult))
            settle()

        for l in range(DEPTH):
            normalise(2 * l, hn)
            def in_lo(q):
                src, width = in_half(l, q)
                dve.wait_ge(s.i_hi_ready, NIN * l + q + 1)
                step(tt(i_lo[:, q % 2, 0:width], src, i_hi[:, q % 2, 0:width].bitcast(F32), ALU.subtract),
                     s.i_lo_ready)

            in_lo(0)
            in_lo(1)
            for r in range(2):
                dve.wait_ge(s.i_x_hi_ready, 2 * l + r + 1)
                four = slice(4 * r, 4 * r + 4)
                step(tt(ix_lo[:, four, :], hnT[:, four, :], ix_hi[:, four, :].bitcast(F32), ALU.subtract),
                     s.i_x_lo_ready)
            for q in range(2, 5):
                in_lo(q)
            if l == 0:
                dve.wait_ge(s.const_loaded, 16)
                dve.wait_ge(s.pos_loaded, 16 * T)
                step(V.tensor_copy(pos_f[:], pos_i[:]))
                settle()
                for t in range(T):
                    step(V.tensor_scalar(sinT[:, t, :], C("inv_freq"), pos_f[:, t:t + 1], None, ALU.mult))
                settle()
                step(V.tensor_scalar(cosT[:], sinT[:], 1.0 / (2 * np.pi), ROUND, ALU.mult, ALU.add))
                settle()
                step(V.tensor_scalar(cosT[:], cosT[:], -ROUND, None, ALU.add))
                settle()
                for part in TWO_PI:
                    step(V.scalar_tensor_tensor(out=sinT[:], in0=cosT[:], scalar=-part, in1=sinT[:], op0=ALU.mult,
                                                op1=ALU.add))
                    settle()
                half_pi, pi = float(np.float32(np.pi / 2)), 3.1415925
                turn = rope_tmp[:, 0:160].rearrange("p (t n) -> p t n", t=T)
                step(V.tensor_scalar(turn, sinT[:], half_pi, -2 * np.pi, ALU.is_gt, ALU.mult))
                settle()
                step(V.scalar_tensor_tensor(out=cosT[:], in0=sinT[:], scalar=half_pi, in1=turn, op0=ALU.add, op1=ALU.add))
                settle()
                step(V.tensor_scalar(cosT[:], cosT[:], -pi, pi, ALU.max, ALU.min))
                step(V.tensor_scalar(sinT[:], sinT[:], -pi, pi, ALU.max, ALU.min), s.angles_ready)
            for j, (a, b_) in enumerate(((1536, RWCOLS), (0, 512), (512, 1024), (1024, 1536))):
                p_, old = pr[:, :, a:b_], prev[:, :, a:b_]
                in_lo(5 + 3 * j)
                dve.wait_ge(shift_loaded[j], 32 * (l + 1))
                step(tt(old, old, p_, ALU.subtract))
                in_lo(6 + 3 * j)
                settle()
                dve.wait_ge(s.mu_loaded, 16 * (l + 1))
                step(tt(old, old, each(VEC("mu", a, b_)), ALU.mult))
                in_lo(7 + 3 * j)
                settle()
                step(tt(p_, p_, old, ALU.add), None if j else s.xs_ready)
            settle()
            r, k, v = (pr[:, :, 512 * i:512 * i + 512] for i in range(3))
            dve.wait_ge(s.vec_loaded, 16 * 6 * (l + 1))
            step(tt(kk[:], k, each(VEC("k_k")), ALU.mult))
            in_lo(17)
            settle()
            step(tt(tmp[:], kk[:], kk[:], ALU.mult))
            settle()
            step(V.reduce_sum(stat[:, 1, :], tmp[:].rearrange("p t (g e) -> p (t g) e", e=HD), AX.X))
            settle()
            step(V.tensor_scalar(stat[:, 1, :], stat[:, 1, :], 1e-12, None, ALU.add))
            dve.wait_ge(s.qa_sumsq, 4 * (l + 1))
            lat = stat[:, 2, 0:4].rearrange("p (t q) -> p t q", t=T)
            step(V.tensor_scalar(lat[:, :, 0], lat[:, :, 0], 1.0 / 256, EPS, ALU.mult, ALU.add))
            step(V.tensor_scalar(lat[:, :, 1], lat[:, :, 1], 1.0 / 128, EPS, ALU.mult, ALU.add), s.knsq_ready)
            dve.wait_ge(s.knroot_ready, l + 1)
            step(V.reciprocal(stat[:, 1, :], stat[:, 1, :]))
            step(V.reciprocal(stat[:, 2, 0:4], stat[:, 2, 0:4]))
            settle()
            for t in range(T):
                step(V.tensor_scalar(qa[:, t, 0:256], qa[:, t, 0:256], stat[:, 2, 2 * t:2 * t + 1], None, ALU.mult))
                step(V.tensor_scalar(qa[:, t, 256:384], qa[:, t, 256:384], stat[:, 2, 2 * t + 1:2 * t + 2], None,
                                     ALU.mult), s.qa_ready if t else None)
            for t in range(T):
                b = product(dve, f"z{t}.{l}")
                free(tt(ld[:, t, :], b[:], VEC("w0"), ALU.add), f"z{t}.{l}")
                b = product(dve, f"a{t}.{l}")
                free(tt(ab[:, t, :], b[:], VEC("a0"), ALU.add), f"a{t}.{l}")
            kg = kk[:].rearrange("p t (g e) -> p (t g) e", e=HD)
            step(tt(kg, kg, wide(stat[:, 1, :], HD), ALU.mult))
            settle()
            dve.wait_ge(s.decay_sig_ready, l + 1)
            step(V.tensor_scalar(ld[:], ld[:], -DECAY, None, ALU.mult), s.logd_ready)
            for i in range(RH):
                b = product(dve, f"sR{i}.{l}")
                step(tt(sR[:, i, 0:256], b[:, 0:256], C("ret_mask", 256 * i, 256 * i + 256), ALU.mult))
                free(tt(sR[:, i, 256:384], b[:, 256:384], C("ret_mask", 256 * i, 256 * i + 128), ALU.mult),
                     f"sR{i}.{l}")
            dve.wait_ge(s.rate_sig_ready, l + 1)
            step(V.scalar_tensor_tensor(out=tmp[:], in0=ab[:], scalar=-1.0, in1=each(VEC("k_a")), op0=ALU.add,
                                        op1=ALU.mult))
            step(tt(ab[:], ab[:], kk[:], ALU.mult))
            settle()
            step(V.scalar_tensor_tensor(out=k, in0=tmp[:], scalar=1.0, in1=k, op0=ALU.add, op1=ALU.mult))
            settle()
            step(tt(tmp[:], r, k, ALU.mult))
            settle()
            step(tt(tmp[:], tmp[:], each(VEC("r_k")), ALU.mult))
            settle()
            step(V.reduce_sum(stat[:, 5, :], tmp[:].rearrange("p t (g e) -> p (t g) e", e=HD), AX.X))
            dve.wait_ge(s.product_ready, JOB_AT[f"pc.{l}"] + 1)
            for t in range(T):
                b = banks[JOB_AT[f"cum{t}.{l}"] % BANKS]
                dve.wait_ge(s.exps_ready, T * l + t + 1)
                step(tt(ld[:, t, :], b[:], ld[:, t, :], ALU.subtract), s.cex_ready)
            read_out(dve, f"cum1.{l}")
            step(tt(kk[:], kk[:], ld[:], ALU.mult))
            step(tt(r, r, ec[:], ALU.mult))
            step(tt(ab[:], ab[:], enc[:], ALU.mult))
            step(tt(k, k, enc[:], ALU.mult), s.scan_in_ready)
            read_out(dve, f"oR1.{l}")
            group_stats(y_ret[:], 8, P, 1e-5, 2 * l)
            dve.wait_ge(s.silu_g_ready, l + 1)
            step(tt(y_ret[:], y_ret[:], raw[:, 3, :, :], ALU.mult), s.ret_done)
            for i in range(NH + 2):
                if i < NH:
                    b = product(dve, f"sM{i}.{l}")
                    if i > 1:
                        dve.wait_ge(s.product_ready, JOB_AT[f"pT{i - 2}.{l}"] + 1)
                    sc = float(QK) ** -0.5
                    m = sm[:, i % 2, :]
                    step(V.scalar_tensor_tensor(out=m[:, 0:128], in0=b[:, 0:128], scalar=sc, in1=C("mla_mask"),
                                                op0=ALU.mult, op1=ALU.add))
                    step(V.tensor_scalar(m[:, 128:256], b[:, 128:256], sc, None, ALU.mult))
                    free(V.scalar_tensor_tensor(out=m[:, 256:384], in0=b[:, 256:384], scalar=sc, in1=C("mla_mask"),
                                                op0=ALU.mult, op1=ALU.add), f"sM{i}.{l}")
                    settle()
                    step(V.reduce_max(smax[:, i, 0:1], m[:, 0:128], AX.X))
                    step(V.reduce_max(smax[:, i, 1:2], m[:, 128:384], AX.X))
                    settle()
                    step(V.tensor_scalar(smax[:, i, :], smax[:, i, :], -1.0, None, ALU.mult), s.masked_ready)
                if i > 1:
                    j = i - 2
                    dve.wait_ge(s.prob_ready, NH * l + j + 1)
                    step(V.reciprocal(den[:, j, :], den[:, j, :]))
                    b = product(dve, f"oM{j}.{l}")
                    settle()
                    free(tt(y_mla[:, :, 64 * j:64 * j + 64], b[:, 0:128].rearrange("p (t e) -> p t e", t=T),
                            wide(den[:, j, :], HD), ALU.mult), f"oM{j}.{l}")
            def gated(n, u, t):
                b = product(dve, f"br{n}{u}{t}.{l}")
                gate = sigs[n][:, u, t, :]
                read_out(dve, f"gt{4 * BRANCHES.index(n) + 2 * u + t}.{l}")
                free(tt(gate, b[:], gate, ALU.mult), f"br{n}{u}{t}.{l}")
                return gate

            for t in range(T):
                for i in range(NH):
                    b = product(dve, f"M{t}{i}.{l}")
                    free(tt(m1[:, i, :], b[:], C("pair_mask"), ALU.mult), f"M{t}{i}.{l}")
                for g in range(2):
                    four = slice(4 * g, 4 * g + 4)
                    b = product(dve, f"A{t}{g}.{l}")
                    quad = b[:].rearrange("p (i n) -> p i n", i=4)
                    free(tt(am[:, four, :], quad, each(C("a_mask"), 4), ALU.mult), f"A{t}{g}.{l}")
                    settle()
                    step(tt(xt[:, four, :], m1[:, four, 0:128], each(C("level0_t"), 4), ALU.mult))
                    settle()
                    step(tt(xi[:, four, :], am[:, four, :], each(C("levels", 0, P), 4), ALU.mult))
                    step(tt(xt[:, four, :], xt[:, four, :], each(C("ident"), 4), ALU.add))
                    settle()
                    step(tt(xi[:, four, :], xi[:, four, :], each(C("ident"), 4), ALU.add), s.x_ready)
                gated(0, t, t)
                for lv in range(1, LEVELS):
                    for g in range(2):
                        four = slice(4 * g, 4 * g + 4)
                        b = product(dve, f"T{t}{lv}{g}.{l}")
                        free(tt(t1[:, four, :], b[:].rearrange("p (i n) -> p i n", i=4),
                                each(C("levels", lv * P, lv * P + P), 4), ALU.mult), f"T{t}{lv}{g}.{l}")
                    for g in range(2):
                        four = slice(4 * g, 4 * g + 4)
                        for x_, name in ((xi, "X"), (xt, "XT")):
                            if name == "X" and lv == LEVELS - 1:
                                continue
                            b = product(dve, f"{name}{t}{lv}{g}.{l}")
                            free(tt(x_[:, four, :], b[:].rearrange("p (i n) -> p i n", i=4), x_[:, four, :],
                                    ALU.add), f"{name}{t}{lv}{g}.{l}")
                for n in (2 * t, 2 * t + 1):
                    o = slice(64 * (n % 2), 64 * (n % 2) + 64)
                    if n == 2 * t:
                        read_out(dve, f"U{t}.{l}")
                    if n:
                        for e in range(2):
                            b = product(dve, f"dU{n}{e}.{l}")
                            u_ = uu[o, t, :].rearrange("p (a b d) -> p a b d", a=4, b=2)[:, :, e, :]
                            free(tt(u_, b[o, 0:256].rearrange("p (a d) -> p a d", a=4), u_, ALU.add),
                                 f"dU{n}{e}.{l}")
                    if n == 1:
                        gated(0, 1, 0)
                    if n < 3:
                        b = product(dve, f"S{n + 1}.{l}")
                        sn = b[:, 0:256].rearrange("p (a d) -> p a d", a=4)
                        dec = wide(decay_end[:, t, :, n % 2], HD)
                        if n == 0:
                            free(V.tensor_copy(st[:, 0, :, :], sn), f"S{n + 1}.{l}")
                        else:
                            free(tt(st[:, n, :, :], sn, st[:, n - 1, :, :], ALU.add), f"S{n + 1}.{l}")
                        settle()
                        step(tt(st[:, n, :, :], st[:, n, :, :], dec, ALU.mult), s.state_ready)
                    if n == 0:
                        gated(0, 0, 1)
            read_out(dve, f"Y11.{l}")
            group_stats(y_rwkv[:], 16, HD, 64e-5, 2 * l + 1)
            step(tt(y_rwkv[:], y_rwkv[:], each(VEC("lnx")), ALU.mult))
            step(tt(tmp[:].rearrange("p t (g e) -> p t g e", e=HD), v.rearrange("p t (g e) -> p t g e", e=HD),
                    wide(stat[:, 5, :].rearrange("p (t g) -> p t g", t=T), HD), ALU.mult))
            settle()
            step(tt(y_rwkv[:], y_rwkv[:], tmp[:], ALU.add))
            settle()
            step(tt(y_rwkv[:], y_rwkv[:], gg[:], ALU.mult), s.rwkv_done)
            for n in BRANCHES[1:]:
                for u in range(2):
                    for t in range(T):
                        gate, total = gated(n, u, t), sigs[0][:, u, t, :]
                        settle()
                        if n == BRANCHES[-1]:
                            step(tt(merged[:, t, 512 * u:512 * u + 512], total, gate, ALU.add), s.merged_done)
                        else:
                            step(tt(total, total, gate, ALU.add))

            def ffn_low(q):
                src, width = ffn_half(q)
                dve.wait_ge(s.f_hi_ready, q + 1)
                step(tt(f_lo[:, q % 2, 0:width], src, f_hi[:, q % 2, 0:width].bitcast(F32), ALU.subtract),
                     s.f_lo_ready)

            if l == 0:
                ffn_low(0)
                ffn_low(1)
            for u in range(2):
                for t in range(T):
                    b = product(dve, f"o{u}{t}.{l}")
                    hs = h[:, t, 512 * u:512 * u + 512]
                    free(tt(hs, b[:], hs, ALU.add), f"o{u}{t}.{l}")
            normalise(2 * l + 1, hn)
            if l == 0:
                for q in range(4):
                    b = product(dve, f"fT{q}.0")
                    dve.wait_ge(s.f_x_hi_ready, q + 1)
                    for i in range(2):
                        c = 2 * q + i
                        ins = V.scalar_tensor_tensor(out=fx_lo[:, c, :], in0=b[:, 256 * i:256 * i + 256],
                                                     scalar=gains[:, 0, 1, c:c + 1],
                                                     in1=fx_hi[:, c, :].bitcast(F32), op0=ALU.mult,
                                                     op1=ALU.subtract)
                        step(ins) if i == 0 else free(ins, f"fT{q}.0")
                for q in range(2, 36):
                    ffn_low(q)
                    if q % 4 == 1 and 5 <= q <= 25:
                        j = (q - 5) // 4
                        w_ = FFN_COLS[j]
                        for t in range(T):
                            b = product(dve, f"fu{j}{t}.0")
                            read_out(dve, f"fg{j}{t}.0")
                            free(tt(hm[:, j % 2, t, 0:w_], b[:, 0:w_], sg[:, j % 2, t, 0:w_], ALU.mult),
                                 f"fu{j}{t}.0")
                    if q % 4 == 2 and 10 <= q <= 30:
                        j = (q - 10) // 4
                        k = FFN_COLS[j] // P
                        for t in range(T):
                            b = product(dve, f"hT{j}{t}.0")
                            dve.wait_ge(s.f_x_hi_ready, 4 + T * j + t + 1)
                            tok = slice(t * P, (t + 1) * P)
                            free(tt(hmT_lo[:, 4 * j:4 * j + k, tok],
                                    b[:, 0:k * P].rearrange("p (c n) -> p c n", c=k),
                                    hmT_hi[:, 4 * j:4 * j + k, tok].bitcast(F32), ALU.subtract), f"hT{j}{t}.0")
                for u in range(2):
                    for t in range(T):
                        b = product(dve, f"fd{u}{t}.0")
                        hs = h[:, t, 512 * u:512 * u + 512]
                        free(tt(hs, b[:], hs, ALU.add), f"fd{u}{t}.0")
        R = lambda i: rt[:, i, :, :]
        few = each(C("experts"), T)
        b = product(dve, "router.1")
        free(V.tensor_copy(R(0), b[:, 0:T * NE].rearrange("p (t e) -> p t e", t=T)), "router.1")
        step(V.tensor_scalar(R(1), few, -99.0, None, ALU.add))
        settle()
        top = stat[:, 7, :].rearrange("p (a t) -> p a t", t=T)
        for i in range(2):
            step(V.reduce_max(top[:, i, :], R(0), AX.X))
            settle()
            step(tt(R(4), R(0), wide(top[:, i, :], NE), ALU.is_equal))
            settle()
            step(tt(R(4), R(4), R(1), ALU.mult))
            settle()
            step(V.tensor_reduce(top[:, 2, :], R(4), AX.X, ALU.min))
            settle()
            step(tt(R(2 + i), R(1), wide(top[:, 2, :], NE), ALU.is_equal))
            settle()
            if i == 0:
                step(V.scalar_tensor_tensor(out=R(0), in0=R(2), scalar=-3e38, in1=R(0), op0=ALU.mult, op1=ALU.add))
                settle()
        step(tt(stat[:, 6, 0:2], top[:, 1, :], top[:, 0, :], ALU.subtract), s.route_diff)
        step(tt(R(8), R(2), R(3), ALU.add), s.mask_ready)
        dve.wait_ge(s.route_exp, 1)
        step(V.tensor_scalar(stat[:, 6, 2:4], stat[:, 6, 0:2], 1.0, None, ALU.add))
        settle()
        step(V.reciprocal(stat[:, 6, 2:4], stat[:, 6, 2:4]))
        settle()
        step(tt(stat[:, 6, 0:2], stat[:, 6, 0:2], stat[:, 6, 2:4], ALU.mult))
        settle()
        step(tt(R(2), R(2), wide(stat[:, 6, 2:4], NE), ALU.mult))
        step(tt(R(3), R(3), wide(stat[:, 6, 0:2], NE), ALU.mult))
        settle()
        for i in range(2):
            step(tt(comb[:, i, :, :], R(2), R(3), ALU.add))
        b = product(dve, "rank.1")
        step(tt(R(5), b[:, 0:T * NE].rearrange("p (t e) -> p t e", t=T), R(8), ALU.mult))
        settle()
        for i in range(2):
            step(V.tensor_scalar(spos[:, i, :, :], R(5), -1.0 - P * i, None, ALU.add))
        f = it_f[0:1, :]
        free(V.tensor_scalar(f[:, 0:8], b[0:1, 16:24], P + 0.5, None, ALU.is_gt), "rank.1")

        def select(column):
            for t in range(T):
                sp_ = spos[:].rearrange("p i t e -> p (i t e)")[:, bass.ds(column + NE * t, 1)]
                cb_ = comb[:].rearrange("p i t e -> p (i t e)")[:, bass.ds(column + NE * t, 1)]
                V.tensor_scalar(sel[:, t, :], C("slots"), sp_, None, ALU.is_equal)
                ins = V.tensor_scalar(csel[:, t, :], C("slots"), sp_, cb_, ALU.is_equal, ALU.mult)
            ins.then_inc(s.sel_ready, 1)

        settle()
        V.memset(cselT[:], 0.0)
        select(0)
        step(V.tensor_scalar(f[:, 8:16], C("experts")[0:1, :], -1.0, 8.0, ALU.mult, ALU.add))
        settle()
        step(tt(f[:, 8:16], f[:, 8:16], f[:, 0:8], ALU.mult))
        step(V.reduce_sum(f[:, 56:57], f[:, 0:8], AX.X))
        settle()
        step(V.max(f[:, 16:24], f[:, 8:16]))
        settle()
        step(V.tensor_scalar(f[:, 40:44], f[:, 16:20], -1.0, 24.0, ALU.mult, ALU.add))
        step(V.tensor_copy(f[:, 32:40], C("experts")[0:1, :]))
        step(V.tensor_copy(f[:, 44:52], C("experts")[0:1, :]))
        step(V.tensor_scalar(f[:, 52:56], f[:, 16:20], -1.0, 8.0, ALU.mult, ALU.add))
        step(V.tensor_scalar(f[:, 56:57], f[:, 56:57], float(NE), None, ALU.add))
        settle()
        step(V.tensor_scalar(f[:, 52:56], f[:, 52:56], float(NE - 1), None, ALU.min))
        step(V.tensor_scalar(f[:, 40:44], f[:, 40:44], float(2 * NE * T // 2 + NE - 1), None, ALU.min))
        settle()
        step(V.tensor_copy(items[0:1, 0:25], f[:, 32:57]), s.items_ready)
        settle()
        V.tensor_copy(smax[:, 1, :], smax[:, 0, :]).then_inc(s.lo_ready, 2 * RING)
        V.tensor_copy(smax[:, 2, :], smax[:, 0, :]).then_inc(s.half_used, HALVES)
        def gathered_lo(bank_of, n):
            for u in range(2):
                b = bank_of(f"gx{u}")
                dve.wait_ge(s.x_hi_ready, n + (u + 1))
                for i in range(4):
                    c = 4 * u + i
                    ins = V.scalar_tensor_tensor(out=xg_lo[:, c, :], in0=b[:, i * P:(i + 1) * P],
                                                 scalar=gains[:, 1, 1, c:c + 1], in1=xg_hi[:, c, :].bitcast(F32),
                                                 op0=ALU.mult, op1=ALU.subtract)
                ins.then_inc(s.freed_vec, 1)

        def down_out(bank_of):
            for u in range(2):
                V.tensor_copy(ey[:, 512 * u:512 * u + 512], bank_of(f"ed{u}")[:]).then_inc(s.freed_vec, 1)

        def add_scattered(bank_of):
            for u in range(2):
                for t in range(T):
                    hs = h[:, t, 512 * u:512 * u + 512]
                    ins = tt(hs, bank_of(f"sc{u}{t}")[:], hs, ALU.add).then_inc(s.freed_vec, 1)

        gathered_lo(lambda job: ahead(dve, job), 0)
        n_items = dve.value_load(items[0:1, 24:25], min_val=SURE, max_val=SURE + 3)
        with dve.Fori(0, n_items) as item:
            next_column = dve.value_load(items[0:1, bass.ds(item + 1, 1)], min_val=0, max_val=NE * T + NE - 1)

            def item_product(job):
                dve.wait_ge(s.product_ready, item * len(ITEM) + (len(JOBS) + AHEAD + ITEM_AT[job] + 1))
                return banks[ITEM_AT[job] % BANKS]

            def before(job):
                dve.wait_ge(s.product_ready,
                            item * len(ITEM) + (len(JOBS) + AHEAD - len(ITEM) + ITEM_AT[job] + 1))
                return banks[ITEM_AT[job] % BANKS]

            def lo(q):
                dve.wait_ge(s.hi_ready, item * (2 * EP) + (q + 1))
                i, o = (NPAN + q // 2) % RING, HALF * (q % 2)
                tt(w_lo[:, q % PARTS, :], ring[:, i, o:o + HALF], w_hi[:, q % PARTS, :].bitcast(F32),
                   ALU.subtract).then_inc(s.lo_ready, 1)

            for q in range(2 * EP):
                lo(q)
                if q == 1:
                    down_out(before)
                if q == 3:
                    add_scattered(item_product)
                if q == 30:
                    select(next_column)
                if q == 36:
                    gathered_lo(item_product, item * 9 + 9)
                if q % 4 == 1 and 5 <= q <= 29:
                    j = (q - 5) // 4
                    b = item_product(f"eu{j}")
                    k = ITEM_AT[f"eg{j}"]
                    dve.wait_ge(s.freed_act, item * IF["act"] + (LOOP_FR["act"] + item_freed(k, "act")))
                    tt(ehm[:, j % 2, :], b[:], esg[:, j % 2, :], ALU.mult).then_inc(s.freed_vec, 1)
                if q % 4 == 2 and 10 <= q <= 34:
                    j = (q - 10) // 4
                    b = item_product(f"eT{j}")
                    dve.wait_ge(s.x_hi_ready, item * 9 + (j + 3))
                    tt(ehT_lo[:, 4 * j:4 * j + 4, :], b[:].rearrange("p (c n) -> p c n", c=4),
                       ehT_hi[:, 4 * j:4 * j + 4, :].bitcast(F32), ALU.subtract).then_inc(s.freed_vec, 1)

        def final(job):
            k = ITEM_AT[job] - (len(ITEM) if job.startswith("ed") else 0)
            if job.startswith("sc"):
                k -= 1
            dve.wait_ge(s.product_ready, n_items * len(ITEM) + (len(JOBS) + AHEAD + k + 1))
            return banks[ITEM_AT[job] % BANKS]

        down_out(final)
        add_scattered(final)
        dve.wait_ge(s.freed_vec, n_items * IF["vec"] + (LOOP_FR["vec"] + 4))
        V.tensor_copy(smax[:, 0, :], smax[:, 0, :]).then_inc(s.items_done, 1)
        normalise(4, fin)
        dve.wait_ge(s.fgain_loaded, 16)
        for t in range(T):
            settle()
            own.step(tt(fin[:, t, :], fin[:, t, :], fgain[:], ALU.mult), s.fin_ready)

    blk.__exit__(None, None, None)


_INS = ["x", "positions", "attn_norm", "w_in", "rwkv_mu", "rwkv_w0", "rwkv_w2", "rwkv_a0", "rwkv_a2", "rwkv_g2",
        "rwkv_k_k", "rwkv_k_a", "rwkv_r_k", "rwkv_lnx_w", "mla_q_norm", "mla_w_qb", "mla_kv_norm", "mla_w_kvb",
        "w_branch", "w_o", "ffn_norm", "ffn_w_gate", "ffn_w_up", "ffn_w_down", "moe_router", "moe_w_gate",
        "moe_w_up", "moe_w_down", "final_norm"]


def kernel(**inputs):
    import concourse.bacc as bacc
    from concourse.bass_utils import run_bass_kernel_spmd

    nc = bacc.Bacc("TRN2", target_bir_lowering=False, num_devices=1)
    arrays, args = {}, []
    for name in _INS:
        a = np.ascontiguousarray(inputs[name])
        arrays[f"{name}_dram"] = a
        args.append(nc.dram_tensor(f"{name}_dram", a.shape, mybir.dt.from_np(a.dtype), kind="ExternalInput").ap())
    arrays["const_dram"] = CONST
    args.append(nc.dram_tensor("const_dram", CONST.shape, F32, kind="ExternalInput").ap())
    args.append(nc.dram_tensor("out_dram", (1, SEQ, D), F32, kind="ExternalOutput").ap())
    build(nc, *args)
    r = run_bass_kernel_spmd(nc, [arrays], core_ids=[0])
    return r.results[0]["out_dram"]
```
